# Optimizing a Trainium2 kernel written in Bass

```python
import jax, jax.numpy as jnp
from jax import lax
import numpy as np
import jax
import jax.numpy as jnp

D_MODEL = 1024
BATCH = 1
SEQ = 256
DEPTH = 1

HEAD_DIM = 64
N_Q_HEADS = 8
N_KV_HEADS = 2
Q_REP = N_Q_HEADS // N_KV_HEADS
ATTN_WIDTH = N_Q_HEADS * HEAD_DIM
KV_WIDTH = N_KV_HEADS * HEAD_DIM
WINDOW = 128
ATTN_BLOCK = 128
N_GMLP_GROUPS = 8
GMLP_WIDTH = D_MODEL - ATTN_WIDTH
GMLP_GROUP_DIM = GMLP_WIDTH // N_GMLP_GROUPS
CHUNK = 128
MIX_WIDTH = ATTN_WIDTH + GMLP_WIDTH
IN_WIDTH = ATTN_WIDTH + 2 * KV_WIDTH + 2 * GMLP_WIDTH
N_EXPERTS = 32
TOP_K = 4
D_FF = D_MODEL
SWIGLU_LIMIT = 7.0
SWIGLU_ALPHA = 1.702
MOE_BLOCK = 128
LN_EPS = 1e-5
DEEPNORM_ALPHA = (2.0 * DEPTH) ** 0.25
DEEPNORM_BETA = (8.0 * DEPTH) ** -0.25
NEG_INF = -1e30


def layer_norm(x, g, b):
    xf = x.astype(jnp.float32)
    mu = jnp.mean(xf, axis=-1, keepdims=True)
    xc = xf - mu
    var = jnp.mean(xc * xc, axis=-1, keepdims=True)
    return (xc * lax.rsqrt(var + LN_EPS)).astype(x.dtype) * g + b

def sliding_window_attention(q, k, v, sinks):
    B, S = q.shape[:2]
    nb = S // ATTN_BLOCK
    q = q.reshape(B, nb, ATTN_BLOCK, N_KV_HEADS, Q_REP, HEAD_DIM)
    k = k.reshape(B, nb, ATTN_BLOCK, N_KV_HEADS, HEAD_DIM)
    v = v.reshape(B, nb, ATTN_BLOCK, N_KV_HEADS, HEAD_DIM)

    def band(t):
        prev = jnp.pad(t[:, :-1], ((0, 0), (1, 0), (0, 0), (0, 0), (0, 0)))
        return jnp.concatenate([prev, t], axis=2)

    kb, vb = band(k), band(v)
    scores = jnp.einsum('bnqgrd,bnkgd->bngrqk', q, kb).astype(jnp.float32) * (HEAD_DIM ** -0.5)
    t_idx = jnp.arange(ATTN_BLOCK)[:, None]
    s_idx = jnp.arange(2 * ATTN_BLOCK)[None, :]
    diff = t_idx + ATTN_BLOCK - s_idx
    in_band = (diff >= 0) & (diff < WINDOW)
    blk = jnp.arange(nb)[:, None, None]
    valid = in_band[None] & ((blk * ATTN_BLOCK - ATTN_BLOCK + s_idx[None]) >= 0)
    scores = jnp.where(valid[None, :, None, None], scores, NEG_INF)
    sink = sinks.astype(jnp.float32).reshape(N_KV_HEADS, Q_REP)[None, None, :, :, None, None]
    sink = jnp.broadcast_to(sink, scores.shape[:-1] + (1,))
    probs = jax.nn.softmax(jnp.concatenate([scores, sink], axis=-1), axis=-1)[..., :-1]
    out = jnp.einsum('bngrqk,bnkgd->bnqgrd', probs.astype(v.dtype), vb)
    return out.reshape(B, S, ATTN_WIDTH)

def chunked_spatial_gating(u, g, ln_g, ln_b, w_s, b_s):
    B, S = u.shape[:2]
    nc = S // CHUNK
    u = jax.nn.gelu(u)
    g = jax.nn.gelu(g).reshape(B, S, N_GMLP_GROUPS, GMLP_GROUP_DIM)
    g = layer_norm(g, ln_g.reshape(N_GMLP_GROUPS, GMLP_GROUP_DIM), ln_b.reshape(N_GMLP_GROUPS, GMLP_GROUP_DIM))
    g = g.reshape(B, nc, CHUNK, N_GMLP_GROUPS, GMLP_GROUP_DIM)
    causal = jnp.tril(jnp.ones((CHUNK, CHUNK), dtype=bool))
    w = jnp.where(causal[None], w_s, jnp.zeros_like(w_s))
    mixed = jnp.einsum('gts,bcsgd->bctgd', w, g) + b_s.T[None, None, :, :, None]
    return u * mixed.reshape(B, S, GMLP_WIDTH)

def token_mixer(x, w_in, b_in, sinks, ln_v_g, ln_v_b, w_spatial, b_spatial, w_out, b_out):
    proj = x @ w_in + b_in
    o1 = ATTN_WIDTH
    o2 = o1 + KV_WIDTH
    o3 = o2 + KV_WIDTH
    o4 = o3 + GMLP_WIDTH
    q, k, v = proj[..., :o1], proj[..., o1:o2], proj[..., o2:o3]
    u, g = proj[..., o3:o4], proj[..., o4:]
    attn = sliding_window_attention(q, k, v, sinks)
    sgu = chunked_spatial_gating(u, g, ln_v_g, ln_v_b, w_spatial, b_spatial)
    return jnp.concatenate([attn, sgu], axis=-1) @ w_out + b_out

def routed_experts(x, w_router, b_router, w_gate, b_gate, w_up, b_up, w_down, b_down):
    B, S, D = x.shape
    T = B * S
    TK = T * TOP_K
    xt = x.reshape(T, D)
    logits = (xt @ w_router + b_router).astype(jnp.float32)
    top_vals, top_idx = lax.top_k(logits, TOP_K)
    gates = jax.nn.softmax(top_vals, axis=-1).astype(x.dtype)
    flat_e = top_idx.reshape(-1)
    flat_tok = jnp.arange(TK, dtype=jnp.int32) // TOP_K
    order = jnp.argsort(flat_e)
    sorted_e = flat_e[order]
    counts = jnp.bincount(flat_e, length=N_EXPERTS)
    start = jnp.cumsum(counts) - counts
    padded = (counts + MOE_BLOCK - 1) // MOE_BLOCK * MOE_BLOCK
    padded_end = jnp.cumsum(padded)
    padded_start = padded_end - padded
    dest = padded_start[sorted_e] + jnp.arange(TK, dtype=jnp.int32) - start[sorted_e]
    n_blocks = TK // MOE_BLOCK + N_EXPERTS
    n_rows = n_blocks * MOE_BLOCK
    row_tok = jnp.full((n_rows,), T, dtype=jnp.int32).at[dest].set(flat_tok[order])
    row_gate = jnp.zeros((n_rows,), x.dtype).at[dest].set(gates.reshape(-1)[order])
    block_e = jnp.minimum(
        jnp.searchsorted(padded_end, jnp.arange(n_blocks, dtype=padded_end.dtype) * MOE_BLOCK, side='right'),
        N_EXPERTS - 1)
    x_rows = jnp.concatenate([xt, jnp.zeros((1, D), xt.dtype)], axis=0)[row_tok]
    x_rows = x_rows.reshape(n_blocks, MOE_BLOCK, D)

    def expert_block(args):
        xb, e = args
        gt = jnp.minimum(xb @ w_gate[e] + b_gate[e], SWIGLU_LIMIT)
        up = jnp.clip(xb @ w_up[e] + b_up[e], -SWIGLU_LIMIT, SWIGLU_LIMIT)
        hid = gt * jax.nn.sigmoid(SWIGLU_ALPHA * gt) * (up + 1.0)
        return hid @ w_down[e] + b_down[e]

    y_rows = lax.map(expert_block, (x_rows, block_e)).reshape(n_rows, D)
    out = jnp.zeros((T + 1, D), x.dtype).at[row_tok].add(y_rows * row_gate[:, None])[:T]
    return out.reshape(B, S, D)

def first_inputs(seed: int = 0) -> dict:
    key = jax.random.key(seed)
    ks = jax.random.split(key, 24)
    f32 = jnp.float32

    def nrm(k, shape, scale):
        return jax.random.normal(k, (DEPTH,) + shape, f32) * scale

    x = jax.random.normal(ks[0], (BATCH, SEQ, D_MODEL), f32)
    col_scale = jnp.concatenate([
        jnp.ones((ATTN_WIDTH + KV_WIDTH,), f32),
        jnp.full((KV_WIDTH,), DEEPNORM_BETA, f32),
        jnp.full((GMLP_WIDTH,), DEEPNORM_BETA, f32),
        jnp.ones((GMLP_WIDTH,), f32)])
    w_in = nrm(ks[1], (D_MODEL, IN_WIDTH), D_MODEL ** -0.5) * col_scale
    b_in = nrm(ks[2], (IN_WIDTH,), 0.02)
    sinks = nrm(ks[3], (N_Q_HEADS,), 0.5)
    ln_v_g = 1.0 + nrm(ks[4], (GMLP_WIDTH,), 0.05)
    ln_v_b = nrm(ks[5], (GMLP_WIDTH,), 0.02)
    w_spatial = nrm(ks[6], (N_GMLP_GROUPS, CHUNK, CHUNK), CHUNK ** -0.5)
    b_spatial = 1.0 + nrm(ks[7], (N_GMLP_GROUPS, CHUNK), 0.05)
    w_out = nrm(ks[8], (MIX_WIDTH, D_MODEL), MIX_WIDTH ** -0.5 * DEEPNORM_BETA)
    b_out = nrm(ks[9], (D_MODEL,), 0.02)
    ln1_g = 1.0 + nrm(ks[10], (D_MODEL,), 0.05)
    ln1_b = nrm(ks[11], (D_MODEL,), 0.02)
    w_router = nrm(ks[12], (D_MODEL, N_EXPERTS), D_MODEL ** -0.5)
    b_router = nrm(ks[13], (N_EXPERTS,), 0.01)
    w_gate = nrm(ks[14], (N_EXPERTS, D_MODEL, D_FF), D_MODEL ** -0.5)
    b_gate = nrm(ks[15], (N_EXPERTS, D_FF), 0.02)
    w_up = nrm(ks[16], (N_EXPERTS, D_MODEL, D_FF), D_MODEL ** -0.5 * DEEPNORM_BETA)
    b_up = nrm(ks[17], (N_EXPERTS, D_FF), 0.02)
    w_down = nrm(ks[18], (N_EXPERTS, D_FF, D_MODEL), D_FF ** -0.5 * DEEPNORM_BETA)
    b_down = nrm(ks[19], (N_EXPERTS, D_MODEL), 0.02)
    ln2_g = 1.0 + nrm(ks[20], (D_MODEL,), 0.05)
    ln2_b = nrm(ks[21], (D_MODEL,), 0.02)
    return {"x": x, "w_in": w_in, "b_in": b_in, "sinks": sinks, "ln_v_g": ln_v_g, "ln_v_b": ln_v_b,
            "w_spatial": w_spatial, "b_spatial": b_spatial, "w_out": w_out, "b_out": b_out,
            "ln1_g": ln1_g, "ln1_b": ln1_b, "w_router": w_router, "b_router": b_router,
            "w_gate": w_gate, "b_gate": b_gate, "w_up": w_up, "b_up": b_up,
            "w_down": w_down, "b_down": b_down, "ln2_g": ln2_g, "ln2_b": ln2_b}

def first_block(x, w_in, b_in, sinks, ln_v_g, ln_v_b, w_spatial, b_spatial, w_out, b_out,
              ln1_g, ln1_b, w_router, b_router, w_gate, b_gate, w_up, b_up,
              w_down, b_down, ln2_g, ln2_b):
    for l in range(DEPTH):
        mix = token_mixer(x, w_in[l], b_in[l], sinks[l], ln_v_g[l], ln_v_b[l],
                          w_spatial[l], b_spatial[l], w_out[l], b_out[l])
        h = layer_norm(DEEPNORM_ALPHA * x + mix, ln1_g[l], ln1_b[l])
        ffn = routed_experts(h, w_router[l], b_router[l], w_gate[l], b_gate[l],
                             w_up[l], b_up[l], w_down[l], b_down[l])
        x = layer_norm(DEEPNORM_ALPHA * h + ffn, ln2_g[l], ln2_b[l])
    return x


RWKV_HEADS = 8
RWKV_WIDTH = RWKV_HEADS * HEAD_DIM
MOBA_HEADS = 8
MOBA_WIDTH = MOBA_HEADS * HEAD_DIM
DECAY_LORA = 64
AAA_LORA = 64
GATE_LORA = 160
MOBA_BLOCK = 256
MOBA_TOPK = 3
Q_CHUNK = 64
ROT_DIM = HEAD_DIM // 4
ROPE_THETA = 500000.0
D_FF_2 = 2816
CONV_WIDTH = 3
NORM_EPS = 1e-6
GN_EPS = 64e-5
N_BRANCH = 2
RWKV_IN = 3 * RWKV_WIDTH + DECAY_LORA + AAA_LORA + GATE_LORA
MOBA_IN = 3 * MOBA_WIDTH
GATE_IN = N_BRANCH * D_MODEL
IN_COLS = RWKV_IN + MOBA_IN + GATE_IN


def rms_norm(x, g):
    xf = x.astype(jnp.float32)
    y = xf * lax.rsqrt(jnp.mean(xf * xf, axis=-1, keepdims=True) + NORM_EPS)
    return (y * g.astype(jnp.float32)).astype(x.dtype)

def shift_right(z):
    return jnp.pad(z, ((0, 0), (1, 0), (0, 0)))[:, :-1]

def partial_rope(x, positions):
    half = ROT_DIM // 2
    inv_freq = ROPE_THETA ** (-jnp.arange(half, dtype=jnp.float32) / half)
    ang = positions.astype(jnp.float32)[..., None] * inv_freq
    cos = jnp.cos(ang)[:, :, None, :]
    sin = jnp.sin(ang)[:, :, None, :]
    xr = x[..., :ROT_DIM].astype(jnp.float32)
    x1, x2 = xr[..., :half], xr[..., half:]
    rot = jnp.concatenate([x1 * cos - x2 * sin, x2 * cos + x1 * sin], axis=-1)
    return jnp.concatenate([rot.astype(x.dtype), x[..., ROT_DIM:]], axis=-1)

def rwkv7_time_mix(z, w_decay_up, decay_bias, w_aaa_up, aaa_bias, w_gate_up,
                   k_k, k_a, r_k, ln_g, ln_b):
    B, S, _ = z.shape
    H, N, C = RWKV_HEADS, HEAD_DIM, RWKV_WIDTH
    f32 = jnp.float32
    o3 = 3 * C
    o4 = o3 + DECAY_LORA
    o5 = o4 + AAA_LORA
    r, k, v = z[..., :C], z[..., C:2 * C], z[..., 2 * C:o3]
    xw, xa, xg = z[..., o3:o4], z[..., o4:o5], z[..., o5:]
    w_log = -jax.nn.softplus(-(decay_bias + jnp.tanh(xw) @ w_decay_up)) - 0.5
    decay = jnp.exp(-jnp.exp(w_log.astype(f32)))
    a = jax.nn.sigmoid(aaa_bias + xa @ w_aaa_up)
    g = jax.nn.sigmoid(xg) @ w_gate_up
    kk = (k * k_k).astype(f32).reshape(B, S, H, N)
    kk = kk / jnp.maximum(jnp.sqrt(jnp.sum(kk * kk, axis=-1, keepdims=True)), 1e-12)
    k = k * (1.0 + (a - 1.0) * k_a)

    def time_major(t):
        return t.astype(f32).reshape(B, S, H, N).transpose(1, 0, 2, 3)

    kk_t = kk.transpose(1, 0, 2, 3)
    inputs = (time_major(r), time_major(decay), time_major(k), time_major(v),
              -kk_t, kk_t * time_major(a))

    def step(state, inp):
        r_t, w_t, k_t, v_t, a_t, b_t = inp
        sa = jnp.einsum('bhvk,bhk->bhv', state, a_t)
        state = (state * w_t[:, :, None, :] + sa[..., None] * b_t[:, :, None, :]
                 + v_t[..., None] * k_t[:, :, None, :])
        return state, jnp.einsum('bhvk,bhk->bhv', state, r_t)

    state0 = jnp.zeros((B, H, N, N), f32)
    _, y = lax.scan(step, state0, inputs)
    y = y.transpose(1, 0, 2, 3)
    mu = jnp.mean(y, axis=-1, keepdims=True)
    var = jnp.mean(jnp.square(y - mu), axis=-1, keepdims=True)
    y = ((y - mu) * lax.rsqrt(var + GN_EPS)).reshape(B, S, C)
    y = y * ln_g.astype(f32) + ln_b.astype(f32)
    rh = r.astype(f32).reshape(B, S, H, N)
    kh = k.astype(f32).reshape(B, S, H, N)
    vh = v.astype(f32).reshape(B, S, H, N)
    bonus = (jnp.sum(rh * kh * r_k.astype(f32), axis=-1, keepdims=True) * vh).reshape(B, S, C)
    return ((y + bonus) * g.astype(f32)).astype(z.dtype)

def moba_attention(q, k, v):
    B, S, H, Dh = q.shape
    f32 = jnp.float32
    n_blk = -(-S // MOBA_BLOCK)
    S_pad = n_blk * MOBA_BLOCK
    pad = ((0, 0), (0, S_pad - S), (0, 0), (0, 0))
    qt = jnp.pad(q, pad).transpose(0, 2, 1, 3)
    kt = jnp.pad(k, pad).transpose(0, 2, 1, 3)
    vt = jnp.pad(v, pad).transpose(0, 2, 1, 3)
    kb = kt.reshape(B, H, n_blk, MOBA_BLOCK, Dh)
    vb = vt.reshape(B, H, n_blk, MOBA_BLOCK, Dh)
    k_mean = jnp.mean(kb.astype(f32), axis=3)
    gate = jnp.einsum('bhsd,bhnd->bhsn', qt.astype(f32), k_mean)
    q_blk = jnp.arange(S_pad) // MOBA_BLOCK
    past = jnp.arange(n_blk)[None, :] < q_blk[:, None]
    gate = jnp.where(past, gate, -jnp.inf)
    n_sel = min(MOBA_TOPK, n_blk)
    _, sel = lax.top_k(gate, n_sel)
    slot_ok = jnp.arange(n_sel)[None, :] < q_blk[:, None]
    b_idx = jnp.arange(B)[:, None, None, None]
    h_idx = jnp.arange(H)[None, :, None, None]
    scale = Dh ** -0.5
    q_off = jnp.arange(Q_CHUNK)
    k_off = jnp.arange(MOBA_BLOCK)
    n_keys_sel = n_sel * MOBA_BLOCK

    def attend_chunk(c):
        start = c * Q_CHUNK
        blk = start // MOBA_BLOCK
        q_c = lax.dynamic_slice_in_dim(qt, start, Q_CHUNK, axis=2)
        sel_c = lax.dynamic_slice_in_dim(sel, start, Q_CHUNK, axis=2)
        ok_c = lax.dynamic_slice_in_dim(slot_ok, start, Q_CHUNK, axis=0)
        k_sel = kb[b_idx, h_idx, sel_c]
        v_sel = vb[b_idx, h_idx, sel_c]
        k_own = lax.dynamic_index_in_dim(kb, blk, axis=2, keepdims=False)
        v_own = lax.dynamic_index_in_dim(vb, blk, axis=2, keepdims=False)
        s_sel = jnp.einsum('bhqd,bhqnkd->bhqnk', q_c, k_sel, preferred_element_type=f32) * scale
        s_sel = jnp.where(ok_c[None, None, :, :, None], s_sel, -jnp.inf)
        s_own = jnp.einsum('bhqd,bhkd->bhqk', q_c, k_own, preferred_element_type=f32) * scale
        causal = (blk * MOBA_BLOCK + k_off)[None, :] <= (start + q_off)[:, None]
        s_own = jnp.where(causal, s_own, -jnp.inf)
        s_all = jnp.concatenate([s_sel.reshape(B, H, Q_CHUNK, n_keys_sel), s_own], axis=-1)
        p = jax.nn.softmax(s_all, axis=-1).astype(v.dtype)
        p_sel = p[..., :n_keys_sel].reshape(B, H, Q_CHUNK, n_sel, MOBA_BLOCK)
        p_own = p[..., n_keys_sel:]
        o = (jnp.einsum('bhqnk,bhqnkd->bhqd', p_sel, v_sel, preferred_element_type=f32)
             + jnp.einsum('bhqk,bhkd->bhqd', p_own, v_own, preferred_element_type=f32))
        return o.astype(v.dtype)

    out = lax.map(attend_chunk, jnp.arange(S_pad // Q_CHUNK))
    out = out.transpose(1, 0, 3, 2, 4).reshape(B, S_pad, H * Dh)
    return out[:, :S]

def conv_ffn(h, w_up, conv_w, conv_b, w_down):
    u = h @ w_up
    a, b = u[..., :D_FF_2], u[..., D_FF_2:]
    a = lax.conv_general_dilated(
        a, conv_w.reshape(CONV_WIDTH, 1, D_FF_2), window_strides=(1,),
        padding=[(CONV_WIDTH - 1, 0)], dimension_numbers=('NWC', 'WIO', 'NWC'),
        feature_group_count=D_FF_2) + conv_b
    return (jax.nn.gelu(a, approximate=False) * b) @ w_down

def second_inputs(seed: int = 0) -> dict:
    key = jax.random.key(seed)
    ks = iter(jax.random.split(key, 32))
    L = DEPTH
    f32 = jnp.float32

    def nrm(shape, scale):
        return jax.random.normal(next(ks), shape, f32) * scale

    def unif(shape, lo, hi):
        return jax.random.uniform(next(ks), shape, f32, lo, hi)

    x = nrm((BATCH, SEQ, D_MODEL), 1.0)
    positions = jnp.broadcast_to(jnp.arange(SEQ, dtype=jnp.int32), (BATCH, SEQ))
    return {
        'x': x,
        'positions': positions,
        'norm1_g': 1.0 + nrm((L, D_MODEL), 0.02),
        'w_in': nrm((L, D_MODEL, IN_COLS), D_MODEL ** -0.5),
        'rwkv_mu': unif((L, RWKV_IN), 0.0, 1.0),
        'w_decay_up': nrm((L, DECAY_LORA, RWKV_WIDTH), 0.5 * DECAY_LORA ** -0.5),
        'decay_bias': unif((L, RWKV_WIDTH), -6.5, -1.5),
        'w_aaa_up': nrm((L, AAA_LORA, RWKV_WIDTH), 0.5 * AAA_LORA ** -0.5),
        'aaa_bias': nrm((L, RWKV_WIDTH), 0.1),
        'w_gate_up': nrm((L, GATE_LORA, RWKV_WIDTH), GATE_LORA ** -0.5),
        'rwkv_k_k': 0.85 + nrm((L, RWKV_WIDTH), 0.05),
        'rwkv_k_a': 1.0 + nrm((L, RWKV_WIDTH), 0.05),
        'rwkv_r_k': nrm((L, RWKV_HEADS, HEAD_DIM), 0.1),
        'rwkv_ln_g': 1.0 + nrm((L, RWKV_WIDTH), 0.02),
        'rwkv_ln_b': nrm((L, RWKV_WIDTH), 0.02),
        'q_norm_g': 1.0 + nrm((L, HEAD_DIM), 0.02),
        'k_norm_g': 1.0 + nrm((L, HEAD_DIM), 0.02),
        'w_branch_a': nrm((L, RWKV_WIDTH, D_MODEL), RWKV_WIDTH ** -0.5),
        'w_branch_b': nrm((L, MOBA_WIDTH, D_MODEL), MOBA_WIDTH ** -0.5),
        'w_out': nrm((L, D_MODEL, D_MODEL), D_MODEL ** -0.5),
        'norm2_g': 1.0 + nrm((L, D_MODEL), 0.02),
        'w_ffn_up': nrm((L, D_MODEL, 2 * D_FF_2), D_MODEL ** -0.5),
        'ffn_conv_w': nrm((L, CONV_WIDTH, D_FF_2), CONV_WIDTH ** -0.5),
        'ffn_conv_b': nrm((L, D_FF_2), 0.02),
        'w_ffn_down': nrm((L, D_FF_2, D_MODEL), D_FF_2 ** -0.5),
    }

def second_block(x, positions, norm1_g, w_in, rwkv_mu, w_decay_up, decay_bias, w_aaa_up,
              aaa_bias, w_gate_up, rwkv_k_k, rwkv_k_a, rwkv_r_k, rwkv_ln_g, rwkv_ln_b,
              q_norm_g, k_norm_g, w_branch_a, w_branch_b, w_out, norm2_g, w_ffn_up,
              ffn_conv_w, ffn_conv_b, w_ffn_down):
    B, S, _ = x.shape
    for l in range(DEPTH):
        h = rms_norm(x, norm1_g[l])
        proj = h @ w_in[l]
        z_rwkv = proj[..., :RWKV_IN]
        z_moba = proj[..., RWKV_IN:RWKV_IN + MOBA_IN]
        gate_pre = proj[..., RWKV_IN + MOBA_IN:]
        z_rwkv = z_rwkv + rwkv_mu[l] * (shift_right(z_rwkv) - z_rwkv)
        y_a = rwkv7_time_mix(z_rwkv, w_decay_up[l], decay_bias[l], w_aaa_up[l], aaa_bias[l],
                             w_gate_up[l], rwkv_k_k[l], rwkv_k_a[l], rwkv_r_k[l],
                             rwkv_ln_g[l], rwkv_ln_b[l])
        q = z_moba[..., :MOBA_WIDTH].reshape(B, S, MOBA_HEADS, HEAD_DIM)
        k = z_moba[..., MOBA_WIDTH:2 * MOBA_WIDTH].reshape(B, S, MOBA_HEADS, HEAD_DIM)
        v = z_moba[..., 2 * MOBA_WIDTH:].reshape(B, S, MOBA_HEADS, HEAD_DIM)
        q = partial_rope(rms_norm(q, q_norm_g[l]), positions)
        k = partial_rope(rms_norm(k, k_norm_g[l]), positions)
        y_b = moba_attention(q, k, v)
        u_a = y_a @ w_branch_a[l]
        u_b = y_b @ w_branch_b[l]
        g_a = jax.nn.sigmoid(gate_pre[..., :D_MODEL])
        g_b = jax.nn.sigmoid(gate_pre[..., D_MODEL:])
        x = x + (g_a * u_a + g_b * u_b) @ w_out[l]
        h2 = rms_norm(x, norm2_g[l])
        x = x + conv_ffn(h2, w_ffn_up[l], ffn_conv_w[l], ffn_conv_b[l], w_ffn_down[l])
    return x


def setup_inputs(seed=0):
    out = dict(first_inputs(seed))
    for name, value in second_inputs(seed + 1).items():
        if name != "x":
            out[name + "_2"] = value
    return out


def reference(
    x, w_in, b_in, sinks, ln_v_g, ln_v_b, w_spatial, b_spatial, w_out, b_out, ln1_g, ln1_b,
    w_router, b_router, w_gate, b_gate, w_up, b_up, w_down, b_down, ln2_g, ln2_b, positions_2,
    norm1_g_2, w_in_2, rwkv_mu_2, w_decay_up_2, decay_bias_2, w_aaa_up_2, aaa_bias_2,
    w_gate_up_2, rwkv_k_k_2, rwkv_k_a_2, rwkv_r_k_2, rwkv_ln_g_2, rwkv_ln_b_2, q_norm_g_2,
    k_norm_g_2, w_branch_a_2, w_branch_b_2, w_out_2, norm2_g_2, w_ffn_up_2, ffn_conv_w_2,
    ffn_conv_b_2, w_ffn_down_2,
):
    x = first_block(
        x, w_in, b_in, sinks, ln_v_g, ln_v_b, w_spatial, b_spatial, w_out, b_out, ln1_g, ln1_b,
        w_router, b_router, w_gate, b_gate, w_up, b_up, w_down, b_down, ln2_g, ln2_b,
    )
    return second_block(
        x, positions_2, norm1_g_2, w_in_2, rwkv_mu_2, w_decay_up_2, decay_bias_2, w_aaa_up_2,
        aaa_bias_2, w_gate_up_2, rwkv_k_k_2, rwkv_k_a_2, rwkv_r_k_2, rwkv_ln_g_2, rwkv_ln_b_2,
        q_norm_g_2, k_norm_g_2, w_branch_a_2, w_branch_b_2, w_out_2, norm2_g_2, w_ffn_up_2,
        ffn_conv_w_2, ffn_conv_b_2, w_ffn_down_2,
    )


_drawn_inputs = setup_inputs


def setup_inputs(seed=0):
    import zlib

    import numpy as np

    out = dict(_drawn_inputs(seed))
    spreads = {}
    factors = {'b_in': 3.254,
     'sinks': 8.0,
     'ln_v_g': 5.522,
     'ln_v_b': 8.0,
     'b_spatial': 3.985,
     'b_router': 3.525,
     'b_gate': 8.0,
     'b_up': 8.0,
     'b_down': 4.965,
     'norm1_g_2': 4.241,
     'w_decay_up_2': 8.0,
     'aaa_bias_2': 4.257,
     'rwkv_k_k_2': 35.88,
     'rwkv_k_a_2': 3.127,
     'rwkv_ln_g_2': 64.0,
     'rwkv_ln_b_2': 63.68,
     'q_norm_g_2': 22.34,
     'k_norm_g_2': 79.735,
     'norm2_g_2': 14.282,
     'ffn_conv_b_2': 22.184}
    for name, (base, spread) in spreads.items():
        noise = np.random.default_rng([zlib.crc32(name.encode()), seed]).standard_normal(out[name].shape)
        drawn = base * np.exp(spread * noise) if base else spread * noise
        out[name] = jnp.asarray(drawn.astype(out[name].dtype))
    for name, factor in factors.items():
        out[name] = (out[name] * factor).astype(out[name].dtype)
    return out
```

```python
from contextlib import ExitStack

import numpy as np

import concourse.bass as bass
from concourse import mybir

F32 = mybir.dt.float32
BF16 = mybir.dt.bfloat16
I32 = mybir.dt.int32
U32 = mybir.dt.uint32
ALU = mybir.AluOpType
ACT = mybir.ActivationFunctionType
AX = mybir.AxisListType

P = 128
T = 256
TT = T // P
D = 1024
KD = D // P
HD = 64
NQ = 8
G1 = 512
NG = 8
GD = G1 // NG
NE = 32
TOPK = 4
CAP = 64
PASSES = T // CAP
COLS = NE * PASSES + 2
BANK = 512
SLOT = 2048
SLOTS = 12
LN_EPS = 1e-5
ALPHA1 = 2.0 ** 0.25
LIMIT = 7.0
SWIGLU_ALPHA = 1.702
NEG = -1e30
W_QK, W_VUG = 640, 1152

ROWS = [("b_in_vug", W_VUG), ("ln_v_g", G1), ("ln_v_b", G1), ("b_router", NE), ("sinks", NQ),
        ("b_out", D), ("ln1_g", D), ("ln1_b", D), ("ln2_g", D), ("ln2_b", D)]
COLUMNS = [("b_in_qk", 5), ("b_s", NG)]
CONSTS = [("ident", P), ("iota2", P), ("iota32", NE), ("upto", P), ("ones", P), ("causal", P), ("before", P)]


KAPPA = float(np.exp(-0.5))
NP2 = 4
CH = 32
SUB = 16
C2 = 512
FT_N = 22
ROT = 8
NORM_EPS, GN_EPS, ROPE_THETA = 1e-6, 64e-5, 500000.0
WBUF = 4096
LORA = 288

ROWS2 = [("q_norm_g_2", HD), ("k_norm_g_2", HD), ("rwkv_ln_g_2", C2), ("rwkv_ln_b_2", C2)]
COLUMNS2 = [("mu_lora", 3), ("mu_r", NP2), ("mu_k", NP2), ("mu_v", NP2), ("decay_bias_2", NP2), ("aaa_bias_2", NP2),
            ("rwkv_k_k_2", NP2), ("rwkv_k_a_2", NP2), ("rwkv_r_k_2", NP2), ("norm1_g_2", KD), ("norm2_g_2", KD),
            ("conv0", FT_N), ("conv1", FT_N), ("conv2", FT_N), ("ffn_conv_b_2", FT_N)]
CONSTS2 = [("sub_before", P), ("subT_before", P), ("chunkT_upto", P), ("off_subT", P), ("chunkT_before", P), ("chunkT_upto2", P),
           ("head_ones", P), ("head_col", 2), ("chunk_start", T), ("ident64", HD), ("inv_freq", ROT)]


def offsets(parts):
    at, n = {}, 0
    for name, width in parts:
        at[name] = (n, width)
        n += width
    return at, n


def constants():
    i = np.arange(P)
    row, col = i[:, None], i[None, :]
    tab = {
        "ident": np.eye(P), "iota2": np.tile(col % CAP, (P, 1)), "iota32": np.tile(np.arange(NE), (P, 1)),
        "upto": row <= col, "ones": np.ones((P, P)),
        "causal": np.where(col <= row, 0.0, NEG), "before": np.where(col > row, 0.0, NEG),
    }
    return np.concatenate([np.asarray(tab[n], np.float32) for n, _ in CONSTS], axis=1)


def constants2():
    i = np.arange(P)
    row, col = i[:, None], i[None, :]
    chunk, sub = row // CH == col // CH, row // SUB == col // SUB
    t = np.arange(T)
    freq = np.float32(ROPE_THETA) ** (-np.arange(ROT, dtype=np.float32) / np.float32(ROT))
    tab = {
        "sub_before": sub & (col < row), "subT_before": sub & (row < col), "chunkT_upto": chunk & (row <= col),
        "off_subT": chunk & ~sub & (row < col), "chunkT_before": chunk & (row < col), "chunkT_upto2": chunk & (row <= col),
        "head_ones": row // HD == col // HD, "head_col": row // HD == np.arange(2)[None, :],
        "chunk_start": np.tile(t % CH != 0, (P, 1)), "ident64": row % HD == np.arange(HD)[None, :],
        "inv_freq": np.tile(freq, (P, 1)),
    }
    return np.concatenate([np.asarray(tab[n], np.float32) for n, _ in CONSTS2], axis=1)


def program(nc, A, out):
    ctx = ExitStack()
    with ctx:
        def sem(name):
            return ctx.enter_context(nc.semaphore(name))

        def area(name, floats):
            return ctx.enter_context(nc.sbuf_tensor(name, [P, floats], F32))

        ring = area("ring", SLOTS * SLOT)
        work = area("work", 27500)
        bank = [ctx.enter_context(nc.psum_tensor(f"bank{i}", [P, BANK], F32)) for i in range(8)]
        top = [0]

        def take(floats):
            a = work[:, top[0]:top[0] + floats]
            top[0] += floats
            assert top[0] <= 27500, top
            return a

        rows_at, rows_n = offsets(ROWS)
        cols_at, cols_n = offsets(COLUMNS)
        const_at, const_n = offsets(CONSTS)
        const_sb = take(const_n)
        cols_sb = take(cols_n)
        rows_sb = take(rows_n)
        const = lambda n: const_sb[:, const_at[n][0]:sum(const_at[n])]
        colv = lambda n: cols_sb[:, cols_at[n][0]:sum(cols_at[n])]
        rowv = lambda n: rows_sb[:, rows_at[n][0]:sum(rows_at[n])]
        ident = const("ident")
        posm = take(TT * COLS).rearrange("p (t e) -> p t e", t=TT)
        gate_of = take(TT * COLS).rearrange("p (t e) -> p t e", t=TT)
        small = take(320)
        small_at = [0]

        def little(*shape):
            n = int(np.prod(shape))
            a = small[:, small_at[0]:small_at[0] + n]
            small_at[0] += n
            assert small_at[0] <= 320
            return a if len(shape) == 1 else a.rearrange("p (a b) -> p a b", a=shape[0])

        eps1, eps2, eps3, n_iter_f = little(1), little(1), little(1), little(4)
        nmax, den, sink_e = little(TT * NQ), little(TT * NQ), little(TT * NQ)
        g_sum, g_sum2, g_std = little(TT * NG), little(TT * NG), little(TT * NG)
        logits, chosen = little(TT, NE), little(TT, NE)
        top8, top_i, top_f, gates4 = little(TT, 8), little(TT, 8).bitcast(U32), little(TT, TOPK), little(TT, TOPK)
        ntop, gsum, rstd, mv, stats = little(TT), little(TT), little(TT), little(TT, 2), little(2, 6)
        w_router = take(KD * NE).rearrange("p (k e) -> p k e", k=KD)
        n_iter = ctx.enter_context(nc.sbuf_tensor("n_iter", [1, 2], I32))

        xT = ring[:, 22528:24576].rearrange("p (k t) -> p k t", k=KD)
        w_in = ring[:, 0:KD * 1792].rearrange("p (k n) -> p k n", k=KD)
        w_out = ring[:, 14336:22528].rearrange("p (k n) -> p k n", k=KD)
        x_nat = take(TT * D).rearrange("p (t d) -> p t d", t=TT)
        r2_at = top[0]
        wsT_qkT = take(NG * P + 5 * T)
        wsT = wsT_qkT[:, 0:NG * P].rearrange("p (g t) -> p g t", g=NG)
        qkT = wsT_qkT[:, NG * P:].rearrange("p (i t) -> p i t", i=5)
        v_nat = take(TT * P).rearrange("p (t c) -> p t c", t=TT)
        ug = take(2 * TT * G1)
        u_nat = ug[:, 0:TT * G1].rearrange("p (t c) -> p t c", t=TT)
        g_nat = ug[:, TT * G1:].rearrange("p (t c) -> p t c", t=TT)
        prob = take(3 * 1024)
        prob0 = prob[:, 0:1024].rearrange("p (h s) -> p h s", h=NQ)
        prob1 = prob[:, 1024:3072].rearrange("p (h s) -> p h s", h=NQ)
        pT = take(3 * 1024).rearrange("p (j h t) -> p j h t", j=3, h=NQ)
        mixT = take(KD * T).rearrange("p (k t) -> p k t", k=KD)
        sq = take(TT * G1).rearrange("p (t c) -> p t c", t=TT)
        h = ug.rearrange("p (t d) -> p t d", t=TT)
        h_part = prob.bitcast(BF16).rearrange("p (i t d) -> p i t d", i=3, t=TT)
        hT = pT.rearrange("p j h t -> p (j h t)")[:, 0:2048].rearrange("p (k t) -> p k t", k=KD)
        resid = x_nat
        ln_tmp = sq.rearrange("p t c -> p (t c)")
        chosen4 = sq.rearrange("p t c -> p (t c)")[:, 0:TT * TOPK * NE].rearrange("p (t k e) -> p t k e", t=TT, k=TOPK)
        pool1 = mixT.rearrange("p k t -> p (k t)")
        gt, sg, uc, vv = (pool1[:, i * 512:(i + 1) * 512] for i in range(4))
        pool2 = rows_sb[:, rows_at["b_out"][0]:rows_at["b_out"][0] + 3072]
        hid, yy = pool2[:, 0:512], pool2[:, 512:1024]
        hidT = pool2[:, 1024:1536].rearrange("p (j c) -> p j c", j=4)
        x_e = pool2[:, 1536:2048].rearrange("p (k s) -> p k s", k=KD)
        place_g = pool2[:, 2048:2304].rearrange("p (t s) -> p t s", t=TT)
        place_T = pool2[:, 2304:2560]
        place = pool2[:, 2560:2624].bitcast(BF16).rearrange("p (t s) -> p t s", t=TT)
        gateT = pool2[0:NE, 2624:2880]
        b_down_area = take(D)
        b_down = b_down_area[0:NE, :]
        bias_row = wsT_qkT[0:1, 0:2 * D]

        consts_in, x_in, xT_in, mix_rows_in = sem("consts_in"), sem("x_in"), sem("xT_in"), sem("mix_rows_in")
        ln_rows_in, wsT_in, b_down_in = sem("ln_rows_in"), sem("wsT_in"), sem("b_down_in")
        w_in_in = [sem(f"w_in_in{i}") for i in range(4)]
        w_out_in = sem("w_out_in")
        router_in = sem("router_in")
        proj_done, qk_ready, v_ready, ug_biased, ug_gelu = (sem(n) for n in ("proj_done", "qk_ready", "v_ready", "ug_biased", "ug_gelu"))
        wsT_masked, g_normed, mixed_done, sgu_ready = (sem(n) for n in ("wsT_masked", "g_normed", "mixed_done", "sgu_ready"))
        scores_done, neg_max, exp_done, prob_ready = (sem(n) for n in ("scores_done", "neg_max", "exp_done", "prob_ready"))
        pT_done, pT_ready, attn_done, attn_ready, sguT_done, sguT_ready = (
            sem(n) for n in ("pT_done", "pT_ready", "attn_done", "attn_ready", "sguT_done", "sguT_ready"))
        mix_done, var_ready, std_ready, h_ready, hT_done, hT_ready = (
            sem(n) for n in ("mix_done", "var_ready", "std_ready", "h_ready", "hT_done", "hT_ready"))
        logits_done, top_ready, top_exp, chosen_ready, place_done = (
            sem(n) for n in ("logits_done", "top_ready", "top_exp", "chosen_ready", "place_done"))
        iter_ready, gateT_done, gateT_ready, split_ready = (sem(n) for n in ("iter_ready", "gateT_done", "gateT_ready", "split_ready"))
        slot_in = [sem(f"slot_in{i}") for i in range(SLOTS)]
        slots_used = sem("slots_used")
        bias_in, bias_free = sem("bias_in"), sem("bias_free")
        place_ready, place_g_ready, gather_done, x_e_ready = (sem(n) for n in ("place_ready", "place_g_ready", "gather_done", "x_e_ready"))
        gt_ready, sg_ready, uc_ready, vv_ready, hid_ready = (sem(n) for n in ("gt_ready", "sg_ready", "uc_ready", "vv_ready", "hid_ready"))
        hidT_done, hidT_ready, place_T_done, place_T_ready, y_ready = (
            sem(n) for n in ("hidT_done", "hidT_ready", "place_T_done", "place_T_ready", "y_ready"))
        acc_done, x1_ready, stored = (sem(n) for n in ("acc_done", "x1_ready", "stored"))
        rest_ready, g_var, g_stds = sem("rest_ready"), sem("g_var"), sem("g_stds")
        bonus_ready = sem("bonus_ready")
        dve_step = sem("dve_step")

        def views(a, *parts):
            n, got = 0, []
            for shape in parts:
                w = int(np.prod(shape))
                v = a[:, n:n + w]
                names = "abcd"[:len(shape)]
                if len(shape) > 1:
                    v = v.rearrange(f"p ({' '.join(names)}) -> p {' '.join(names)}", **dict(zip(names, shape)))
                got.append(v)
                n += w
            assert n <= a.shape[1], (n, a.shape)
            return got

        rows2_at, rows2_n = offsets(ROWS2)
        cols2_at, cols2_n = offsets(COLUMNS2)
        const2_at, const2_n = offsets(CONSTS2)
        kept = pT.rearrange("p j h t -> p (j h t)")
        const2_sb, cols2_sb, rows2_sb, w_lora_up, pos_f = views(kept, (const2_n,), (cols2_n,), (rows2_n,), (C2,), (TT,))
        pos_i = pos_f.bitcast(I32)
        const2 = lambda n: const2_sb[:, const2_at[n][0]:sum(const2_at[n])]
        col2 = lambda n: cols2_sb[:, cols2_at[n][0]:sum(cols2_at[n])]
        row2 = lambda n: rows2_sb[:, rows2_at[n][0]:sum(rows2_at[n])]
        w_gate_up = views(sq.rearrange("p t c -> p (t c)"), (2, C2))[0]
        r1 = rows_sb
        r2 = work[:, r2_at:r2_at + 7680]
        rt = ring[:, 4 * WBUF:4 * WBUF + 8192]
        x1 = resid
        hnT = views(mixT.rearrange("p k t -> p (k t)"), (KD, T))[0]
        hn = views(r2, (TT, D))[0]
        zr, zk, zv, lora, tmp, sd, aa = views(r1, (NP2, T), (NP2, T), (NP2, T), (3, T), (NP2, T), (NP2, T), (NP2, T))
        cs = tmp
        small2 = r1[:, 6912:rows_n]
        (ss, rms, ss_qk, rs_qk, cosv, sinv, ang, ang_n, nmax2, den2, bonus, y_sum, y_sum2, y_std) = views(
            small2, (TT,), (TT,), (2 * TT * NQ,), (2 * TT * NQ,), (TT, ROT), (TT, ROT), (TT, ROT), (TT, ROT),
            (TT * NQ,), (TT * NQ,), (TT, NQ), (TT * NQ,), (TT * NQ,), (TT * NQ,))
        ar, b_hat, k_hat, e_pos, g_gate, ybT = views(r2, (NP2, 2, T), (NP2, T), (NP2, T), (NP2, T), (TT, C2), (NP2, T))
        qk2, _, qkT2, prob_2 = views(rt, (2, TT, C2), (1024,), (2, NP2, T), (3072,))
        pT2 = views(rt, (3, NQ, P))[0]
        sq2 = views(rt[:, 5120:7168], (2, TT, C2))[0]
        rope_t = views(rt[:, 7168:7680], (2, TT * NQ, ROT))[0]
        prob2_0, prob2_1 = views(prob_2, (NQ, P), (NQ, T))
        v2 = views(b_down_area, (TT, C2))[0]
        _, e_neg, e_before, kk, kk2, nrm = views(rt, (3072,), (NP2, T), (NP2, T), (NP2, T), (NP2, T), (NP2, T))
        x0, = views(r1, (TT, NQ, P))
        vn, bn, kn = views(r1[:, 3840:6912], (TT, C2), (TT, C2), (TT, C2))
        batch = []
        for b, a in enumerate((rt, ring[:, 2 * WBUF:4 * WBUF])):
            names = "Mb MA MoT NK P2 PU X1".split()
            parts = [(4, P), (4, 2, P), (4, P), (4, 2, P), (4, P), (4, 2, P), (4, P)]
            batch.append(dict(zip(names, views(a, *parts))))
        ft, hs, rT = views(rt[:, 5120:8192], (4, NP2, HD), (4, NP2, HD), (NP2, P))
        y2, state, st_tmp = views(ring[:, 2 * WBUF + 5120:4 * WBUF], (TT, C2), (NP2, HD), (NP2, HD))
        sqy, bv = views(r1, (TT, C2), (TT, C2))
        yaT = views(r2, (NP2, T))[0]
        sga, sgb, mm, mT = views(r1, (TT, BANK), (TT, BANK), (TT, D), (KD, T))
        hn2 = views(r1, (TT, D))[0]
        conv, hid2 = views(r2[:, 1024:2048], (2, T), (2, T))
        out_sb = views(r1[:, 2048:4096], (TT, D))[0]
        ffu = [ring[:, 4 * WBUF + 2048 * i:4 * WBUF + 2048 * (i + 1)].rearrange("p (c k n) -> p c k n", c=2, k=KD) for i in range(2)]
        ffd = [ring[:, 5 * WBUF + 1024 * i:5 * WBUF + 1024 * (i + 1)] for i in range(2)]

        FILLS = ["lora", "r", "k", "v", "q2", "k2", "v2", "branch_a", "branch_b", "gate_a0", "gate_b0", "gate_a1", "gate_b1", "out0", "out1"]
        BUFFER = [0, 1, 2, 3, 0, 1, 2, 0, 1, 2, 3, 2, 3, 0, 1]
        BEFORE = [None, None, None, None, "lora", "r", "k", "q2", "k2", None, None, "gate_a0", "gate_b0", "branch_a", "branch_b"]
        at2 = {f: ring[:, b * WBUF:(b + 1) * WBUF] for f, b in zip(FILLS, BUFFER)}

        def by_k(f, k):
            a = at2[f] if f != "lora" else at2[f][:, 0:KD * LORA]
            return a.rearrange("p (k n) -> p k n", k=k)

        small2_in, rows2_in = sem("small2_in"), sem("rows2_in")
        w2_in, w2_used = [sem(f"w2_in{b}") for b in range(4)], sem("w2_used")
        USES = ["lora", "r", "k", "v", "q2", "k2", "v2", "gate_a0", "branch_a", "gate_b0", "branch_b",
                "gate_a1", "branch_a", "gate_b1", "branch_b"]

        def fill_count(f):
            return 16 * BUFFER[:FILLS.index(f) + 1].count(BUFFER[FILLS.index(f)])

        def use_count(f, use=1):
            return [n + 1 for n, g in enumerate(USES) if g == f][use - 1]

        sq_done, rms_std, hn_ready = (sem(n) for n in ("sq_done", "rms_std", "hn_ready"))
        z_raw, lora_mixed, lora_ready, zv_ready, kk2_ready, cs_ready, exp3_ready = (
            sem(n) for n in ("z_raw", "lora_mixed", "lora_ready", "zv_ready", "kk2_ready", "cs_ready", "exp3_ready"))
        lora_up_done, sd_ready, aa_ready, g_ready, nrm_done, nrm_ready = (
            sem(n) for n in ("lora_up_done", "sd_ready", "aa_ready", "g_ready", "nrm_done", "nrm_ready"))
        rk_ready, bonus_done, hats_ready, nat_done, nat_ready = (sem(n) for n in ("rk_ready", "bonus_done", "hats_ready", "nat_done", "nat_ready"))
        qkv2_raw, ang_ready, trig_ready, ss_ready, rs_ready, qk2_ready, qkT2_done, qkT2_ready = (
            sem(n) for n in ("qkv2_raw", "ang_ready", "trig_ready", "ss_ready", "rs_ready", "qk2_ready", "qkT2_done", "qkT2_ready"))
        tensor_steps = ["m", "nk", "p2", "nv", "p4", "p8", "du", "x1", "x2", "x3", "rT", "fh"]
        scalar_steps = ["P2", "x0", "P4", "P8", "X1", "X2"]
        vector_steps = ["Mb", "MA", "NK", "U2", "U4", "U8", "X3", "rT", "FH"]
        rec_done, rec_copied, rec_ready = sem("rec_done"), sem("rec_copied"), sem("rec_ready")
        one_added, st_done, st_ready, y2_done, y2_ready = (sem(n) for n in ("one_added", "st_done", "st_ready", "y2_done", "y2_ready"))

        def count(steps, step, tt, b):
            return (tt * len(steps) + steps.index(step)) * 2 + b + 1

        ya_ready = sem("ya_ready")
        u_done, sg_a, mm_ready, x2_ready = (sem(n) for n in ("u_done", "sg_a", "mm_ready", "x2_ready"))
        ffu_in, ffu_used, ffd_in, ffd_used = ([sem(f"{n}{i}") for i in range(2)] for n in ("ffu_in", "ffu_used", "ffd_in", "ffd_used"))
        conv1, conv2, conv_ready, gelu_ready, hid2_ready = (
            [sem(f"{n}{i}") for i in range(2)] for n in ("conv1", "conv2", "conv_ready", "gelu_ready", "hid2_ready"))
        ffn_done, out_ready = sem("ffn_done"), [sem(f"out_ready{t}") for t in range(TT)]

        block = ctx.enter_context(nc.Block())

        def expert_slot(e, j):
            which, c = (("w_gate", "w_up")[j % 2], j // 2) if j < 8 else ("w_down", j - 8)
            return A[which][bass.ds(e, 1), c * 256:(c + 1) * 256, :].rearrange("o (k p) n -> p (o k) n", p=P)

        def slot_view(j):
            return ring[:, j * SLOT:(j + 1) * SLOT].rearrange("p (k n) -> p k n", k=2)

        @block.sync
        def _(sp):
            sp.dma_start(xT, A["xT"]).then_inc(xT_in, 16)
            sp.dma_start(const_sb, A["consts"]).then_inc(consts_in, 16)
            sp.dma_start(cols_sb, A["columns"]).then_inc(consts_in, 16)
            for i in range(4):
                sp.dma_start(w_in[:, 2 * i:2 * i + 2, :], A["w_in"][:, 2 * i:2 * i + 2, :]).then_inc(w_in_in[i], 16)
            mix_n = rows_at["b_out"][0]
            sp.dma_start(rows_sb[:, 0:mix_n], A["rows"][0:mix_n].partition_broadcast(P)).then_inc(mix_rows_in, 16)
            sp.dma_start(wsT, A["wsT"]).then_inc(wsT_in, 16)
            for i in range(4):
                sp.dma_start(w_out[:, 2 * i:2 * i + 2, :], A["w_out"][:, 2 * i:2 * i + 2, :]).then_inc(w_out_in, 16)
            sp.dma_start(x_nat, A["x"].rearrange("(t p) d -> p t d", p=P)).then_inc(x_in, 16)
            sp.dma_start(rows_sb[:, mix_n:rows_n], A["rows"][mix_n:rows_n].partition_broadcast(P)).then_inc(ln_rows_in, 16)
            sp.dma_start(b_down, A["b_down"]).then_inc(b_down_in, 16)
            sp.wait_ge(proj_done, 7)
            for j in range(SLOTS):
                if j == 7:
                    sp.wait_ge(mix_done, 4)
                    sp.dma_start(bias_row, A["b_gate_up"][0:1, :]).then_inc(bias_in, 16)
                sp.dma_start(slot_view(j), expert_slot(0, j)).then_inc(slot_in[j], 16)
            sp.wait_ge(iter_ready, 1)
            sp.dma_start(const2_sb, A["consts2"]).then_inc(small2_in, 16)
            sp.dma_start(cols2_sb, A["columns2"]).then_inc(small2_in, 16)
            sp.dma_start(w_lora_up, A["w_lora_up"]).then_inc(small2_in, 16)
            sp.dma_start(w_gate_up[:, 0, :], A["w_gate_up_2"][0:P, :]).then_inc(small2_in, 16)
            sp.dma_start(w_gate_up[0:CH, 1, :], A["w_gate_up_2"][P:, :]).then_inc(small2_in, 16)
            sp.dma_start(pos_i, A["pos"]).then_inc(small2_in, 16)
            sp.dma_start(rows2_sb, A["rows2"].partition_broadcast(P)).then_inc(rows2_in, 16)
            n = sp.value_load(n_iter[0:1, 0:1], min_val=NE, max_val=NE * PASSES)
            n_rest = sp.value_load(n_iter[0:1, 1:2], min_val=NE - 1, max_val=NE * PASSES - 1)
            with sp.Fori(1, n) as it:
                e = it % NE
                sp.wait_ge(bias_free, it)
                sp.dma_start(bias_row, A["b_gate_up"][bass.ds(e, 1), :]).then_inc(bias_in, 16)
                for j in range(SLOTS):
                    sp.wait_ge(slots_used, sp.snap(it * SLOTS - (SLOTS - j - 1)))
                    sp.dma_start(slot_view(j), expert_slot(e, j)).then_inc(slot_in[j], 16)
            for f, b, used in zip(FILLS, BUFFER, BEFORE):
                if used is not None:
                    sp.wait_ge(w2_used, use_count(used, USES.count(used)))
                elif f == "gate_a0":
                    sp.wait_ge(y2_ready, 4)
                elif f == "gate_b0":
                    sp.wait_ge(sguT_done, 2)
                else:
                    sp.wait_ge(slots_used, sp.snap(n_rest * SLOTS + 2 * b + 2))
                width = KD * LORA if f == "lora" else WBUF
                sp.dma_start(at2[f][:, 0:width], A[f"w2_{f}"]).then_inc(w2_in[b], 16)
            for i in range(2):
                sp.dma_start(ffu[i].rearrange("p c k n -> p (c k n)"), A["ffn_up"][i]).then_inc(ffu_in[i], 16)
                sp.dma_start(ffd[i], A["ffn_down"][i * P:(i + 1) * P, :]).then_inc(ffd_in[i], 16)
            with sp.Fori(1, FT_N // 2) as it:
                for i in range(2):
                    j = it * 2 + i
                    sp.wait_ge(ffu_used[i], it)
                    sp.dma_start(ffu[i].rearrange("p c k n -> p (c k n)"),
                                 A["ffn_up"][bass.ds(j, 1), :, :].rearrange("o p n -> p (o n)")).then_inc(ffu_in[i], 16)
                    sp.wait_ge(ffd_used[i], it)
                    sp.dma_start(ffd[i], A["ffn_down"][bass.ds(j * P, P), :]).then_inc(ffd_in[i], 16)
            for t in range(TT):
                sp.wait_ge(out_ready[t], 2)
                sp.dma_start(out[t * P:(t + 1) * P, :], out_sb[:, t, :]).then_inc(stored, 16)
            sp.wait_ge(stored, 32)

        @block.tensor
        def _(pe):
            pe.wait_ge(xT_in, 16)
            for k in range(KD):
                first, last = k == 0, k == KD - 1
                if k % 2 == 0:
                    pe.wait_ge(w_in_in[k // 2], 16)
                for i in range(5):
                    ins = pe.matmul(bank[i // 2][:, (i % 2) * T:(i % 2 + 1) * T], w_in[:, k, i * P:(i + 1) * P], xT[:, k, :],
                                    start=first and i % 2 == 0, stop=last, skip_group_check=True)
                if last:
                    ins.then_inc(proj_done, 1)
                for c in range(3):
                    for t in range(TT):
                        to = bank[2][:, T + t * P:T + (t + 1) * P] if c == 0 else bank[3 + 2 * (c - 1) + t][:, :]
                        lo = W_QK + (0 if c == 0 else P + (c - 1) * G1)
                        ins = pe.matmul(to, xT[:, k, t * P:(t + 1) * P], w_in[:, k, lo:lo + (P if c == 0 else G1)],
                                        start=first and c > 0, stop=last, skip_group_check=True)
                        if last:
                            ins.then_inc(proj_done, 1)
            pe.wait_ge(qk_ready, 5)
            pe.wait_ge(v_ready, 2)
            s1_bank = [0, 1, 2, 7]
            for i in range(4):
                for half in range(2):
                    lo = half * HD
                    ins = pe.matmul(bank[s1_bank[2 * half + i // 2]][:, (i % 2) * T:(i % 2 + 1) * T],
                                    qkT[lo:lo + HD, i, P:T], qkT[lo:lo + HD, 4, :],
                                    start=i % 2 == 0, stop=True, skip_group_check=True)
            ins.then_inc(scores_done, 1)
            pe.wait_ge(ug_biased, 2)
            for i in range(4):
                for half in range(2):
                    lo = half * HD
                    ins = pe.matmul(bank[3 + half][:, i * P:(i + 1) * P], qkT[lo:lo + HD, i, 0:P], qkT[lo:lo + HD, 4, 0:P],
                                    start=i == 0, stop=True, skip_group_check=True)
            ins.then_inc(scores_done, 1)
            pe.wait_ge(ug_biased, 4)
            pe.wait_ge(wsT_masked, 1)
            pe.wait_ge(g_normed, 1)
            for g in range(NG):
                ins = pe.matmul(bank[5 + g // 4][:, (g % 4) * P:(g % 4 + 1) * P].rearrange("p (c d) -> p c d", c=TT),
                                wsT[:, g, :], g_nat[:, :, g * GD:(g + 1) * GD],
                                start=g % 4 == 0, stop=True, skip_group_check=True)
            ins.then_inc(mixed_done, 1)
            pe.wait_ge(prob_ready, 2)
            t_bank = [[3, 4], [0, 1], [2, 7]]
            for j in range(3):
                for hh in range(NQ):
                    src = prob0[:, hh, :] if j == 0 else prob1[:, hh, (j - 1) * P:j * P]
                    ins = pe.transpose(bank[t_bank[j][hh // 4]][:, (hh % 4) * P:(hh % 4 + 1) * P], src, ident)
                ins.then_inc(pT_done, 1)
            pe.wait_ge(sgu_ready, 1)
            for c in range(4):
                for t in range(TT):
                    ins = pe.transpose(bank[5 + c // 2][:, (c % 2) * T + t * P:(c % 2) * T + (t + 1) * P],
                                       u_nat[:, t, c * P:(c + 1) * P], ident)
            ins.then_inc(sguT_done, 1)
            pe.wait_ge(pT_ready, 3)
            for hh in range(NQ):
                kv = hh // 4 * HD
                half = hh % 2 * HD
                for t in range(TT):
                    to = bank[3 + hh // 4][half:half + HD, (hh // 2 % 2) * T + t * P:(hh // 2 % 2) * T + (t + 1) * P]
                    fresh = hh // 2 % 2 == 0 and t == 0
                    if t == 0:
                        ins = pe.matmul(to, v_nat[:, 0, kv:kv + HD], pT[:, 0, hh, :], start=fresh, stop=True, skip_group_check=True)
                    else:
                        pe.matmul(to, v_nat[:, 0, kv:kv + HD], pT[:, 1, hh, :], start=False, stop=False, skip_group_check=True)
                        ins = pe.matmul(to, v_nat[:, 1, kv:kv + HD], pT[:, 2, hh, :], start=False, stop=True, skip_group_check=True)
            ins.then_inc(attn_done, 1)
            pe.wait_ge(attn_ready, 2)
            pe.wait_ge(sguT_ready, 2)
            pe.wait_ge(w_out_in, 4 * 16)
            mix_bank = [[0, 1], [2, 7]]
            for t in range(TT):
                for n in range(2):
                    for k in range(KD):
                        ins = pe.matmul(bank[mix_bank[t][n]][:, :], mixT[:, k, t * P:(t + 1) * P], w_out[:, k, n * BANK:(n + 1) * BANK],
                                        start=k == 0, stop=k == KD - 1)
                    ins.then_inc(mix_done, 1)
            for t in range(TT):
                pe.wait_ge(h_ready, t + 1)
                for k in range(KD):
                    ins = pe.transpose(bank[3 + 2 * t + k // 4][:, (k % 4) * P:(k % 4 + 1) * P], h[:, t, k * P:(k + 1) * P], ident)
                ins.then_inc(hT_done, 1)
            pe.wait_ge(router_in, 16)
            pe.wait_ge(hT_ready, 4)
            for t in range(TT):
                for k in range(KD):
                    ins = pe.matmul(bank[7][:, t * NE:(t + 1) * NE], hT[:, k, t * P:(t + 1) * P], w_router[:, k, :],
                                    start=k == 0, stop=k == KD - 1, skip_group_check=True)
            ins.then_inc(logits_done, 1)
            pe.wait_ge(chosen_ready, 1)
            m0, m1 = chosen[:, 0, :], chosen[:, 1, :]
            pe.matmul(bank[3][:, 0:NE], const("upto"), m0, start=True, stop=True, skip_group_check=True)
            pe.matmul(bank[3][:, NE:2 * NE], const("ones"), m0, start=False, stop=False, skip_group_check=True)
            pe.matmul(bank[3][:, NE:2 * NE], const("upto"), m1, start=False, stop=True, skip_group_check=True).then_inc(place_done, 1)
            pe.matmul(bank[4][0:1, 0:NE], const("ones")[:, 0:1], m0, start=True, stop=False)
            pe.matmul(bank[4][0:1, 0:NE], const("ones")[:, 0:1], m1, start=False, stop=True).then_inc(place_done, 1)
            pe.wait_ge(chosen_ready, 2)
            for t in range(TT):
                ins = pe.transpose(bank[5][0:NE, t * P:(t + 1) * P], gate_of[:, t, 0:NE], ident)
            ins.then_inc(gateT_done, 1)
            pe.wait_ge(gateT_ready, 1)
            pe.wait_ge(b_down_in, 16)
            pe.wait_ge(iter_ready, 1)
            for t in range(TT):
                for n in range(2):
                    pe.matmul(bank[2 * t + n][:, :], gateT[:, t * P:(t + 1) * P], b_down[:, n * BANK:(n + 1) * BANK],
                              start=True, stop=False, skip_group_check=True)

            gate_bank, up_bank, x_bank, y_bank = bank[4], bank[5], bank[6], bank[7]

            def gather():
                for k in range(KD):
                    for n, (t, part) in enumerate((t, part) for t in range(TT) for part in range(3)):
                        ins = pe.matmul(x_bank[:, k * CAP:(k + 1) * CAP], h_part[:, part, t, k * P:(k + 1) * P], place[:, t, :],
                                        start=n == 0, stop=n == 5, skip_group_check=True)
                ins.then_inc(gather_done, 1)

            def scatter(stop):
                for t in range(TT):
                    for n in range(2):
                        lo = n * CAP
                        ins = pe.matmul(bank[2 * t + n][:, :], place_T[lo:lo + CAP, t * P:(t + 1) * P], yy[lo:lo + CAP, :],
                                        start=False, stop=stop, skip_group_check=True)
                return ins

            pe.wait_ge(split_ready, 3)
            pe.wait_ge(place_ready, 1)
            gather()
            n = pe.value_load(n_iter[0:1, 0:1], min_val=NE, max_val=NE * PASSES)
            with pe.Fori(0, n) as it:
                now, ahead, landed = pe.snap(it + 1), pe.snap(it + 2), pe.snap(it * 16 + 16)
                pe.wait_ge(x_e_ready, now)
                pe.wait_ge(place_T_ready, now)
                pe.wait_ge(bias_in, landed)
                for b, to in enumerate((gate_bank, up_bank)):
                    for n2 in range(2):
                        ins = pe.matmul(to[n2 * CAP:(n2 + 1) * CAP, :], const("ones")[0:1, 0:CAP],
                                        bias_row[:, b * D + n2 * BANK:b * D + (n2 + 1) * BANK], start=True, stop=False)
                ins.then_inc(bias_free, 1)
                for j in range(8):
                    to = (gate_bank, up_bank)[j % 2]
                    pe.wait_ge(slot_in[j], landed)
                    for kk in range(2):
                        for n2 in range(2):
                            ins = pe.matmul(to[n2 * CAP:(n2 + 1) * CAP, :], x_e[:, j // 2 * 2 + kk, :],
                                            slot_view(j)[:, kk, n2 * BANK:(n2 + 1) * BANK],
                                            start=False, stop=j >= 6 and kk == 1)
                    ins.then_inc(slots_used, 1)
                pe.wait_ge(place_ready, ahead)
                gather()
                pe.wait_ge(y_ready, now)
                scatter(False)
                pe.wait_ge(hid_ready, now)
                for j in range(4):
                    ins = pe.transpose(gate_bank[:, j * P:(j + 1) * P], hid[:, j * P:(j + 1) * P], ident)
                ins.then_inc(hidT_done, 1)
                pe.wait_ge(place_g_ready, now)
                for t in range(TT):
                    ins = pe.transpose(up_bank[:, t * P:(t + 1) * P], place_g[:, t, :], ident)
                ins.then_inc(place_T_done, 1)
                pe.wait_ge(hidT_ready, now)
                for j in range(4):
                    pe.wait_ge(slot_in[8 + j], landed)
                    for kk in range(2):
                        k = 2 * j + kk
                        for n2 in range(2):
                            ins = pe.matmul(y_bank[n2 * CAP:(n2 + 1) * CAP, :], hidT[:, k % 4, k // 4 * CAP:(k // 4 + 1) * CAP],
                                            slot_view(8 + j)[:, kk, n2 * BANK:(n2 + 1) * BANK], start=k == 0, stop=k == 7)
                    ins.then_inc(slots_used, 1)
            pe.wait_ge(y_ready, pe.snap(n + 1))
            pe.wait_ge(place_T_ready, pe.snap(n + 1))
            scatter(True).then_inc(acc_done, 1)

            def transpose_hn(src, before):
                for t in range(TT):
                    pe.wait_ge(hn_ready, before + t + 1)
                    for k in range(KD):
                        ins = pe.transpose(bank[4 + 2 * t + k // 4][:, (k % 4) * P:(k % 4 + 1) * P], src[:, t, k * P:(k + 1) * P], ident)
                    ins.then_inc(hT_done, 1)

            transpose_hn(hn, 0)
            pe.wait_ge(hT_ready, 8)

            def project_T(f, pair):
                pe.wait_ge(w2_in[BUFFER[FILLS.index(f)]], fill_count(f))
                w = by_k(f, KD)
                for i in range((w.shape[2] + P - 1) // P):
                    m = min(P, w.shape[2] - i * P)
                    for k in range(KD):
                        ins = pe.matmul(bank[2 * pair + i // 2][0:m, (i % 2) * T:(i % 2 + 1) * T], w[:, k, i * P:i * P + m], hnT[:, k, :],
                                        start=k == 0, stop=k == KD - 1, skip_group_check=True)
                ins.then_inc(w2_used, 1)

            def project(f, pair):
                pe.wait_ge(w2_in[BUFFER[FILLS.index(f)]], fill_count(f))
                for t in range(TT):
                    for k in range(KD):
                        ins = pe.matmul(bank[2 * pair + t][:, :], hnT[:, k, t * P:(t + 1) * P], by_k(f, KD)[:, k, :],
                                        start=k == 0, stop=k == KD - 1)
                ins.then_inc(w2_used, 1)

            for n2, f in enumerate(("lora", "r", "k", "v")):
                project_T(f, (n2 + 3) % 4)
            pe.wait_ge(small2_in, 96)
            pe.wait_ge(lora_ready, 1)
            for i in range(NP2):
                ins = pe.matmul(bank[6 + i // 2][:, (i % 2) * T:(i % 2 + 1) * T], w_lora_up[0:HD, i * P:(i + 1) * P], lora[0:HD, 0, :],
                                start=True, stop=True, skip_group_check=True)
            ins.then_inc(lora_up_done, 1)
            pe.wait_ge(z_raw, 4)
            for i in range(NP2):
                ins = pe.matmul(bank[i // 2][:, (i % 2) * T:(i % 2 + 1) * T], w_lora_up[HD:P, i * P:(i + 1) * P], lora[HD:P, 0, :],
                                start=True, stop=True, skip_group_check=True)
            ins.then_inc(lora_up_done, 1)
            pe.wait_ge(z_raw, 6)
            pe.wait_ge(lora_ready, 3)
            for t in range(TT):
                pe.matmul(bank[2 + t][:, :], lora[:, 1, t * P:(t + 1) * P], w_gate_up[:, 0, :], start=True, stop=False)
                ins = pe.matmul(bank[2 + t][:, :], lora[0:CH, 2, t * P:(t + 1) * P], w_gate_up[0:CH, 1, :], start=False, stop=True)
            ins.then_inc(lora_up_done, 1)
            pe.wait_ge(z_raw, 8)
            project("q2", 2)
            pe.wait_ge(kk2_ready, 1)
            pe.wait_ge(sd_ready, 4)
            for b in range(2):
                ins = pe.matmul(bank[6 + b][:, :].rearrange("p (i t) -> p i t", i=2), const2("head_ones"), kk2[:, 2 * b:2 * b + 2, :],
                                start=True, stop=True)
            ins.then_inc(nrm_done, 1)
            pe.wait_ge(aa_ready, 4)
            project("k2", 0)
            pe.wait_ge(g_ready, 2)
            project("v2", 1)
            pe.wait_ge(rk_ready, 1)
            pe.wait_ge(nrm_ready, 2)
            for t in range(TT):
                for i in range(NP2):
                    ins = pe.matmul(bank[6][:, t * NQ + 2 * i:t * NQ + 2 * i + 2], kk2[:, i, t * P:(t + 1) * P], const2("head_col"),
                                    start=t == 0 and i == 0, stop=True, skip_group_check=True)
            ins.then_inc(bonus_done, 1)
            pe.wait_ge(hats_ready, 1)
            pe.wait_ge(qkv2_raw, 6)
            for y in (1, 2, 0, 3):
                if y == 3:
                    pe.wait_ge(bonus_ready, 1)
                for t in range(TT):
                    for i in range(NP2):
                        src = (ar[:, i, 0, :], b_hat[:, i, :], k_hat[:, i, :], zv[:, i, :])[y][:, t * P:(t + 1) * P]
                        ins = pe.transpose(bank[2 * y + t][:, i * P:(i + 1) * P], src, ident)
                    ins.then_inc(nat_done, 1)

            pe.wait_ge(nat_ready, 8)
            pe.wait_ge(qk2_ready, 1)
            for w in range(2):
                for i in range(NP2):
                    for t in range(TT):
                        ins = pe.transpose(bank[2 * w + i // 2][:, (i % 2) * T + t * P:(i % 2) * T + (t + 1) * P],
                                           qk2[:, w, t, i * P:(i + 1) * P], ident)
            ins.then_inc(qkT2_done, 1)
            pe.wait_ge(qkT2_ready, 4)
            for i in range(NP2):
                for half in range(2):
                    lo = half * HD
                    ins = pe.matmul(bank[4 + 2 * half + i // 2][:, (i % 2) * T:(i % 2 + 1) * T], qkT2[lo:lo + HD, 0, i, P:T],
                                    qkT2[lo:lo + HD, 1, i, :], start=i % 2 == 0, stop=True, skip_group_check=True)
            ins.then_inc(scores_done, 1)
            for i in range(NP2):
                for half in range(2):
                    lo = half * HD
                    ins = pe.matmul(bank[half][:, i * P:(i + 1) * P], qkT2[lo:lo + HD, 0, i, 0:P], qkT2[lo:lo + HD, 1, i, 0:P],
                                    start=i == 0, stop=True, skip_group_check=True)
            ins.then_inc(scores_done, 1)
            pe.wait_ge(prob_ready, 4)
            for j in range(3):
                for m in range(NQ):
                    src = prob2_0[:, m, :] if j == 0 else prob2_1[:, m, (j - 1) * P:j * P]
                    ins = pe.transpose(bank[2 * j + m // 4][:, (m % 4) * P:(m % 4 + 1) * P], src, ident)
                ins.then_inc(pT_done, 1)
            pe.wait_ge(pT_ready, 6)
            for m in range(NQ):
                half, i = m // 4, m % 4
                hh = 2 * i + half
                for t in range(TT):
                    to = bank[6 + i // 2][half * HD:(half + 1) * HD, (i % 2) * T + t * P:(i % 2) * T + (t + 1) * P]
                    for j in ([0] if t == 0 else [1, 2]):
                        ins = pe.matmul(to, v2[:, max(j - 1, 0), hh * HD:(hh + 1) * HD], pT2[:, j, m, :],
                                        start=i % 2 == 0 and j == 0, stop=j != 1, skip_group_check=True)
            ins.then_inc(attn_done, 1)

            def head(b, m):
                half, i = m // 2, 2 * b + m % 2
                return 2 * i + half, i, half * HD

            pe.wait_ge(attn_ready, 4)
            for tt in range(TT):
                cols = slice(tt * P, (tt + 1) * P)
                if tt > 0:
                    pe.wait_ge(y2_ready, 2 * tt)
                    pe.wait_ge(st_ready, 4 * tt)
                for b in range(2):
                    B = bank[4 * b:4 * b + 4]
                    for m in range(4):
                        hh, i, lo = head(b, m)
                        pe.matmul(B[2 * (m // 2)][:, (m % 2) * P:(m % 2 + 1) * P], ar[lo:lo + HD, i, 0, cols], b_hat[lo:lo + HD, i, cols],
                                  start=m % 2 == 0, stop=True, skip_group_check=True)
                        ins = pe.matmul(B[2 * (m // 2) + 1][:, (m % 2) * T:(m % 2 + 1) * T].rearrange("p (w t) -> p w t", w=2),
                                        b_hat[lo:lo + HD, i, cols], ar[lo:lo + HD, i, :, cols],
                                        start=m % 2 == 0, stop=True, skip_group_check=True)
                    ins.then_inc(rec_done, 1)
                for b in range(2):
                    B = bank[4 * b:4 * b + 4]
                    pe.wait_ge(rec_ready, count(vector_steps, "Mb", tt, b))
                    for m in range(4):
                        hh, i, lo = head(b, m)
                        ins = pe.matmul(B[2 * (m // 2)][:, (m % 2) * T:(m % 2 + 1) * T].rearrange("p (w t) -> p w t", w=2),
                                        k_hat[lo:lo + HD, i, cols], ar[lo:lo + HD, i, :, cols],
                                        start=m % 2 == 0, stop=True, skip_group_check=True)
                    ins.then_inc(rec_done, 1)
                for b in range(2):
                    B, Z = bank[4 * b:4 * b + 4], batch[b]
                    pe.wait_ge(rec_ready, count(vector_steps, "MA", tt, b))
                    for m in range(4):
                        c = slice(m * P, (m + 1) * P)
                        pe.matmul(B[1][:, c], Z["MA"][:, m, 0, :], Z["Mb"][:, m, :], start=m == 0, stop=True, skip_group_check=True)
                        ins = pe.matmul(B[3][:, c], Z["Mb"][:, m, :], Z["MA"][:, m, 0, :], start=m == 0, stop=True, skip_group_check=True)
                    ins.then_inc(rec_done, 1)
                for b in range(2):
                    B, Z = bank[4 * b:4 * b + 4], batch[b]
                    pe.wait_ge(rec_ready, count(vector_steps, "NK", tt, b))
                    for m in range(4):
                        hh, i, lo = head(b, m)
                        ins = pe.matmul(B[2][:, m * HD:(m + 1) * HD], Z["NK"][:, m, 0, :], vn[:, tt, hh * HD:(hh + 1) * HD],
                                        start=m == 0, stop=True, skip_group_check=True)
                    ins.then_inc(rec_done, 1)
                for b in range(2):
                    B, Z = bank[4 * b:4 * b + 4], batch[b]
                    pe.wait_ge(rec_copied, count(scalar_steps, "P2", tt, b))
                    pe.wait_ge(one_added, 2 * tt + b + 1)
                    for m in range(4):
                        pe.matmul(B[m // 2][:, (m % 2) * T:(m % 2 + 1) * T].rearrange("p (w t) -> p w t", w=2), Z["P2"][:, m, :], Z["PU"][:, m],
                                  start=m % 2 == 0, stop=True, skip_group_check=True)
                        ins = pe.matmul(B[3][:, m * P:(m + 1) * P], Z["PU"][:, m, 0, :], Z["P2"][:, m, :],
                                        start=m == 0, stop=True, skip_group_check=True)
                    ins.then_inc(rec_done, 1)
                for b in range(2):
                    B, Z = bank[4 * b:4 * b + 4], batch[b]
                    pe.wait_ge(rec_copied, count(scalar_steps, "P4", tt, b))
                    pe.wait_ge(rec_ready, count(vector_steps, "U2", tt, b))
                    pe.wait_ge(rec_copied, count(scalar_steps, "x0", tt, b))
                    for m in range(4):
                        c = slice(m * P, (m + 1) * P)
                        pe.matmul(B[2][:, c], Z["MA"][:, m, 0, :], Z["Mb"][:, m, :], start=m == 0, stop=True, skip_group_check=True)
                        ins = pe.matmul(B[0][:, c], Z["Mb"][:, m, :], Z["PU"][:, m, 1, :], start=m == 0, stop=True, skip_group_check=True)
                    ins.then_inc(rec_done, 1)
                for b in range(2):
                    B, Z = bank[4 * b:4 * b + 4], batch[b]
                    pe.wait_ge(rec_copied, count(scalar_steps, "P8", tt, b))
                    pe.wait_ge(rec_ready, count(vector_steps, "U4", tt, b))
                    for m in range(4):
                        ins = pe.matmul(B[1][:, m * P:(m + 1) * P], Z["P2"][:, m, :], Z["PU"][:, m, 1, :],
                                        start=m == 0, stop=True, skip_group_check=True)
                    ins.then_inc(rec_done, 1)
                for b in range(2):
                    B, Z = bank[4 * b:4 * b + 4], batch[b]
                    pe.wait_ge(rec_ready, count(vector_steps, "U8", tt, b))
                    for m in range(4):
                        ins = pe.matmul(B[3][:, m * P:(m + 1) * P], Z["PU"][:, m, 1, :], x0[:, tt, head(b, m)[0], :],
                                        start=m == 0, stop=True, skip_group_check=True)
                    ins.then_inc(rec_done, 1)
                for b in range(2):
                    B, Z = bank[4 * b:4 * b + 4], batch[b]
                    pe.wait_ge(rec_copied, count(scalar_steps, "X1", tt, b))
                    for m in range(4):
                        ins = pe.matmul(B[2][:, m * P:(m + 1) * P], Z["MoT"][:, m, :], Z["X1"][:, m, :],
                                        start=m == 0, stop=True, skip_group_check=True)
                    ins.then_inc(rec_done, 1)
                for b in range(2):
                    B, Z = bank[4 * b:4 * b + 4], batch[b]
                    pe.wait_ge(rec_copied, count(scalar_steps, "X2", tt, b))
                    for m in range(4):
                        ins = pe.matmul(B[0][:, m * P:(m + 1) * P], Z["PU"][:, m, 1, :], Z["Mb"][:, m, :],
                                        start=m == 0, stop=True, skip_group_check=True)
                    ins.then_inc(rec_done, 1)
                for b in range(2):
                    B, Z = bank[4 * b:4 * b + 4], batch[b]
                    pe.wait_ge(rec_ready, count(vector_steps, "X3", tt, b))
                    for m in range(4):
                        hh, i, lo = head(b, m)
                        ins = pe.matmul(B[1][lo:lo + HD, (m % 2) * P:(m % 2 + 1) * P], Z["X1"][:, m, 0:HD], Z["MA"][:, m, 1, :],
                                        start=m % 2 == 0, stop=True, skip_group_check=True)
                    ins.then_inc(rec_done, 1)
                for b in range(2):
                    B, Z = bank[4 * b:4 * b + 4], batch[b]
                    pe.wait_ge(rec_ready, count(vector_steps, "rT", tt, b))
                    for c in range(4):
                        rows = slice(c * CH, (c + 1) * CH)
                        for m in range(4):
                            hh, i, lo = head(b, m)
                            hc = slice(hh * HD, (hh + 1) * HD)
                            o = (m % 2) * HD
                            pe.matmul(B[c][lo:lo + HD, o:o + HD], Z["X1"][rows, m, 0:HD], bn[rows, tt, hc],
                                      start=m % 2 == 0, stop=True, skip_group_check=True)
                            pe.matmul(B[c][lo:lo + HD, P + o:P + o + HD], bn[rows, tt, hc], Z["X1"][rows, m, HD:P],
                                      start=False, stop=False, skip_group_check=True)
                            ins = pe.matmul(B[c][lo:lo + HD, P + o:P + o + HD], kn[rows, tt, hc], vn[rows, tt, hc],
                                            start=False, stop=True, skip_group_check=True)
                    ins.then_inc(rec_done, 1)
                pe.wait_ge(rec_ready, count(vector_steps, "FH", tt, 1))
                for b in range(2):
                    Z = batch[b]
                    for m in range(4):
                        hh, i, lo = head(b, m)
                        y_to = bank[2 + 4 * (m // 2)][:, i * HD:(i + 1) * HD]
                        pe.matmul(y_to, Z["MA"][:, m, 1, :], Z["X1"][:, m, HD:P], start=b == 0 and m % 2 == 0, stop=False, skip_group_check=True)
                        pe.matmul(y_to, Z["NK"][:, m, 1, :], vn[:, tt, hh * HD:(hh + 1) * HD], start=False, stop=False, skip_group_check=True)
                for c in range(4):
                    rows = slice(c * CH, (c + 1) * CH)
                    number = 4 * tt + c
                    if number == 0:
                        continue
                    pe.wait_ge(st_ready, number)
                    for i in range(NP2):
                        for half in range(2):
                            lo = half * HD
                            ins = pe.matmul(bank[2 + 4 * half][rows, i * HD:(i + 1) * HD], rT[lo:lo + HD, i, rows], state[lo:lo + HD, i, :],
                                            start=False, stop=True, skip_group_check=True)
                    if c == 3:
                        ins.then_inc(y2_done, 1)
                    if number < 2 * 4 - 1:
                        for i in range(NP2):
                            for half in range(2):
                                lo = half * HD
                                ins = pe.matmul(bank[0][lo:lo + HD, i * HD:(i + 1) * HD], ft[lo:lo + HD, c, i, :], state[lo:lo + HD, i, :],
                                                start=i == 0, stop=True, skip_group_check=True)
                        ins.then_inc(st_done, 1)
            pe.wait_ge(ya_ready, 1)
            for i in range(NP2):
                for t in range(TT):
                    ins = pe.transpose(bank[i // 2][:, (i % 2) * T + t * P:(i % 2) * T + (t + 1) * P], y2[:, t, i * P:(i + 1) * P], ident)
            ins.then_inc(sguT_done, 1)
            for n2 in range(2):
                for br, (yT, f) in enumerate(((yaT, "branch_a"), (ybT, "branch_b"))):
                    if n2 == 0 and br == 0:
                        pe.wait_ge(y2_ready, 4)
                    if n2 == 1:
                        pe.wait_ge(mm_ready, 1)
                    project(("gate_a", "gate_b")[br] + str(n2), 2 if br == 0 else 0)
                    if n2 == 0 and br == 0:
                        pe.wait_ge(sguT_ready, 4)
                    pe.wait_ge(w2_in[BUFFER[FILLS.index(f)]], fill_count(f))
                    for t in range(TT):
                        for k in range(NP2):
                            ins = pe.matmul(bank[(6 if br == 0 else 2) + t][:, :], yT[:, k, t * P:(t + 1) * P],
                                            by_k(f, NP2)[:, k, n2 * BANK:(n2 + 1) * BANK], start=k == 0, stop=k == NP2 - 1)
                    ins.then_inc(w2_used, 1)
            pe.wait_ge(mm_ready, 2)
            for t in range(TT):
                for k in range(KD):
                    ins = pe.transpose(bank[4 + 2 * t + k // 4][:, (k % 4) * P:(k % 4 + 1) * P], mm[:, t, k * P:(k + 1) * P], ident)
                ins.then_inc(hT_done, 1)
            pe.wait_ge(hT_ready, 12)
            pe.wait_ge(w2_in[BUFFER[FILLS.index("out0")]], fill_count("out0"))
            pe.wait_ge(w2_in[BUFFER[FILLS.index("out1")]], fill_count("out1"))
            for t in range(TT):
                for n2 in range(2):
                    for k in range(KD):
                        ins = pe.matmul(bank[2 * t + n2][:, :], mT[:, k, t * P:(t + 1) * P],
                                        by_k("out0" if k < 4 else "out1", 4)[:, k % 4, n2 * BANK:(n2 + 1) * BANK], start=k == 0, stop=k == KD - 1)
                    ins.then_inc(u_done, 1)
            transpose_hn(hn2, TT)
            pe.wait_ge(hT_ready, 16)
            for t in range(TT):
                for n2 in range(2):
                    pe.matmul(bank[2 * t + n2][:, :], ident, x1[:, t, n2 * BANK:(n2 + 1) * BANK], start=True, stop=False, skip_group_check=True)

            def ffn_up(i, use):
                pe.wait_ge(ffu_in[i], use * 16)
                for c in range(2):
                    for k in range(KD):
                        ins = pe.matmul(bank[4 + i][:, c * T:(c + 1) * T], ffu[i][:, c, k, :], hnT[:, k, :],
                                        start=k == 0, stop=k == KD - 1, skip_group_check=True)
                ins.then_inc(ffu_used[i], 1)

            def ffn_down(i, use, last=False):
                pe.wait_ge(ffd_in[i], use * 16)
                pe.wait_ge(hid2_ready[i], use)
                for t in range(TT):
                    for n2 in range(2):
                        ins = pe.matmul(bank[2 * t + n2][:, :], hid2[:, i, t * P:(t + 1) * P], ffd[i][:, n2 * BANK:(n2 + 1) * BANK],
                                        start=False, stop=last, skip_group_check=True)
                ins.then_inc(ffn_done if last else ffd_used[i], 1)

            ffn_up(0, 1)
            with pe.Fori(0, FT_N // 2 - 1) as it:
                now, ahead = pe.snap(it + 1), pe.snap(it + 2)
                ffn_up(1, now)
                ffn_down(0, now)
                ffn_up(0, ahead)
                ffn_down(1, now)
            ffn_up(1, FT_N // 2)
            ffn_down(0, FT_N // 2)
            ffn_down(1, FT_N // 2, last=True)

        @block.scalar
        def _(act):
            act.dma_start(w_router, A["w_router"]).then_inc(router_in, 16)
            act.wait_ge(consts_in, 32)
            act.wait_ge(proj_done, 1)
            for i in range(4):
                act.activation(qkT[:, i, :], bank[i // 2][:, (i % 2) * T:(i % 2 + 1) * T], ACT.Identity,
                               bias=colv("b_in_qk")[:, i:i + 1]).then_inc(qk_ready, 1)
            for i, a in enumerate((g_nat, u_nat)):
                act.wait_ge(ug_biased, 2 * (2 - i))
                act.activation(a, a, ACT.Gelu_apprx_tanh).then_inc(ug_gelu, 1)
            act.wait_ge(g_var, 1)
            act.activation(g_std, g_sum2, ACT.Sqrt, bias=eps1, scale=1.0 / GD).then_inc(g_stds, 1)
            act.wait_ge(neg_max, 1)
            for t, pr in enumerate((prob1, prob0)):
                act.wait_ge(neg_max, t + 1)
                for hh in range(NQ):
                    act.activation(pr[:, hh, :], pr[:, hh, :], ACT.Exp, bias=nmax[:, t * NQ + hh:t * NQ + hh + 1],
                                   accum_out=den[:, t * NQ + hh:t * NQ + hh + 1]).then_inc(exp_done, 1)
                act.activation(sink_e[:, t * NQ:(t + 1) * NQ], sink_e[:, t * NQ:(t + 1) * NQ], ACT.Exp).then_inc(exp_done, 1)
            t_bank = [[3, 4], [0, 1], [2, 7]]
            for j in range(3):
                act.wait_ge(pT_done, j + 1)
                for b in range(2):
                    ins = act.copy(pT[:, j, 4 * b:4 * b + 4, :], bank[t_bank[j][b]][:, :].rearrange("p (h t) -> p h t", h=4))
                ins.then_inc(pT_ready, 1)
            act.wait_ge(attn_done, 1)
            for b in range(2):
                act.copy(mixT[:, 2 * b:2 * b + 2, :], bank[3 + b][:, :].rearrange("p (k t) -> p k t", k=2)).then_inc(attn_ready, 1)
            for t in range(TT):
                act.wait_ge(var_ready, t + 1)
                act.activation(rstd[:, t:t + 1], mv[:, t, 1:2], ACT.Sqrt, bias=eps1).then_inc(std_ready, 1)
            for t in range(TT):
                act.wait_ge(hT_done, t + 1)
                for b in range(2):
                    act.copy(hT[:, 4 * b:4 * b + 4, t * P:(t + 1) * P],
                             bank[3 + 2 * t + b][:, :].rearrange("p (k t) -> p k t", k=4)).then_inc(hT_ready, 1)
            act.copy(h_part[:, 0], h).then_inc(split_ready, 1)
            act.wait_ge(top_ready, 2)
            for t in range(TT):
                act.activation(gates4[:, t, :], gates4[:, t, :], ACT.Exp, bias=ntop[:, t:t + 1],
                               accum_out=gsum[:, t:t + 1]).then_inc(top_exp, 1)
            act.wait_ge(gateT_done, 1)
            act.copy(gateT, bank[5][0:NE, 0:T]).then_inc(gateT_ready, 1)
            act.wait_ge(rest_ready, 1)
            act.copy(h_part[:, 1], resid).then_inc(split_ready, 1)
            act.wait_ge(gather_done, 1)
            act.copy(x_e, bank[6][:, :].rearrange("p (k s) -> p k s", k=KD)).then_inc(x_e_ready, 1)
            act.wait_ge(iter_ready, 1)
            n = act.value_load(n_iter[0:1, 0:1], min_val=NE, max_val=NE * PASSES)
            with act.Fori(0, n) as it:
                now, ahead = act.snap(it + 1), act.snap(it + 2)
                act.wait_ge(gt_ready, now)
                act.activation(sg, gt, ACT.Sigmoid, scale=SWIGLU_ALPHA).then_inc(sg_ready, 1)
                act.wait_ge(gather_done, ahead)
                act.copy(x_e, bank[6][:, :].rearrange("p (k s) -> p k s", k=KD)).then_inc(x_e_ready, 1)
                act.wait_ge(hidT_done, now)
                act.copy(hidT, bank[4][:, :].rearrange("p (j c) -> p j c", j=4)).then_inc(hidT_ready, 1)
                act.wait_ge(slots_used, act.snap(it * SLOTS + SLOTS))
                act.copy(yy, bank[7][:, :]).then_inc(y_ready, 1)
            for t in range(TT):
                act.wait_ge(var_ready, TT + t + 1)
                act.activation(rstd[:, t:t + 1], mv[:, t, 1:2], ACT.Sqrt, bias=eps1).then_inc(std_ready, 1)

            def root_mean_square(src, ready, base, scratch):
                act.wait_ge(ready, TT)
                for t in range(TT):
                    act.activation(scratch[:, t, :], src[:, t, :], ACT.Square, accum_out=ss[:, t:t + 1]).then_inc(sq_done, 1)
                act.wait_ge(sq_done, base + 2)
                act.activation(rms, ss, ACT.Sqrt, bias=eps2, scale=1.0 / D).then_inc(rms_std, 1)

            root_mean_square(x1, x1_ready, 0, hn)
            act.wait_ge(w2_used, use_count("lora"))
            act.copy(lora[:, 0:2, :], bank[6][:, :].rearrange("p (i t) -> p i t", i=2)).then_inc(z_raw, 1)
            act.copy(lora[0:CH, 2, :], bank[7][0:CH, 0:T]).then_inc(z_raw, 1)
            act.wait_ge(lora_mixed, 1)
            act.activation(lora[0:HD, 0, :], lora[0:HD, 0, :], ACT.Tanh).then_inc(lora_ready, 1)
            act.activation(lora[:, 1, :], lora[:, 1, :], ACT.Sigmoid).then_inc(lora_ready, 1)
            act.activation(lora[0:CH, 2, :], lora[0:CH, 2, :], ACT.Sigmoid).then_inc(lora_ready, 1)
            for n2, (f, z) in enumerate((("r", zr), ("k", zk), ("v", zv))):
                act.wait_ge(w2_used, use_count(f))
                for b in range(2):
                    act.copy(z[:, 2 * b:2 * b + 2, :], bank[2 * n2 + b][:, :].rearrange("p (i t) -> p i t", i=2)).then_inc(z_raw, 1)
            act.wait_ge(lora_up_done, 1)
            for i in range(NP2):
                act.activation(sd[:, i, :], bank[6 + i // 2][:, (i % 2) * T:(i % 2 + 1) * T], ACT.Sigmoid,
                               bias=col2("decay_bias_2")[:, i:i + 1]).then_inc(sd_ready, 1)
            act.wait_ge(lora_up_done, 2)
            for i in range(NP2):
                act.activation(aa[:, i, :], bank[i // 2][:, (i % 2) * T:(i % 2 + 1) * T], ACT.Sigmoid,
                               bias=col2("aaa_bias_2")[:, i:i + 1]).then_inc(aa_ready, 1)
            act.wait_ge(lora_up_done, 3)
            for t in range(TT):
                act.copy(g_gate[:, t, :], bank[2 + t][:, :]).then_inc(g_ready, 1)
            act.wait_ge(cs_ready, 1)
            act.activation(e_pos, cs, ACT.Exp, scale=-KAPPA).then_inc(exp3_ready, 1)
            act.activation(e_neg, cs, ACT.Exp, scale=KAPPA).then_inc(exp3_ready, 1)
            act.activation(e_before, sd, ACT.Exp, scale=-KAPPA).then_inc(exp3_ready, 1)
            act.wait_ge(nrm_done, 1)
            for b in range(2):
                act.activation(nrm[:, 2 * b:2 * b + 2, :], bank[6 + b][:, :].rearrange("p (i t) -> p i t", i=2), ACT.Sqrt).then_inc(nrm_ready, 1)
            for w, (f, pair) in enumerate((("q2", 2), ("k2", 0))):
                act.wait_ge(w2_used, use_count(f))
                for t in range(TT):
                    act.copy(qk2[:, w, t, :], bank[2 * pair + t][:, :]).then_inc(qkv2_raw, 1)
            act.wait_ge(w2_used, use_count("v2"))
            for t in range(TT):
                act.copy(v2[:, t, :], bank[2 + t][:, :]).then_inc(qkv2_raw, 1)
            for n2, to in enumerate((bn, kn)):
                for t in range(TT):
                    act.wait_ge(nat_done, 2 * n2 + t + 1)
                    act.copy(to[:, t, :], bank[2 * (n2 + 1) + t][:, :]).then_inc(nat_ready, 1)
            act.wait_ge(ang_ready, 1)
            act.activation(sinv, ang, ACT.Sin).then_inc(trig_ready, 1)
            act.activation(cosv, ang_n, ACT.Sin).then_inc(trig_ready, 1)
            act.wait_ge(ss_ready, 1)
            act.activation(rs_qk, ss_qk, ACT.Sqrt, bias=eps2, scale=1.0 / HD).then_inc(rs_ready, 1)
            act.wait_ge(qkT2_done, 1)
            for w in range(2):
                for b in range(2):
                    act.copy(qkT2[:, w, 2 * b:2 * b + 2, :], bank[2 * w + b][:, :].rearrange("p (i t) -> p i t", i=2)).then_inc(qkT2_ready, 1)
            for t, pr in enumerate((prob2_1, prob2_0)):
                act.wait_ge(neg_max, 2 + t + 1)
                for m in range(NQ):
                    o = t * NQ + m
                    act.activation(pr[:, m, :], pr[:, m, :], ACT.Exp, bias=nmax2[:, o:o + 1], accum_out=den2[:, o:o + 1]).then_inc(exp_done, 1)
            for j in range(3):
                act.wait_ge(pT_done, 3 + j + 1)
                for b in range(2):
                    ins = act.copy(pT2[:, j, 4 * b:4 * b + 4, :], bank[2 * j + b][:, :].rearrange("p (h t) -> p h t", h=4))
                ins.then_inc(pT_ready, 1)
            act.wait_ge(attn_done, 2)
            for b in range(2):
                act.copy(ybT[:, 2 * b:2 * b + 2, :], bank[6 + b][:, :].rearrange("p (i t) -> p i t", i=2)).then_inc(attn_ready, 1)
            four = lambda a: a[:, :].rearrange("p (m t) -> p m t", m=4)
            for tt in range(TT):
                for b in range(2):
                    B, Z = bank[4 * b:4 * b + 4], batch[b]
                    act.wait_ge(rec_done, count(tensor_steps, "p2", tt, b))
                    act.copy(Z["P2"], four(B[1]))
                    act.copy(Z["PU"][:, :, 0, :], four(B[3])).then_inc(rec_copied, 1)
                for b in range(2):
                    B = bank[4 * b:4 * b + 4]
                    act.wait_ge(rec_done, count(tensor_steps, "nv", tt, b))
                    for half in range(2):
                        ins = act.copy(x0[:, tt, 4 * b + half:4 * b + half + 3:2, HD:P],
                                       B[2][:, half * P:(half + 1) * P].rearrange("p (m v) -> p m v", m=2))
                    ins.then_inc(rec_copied, 1)
                for b in range(2):
                    B, Z = bank[4 * b:4 * b + 4], batch[b]
                    act.wait_ge(rec_done, count(tensor_steps, "p4", tt, b))
                    act.copy(Z["Mb"], four(B[3])).then_inc(rec_copied, 1)
                for b in range(2):
                    B, Z = bank[4 * b:4 * b + 4], batch[b]
                    act.wait_ge(rec_done, count(tensor_steps, "p8", tt, b))
                    act.copy(Z["P2"], four(B[2])).then_inc(rec_copied, 1)
                for b in range(2):
                    B, Z = bank[4 * b:4 * b + 4], batch[b]
                    act.wait_ge(rec_done, count(tensor_steps, "x1", tt, b))
                    act.copy(Z["X1"], four(B[3])).then_inc(rec_copied, 1)
                for b in range(2):
                    B, Z = bank[4 * b:4 * b + 4], batch[b]
                    act.wait_ge(rec_done, count(tensor_steps, "x2", tt, b))
                    act.copy(Z["Mb"], four(B[2])).then_inc(rec_copied, 1)
                act.wait_ge(y2_done, tt + 1)
                for half in range(2):
                    act.copy(y2[:, tt, :].rearrange("p (i h v) -> p i h v", i=NP2, h=2)[:, :, half, :],
                             bank[2 + 4 * half][:, 0:T].rearrange("p (i v) -> p i v", i=NP2)).then_inc(y2_ready, 1)
            act.wait_ge(g_var, 2)
            act.activation(y_std, y_sum2, ACT.Sqrt, bias=eps3, scale=1.0 / HD).then_inc(g_stds, 1)
            act.wait_ge(sguT_done, 2)
            for b in range(2):
                act.copy(yaT[:, 2 * b:2 * b + 2, :], bank[b][:, :].rearrange("p (i t) -> p i t", i=2)).then_inc(sguT_ready, 1)
            for n2 in range(2):
                for br, to in enumerate((sga, sgb)):
                    f = ("gate_a", "gate_b")[br] + str(n2)
                    act.wait_ge(w2_used, use_count(f))
                    if n2 == 1:
                        act.wait_ge(mm_ready, 1)
                    for t in range(TT):
                        act.activation(to[:, t, :], bank[(4 if br == 0 else 0) + t][:, :], ACT.Sigmoid).then_inc(sg_a, 1)
            for t in range(TT):
                act.wait_ge(hT_done, 4 + t + 1)
                for b in range(2):
                    act.copy(mT[:, 4 * b:4 * b + 4, t * P:(t + 1) * P], bank[4 + 2 * t + b][:, :].rearrange("p (k t) -> p k t", k=4)).then_inc(hT_ready, 1)
            root_mean_square(x1, x2_ready, 2, hn2)
            with act.Fori(0, FT_N // 2) as it:
                for i in range(2):
                    act.wait_ge(conv_ready[i], it + 1)
                    act.activation(conv[:, i, :], conv[:, i, :], ACT.Gelu).then_inc(gelu_ready[i], 1)
            act.wait_ge(ffn_done, 1)
            for n2 in range(2):
                act.copy(out_sb[:, 0, n2 * BANK:(n2 + 1) * BANK], bank[n2][:, :]).then_inc(out_ready[0], 1)

        @block.vector
        def _(dve):
            step = [0]

            def link(ins):
                step[0] += 1
                ins.then_inc(dve_step, 1)
                dve.wait_ge(dve_step, step[0])

            def wide(a, n):
                return a.unsqueeze(len(a.shape)).broadcast_to(list(a.shape) + [n])

            link(dve.memset(eps1, LN_EPS))
            link(dve.memset(eps2, NORM_EPS))
            link(dve.memset(eps3, GN_EPS))
            dve.wait_ge(consts_in, 32)
            dve.wait_ge(wsT_in, 16)
            dve.tensor_tensor(wsT, wsT, const("upto").unsqueeze(1).broadcast_to([P, NG, P]), ALU.mult).then_inc(wsT_masked, 1)
            dve.wait_ge(mix_rows_in, 16)
            b_vug = rowv("b_in_vug")
            dve.wait_ge(proj_done, 3)
            dve.tensor_scalar(qkT[:, 4, :], bank[2][:, 0:T], colv("b_in_qk")[:, 4:5], None, ALU.add).then_inc(qk_ready, 1)
            for t in range(TT):
                dve.tensor_tensor(v_nat[:, t, :], bank[2][:, T + t * P:T + (t + 1) * P], b_vug[:, 0:P], ALU.add).then_inc(v_ready, 1)
            for c, a in enumerate((u_nat, g_nat)):
                for t in range(TT):
                    dve.wait_ge(proj_done, 4 + 2 * c + t)
                    dve.tensor_tensor(a[:, t, :], bank[3 + 2 * c + t][:, :], b_vug[:, P + c * G1:P + (c + 1) * G1],
                                      ALU.add).then_inc(ug_biased, 1)
            def masked(to, frm, masks):
                link(dve.scalar_tensor_tensor(out=to, in0=frm, scalar=HD ** -0.5, in1=masks, op0=ALU.mult, op1=ALU.add))

            def soft_max(t, pr):
                o = t * NQ
                link(dve.tensor_reduce(nmax[:, o:o + NQ], pr, AX.X, ALU.max))
                link(dve.tensor_tensor(nmax[:, o:o + NQ], nmax[:, o:o + NQ], rowv("sinks"), ALU.max))
                link(dve.tensor_tensor(sink_e[:, o:o + NQ], rowv("sinks"), nmax[:, o:o + NQ], ALU.subtract))
                dve.tensor_scalar(nmax[:, o:o + NQ], nmax[:, o:o + NQ], -1.0, None, ALU.mult).then_inc(neg_max, 1)

            dve.wait_ge(scores_done, 1)
            for b, nb in enumerate((0, 1, 2, 7)):
                for q in range(2):
                    o = q * T
                    hh = 2 * b + q
                    masked(prob1[:, hh, 0:P], bank[nb][:, o:o + P], const("before"))
                    masked(prob1[:, hh, P:T], bank[nb][:, o + P:o + T], const("causal"))
            soft_max(0, prob1)
            g3 = g_nat.rearrange("p t (g d) -> p (t g) d", d=GD)
            sq3 = sq.rearrange("p t (g d) -> p (t g) d", d=GD)
            dve.wait_ge(ug_gelu, 1)
            link(dve.tensor_reduce(g_sum, g3, AX.X, ALU.add))
            link(dve.tensor_scalar(g_sum, g_sum, 1.0 / GD, None, ALU.mult))
            link(dve.tensor_tensor(g3, g3, wide(g_sum, GD), ALU.subtract))
            link(dve.tensor_tensor(sq3, g3, g3, ALU.mult))
            dve.tensor_reduce(g_sum2, sq3, AX.X, ALU.add).then_inc(g_var, 1)
            dve.wait_ge(scores_done, 2)
            for half in range(2):
                masked(prob0[:, 4 * half:4 * half + 4, :], bank[3 + half][:, :].rearrange("p (h s) -> p h s", h=4),
                       const("causal").unsqueeze(1).broadcast_to([P, 4, P]))
            soft_max(1, prob0)
            dve.wait_ge(g_stds, 1)
            link(dve.reciprocal(g_sum2, g_std))
            link(dve.tensor_tensor(g3, g3, wide(g_sum2, GD), ALU.mult))
            link(dve.tensor_tensor(g_nat, g_nat, rowv("ln_v_g").unsqueeze(1).broadcast_to([P, TT, G1]), ALU.mult))
            dve.tensor_tensor(g_nat, g_nat, rowv("ln_v_b").unsqueeze(1).broadcast_to([P, TT, G1]), ALU.add).then_inc(g_normed, 1)
            for t, pr in enumerate((prob1, prob0)):
                o = t * NQ
                dve.wait_ge(exp_done, (t + 1) * (NQ + 1))
                link(dve.tensor_tensor(den[:, o:o + NQ], den[:, o:o + NQ], sink_e[:, o:o + NQ], ALU.add))
                link(dve.reciprocal(den[:, o:o + NQ], den[:, o:o + NQ]))
                dve.tensor_tensor(pr, pr, wide(den[:, o:o + NQ], pr.shape[2]), ALU.mult).then_inc(prob_ready, 1)
            dve.wait_ge(mixed_done, 1)
            dve.wait_ge(ug_gelu, 2)
            for b in range(2):
                m4 = bank[5 + b][:, :].rearrange("p (g c d) -> p c g d", g=4, c=TT)
                s4 = sq[:, :, b * T:(b + 1) * T].rearrange("p c (g d) -> p c g d", g=4)
                for c in range(TT):
                    link(dve.tensor_tensor(s4[:, c], m4[:, c], wide(colv("b_s")[:, 4 * b:4 * b + 4], GD), ALU.add))
            dve.tensor_tensor(u_nat, u_nat, sq, ALU.mult).then_inc(sgu_ready, 1)
            dve.wait_ge(sguT_done, 1)
            for b in range(2):
                dve.tensor_copy(mixT[:, 4 + 2 * b:6 + 2 * b, :], bank[5 + b][:, :].rearrange("p (k t) -> p k t", k=2)).then_inc(sguT_ready, 1)

            def layer_norm(t, src, frm_banks, add_row, g, b, done, before, to):
                for n in range(2):
                    cols = slice(n * BANK, (n + 1) * BANK)
                    if add_row is not None:
                        dve.wait_ge(mix_done, 2 * t + n + 1)
                        link(dve.tensor_tensor(ln_tmp[:, cols], frm_banks[n][:, :], add_row[:, cols], ALU.add))
                        link(dve.scalar_tensor_tensor(out=resid[:, t, cols], in0=src[:, t, cols], scalar=ALPHA1, in1=ln_tmp[:, cols],
                                                      op0=ALU.mult, op1=ALU.add))
                    else:
                        link(dve.scalar_tensor_tensor(out=resid[:, t, cols], in0=src[:, t, cols], scalar=ALPHA1, in1=frm_banks[n][:, :],
                                                      op0=ALU.mult, op1=ALU.add))
                    link(dve.bn_stats(stats[:, n, :], resid[:, t, cols]))
                dve.bn_aggr(mv[:, t, :], stats.rearrange("p n s -> p (n s)")).then_inc(var_ready, 1)
                dve.wait_ge(std_ready, before + t + 1)
                link(dve.reciprocal(rstd[:, t:t + 1], rstd[:, t:t + 1]))
                link(dve.tensor_scalar(resid[:, t, :], resid[:, t, :], mv[:, t, 0:1], rstd[:, t:t + 1], ALU.subtract, ALU.mult))
                link(dve.tensor_tensor(resid[:, t, :], resid[:, t, :], g, ALU.mult))
                dve.tensor_tensor(to[:, t, :], resid[:, t, :], b, ALU.add).then_inc(done, 1)

            dve.wait_ge(x_in, 16)
            dve.wait_ge(ln_rows_in, 16)
            mix_bank = [[0, 1], [2, 7]]
            for t in range(TT):
                layer_norm(t, x_nat, [bank[i] for i in mix_bank[t]], rowv("b_out"), rowv("ln1_g"), rowv("ln1_b"), h_ready,
                           0, h)
            dve.wait_ge(split_ready, 1)
            dve.tensor_tensor(resid, h, h_part[:, 0], ALU.subtract).then_inc(rest_ready, 1)
            dve.wait_ge(logits_done, 1)
            for t in range(TT):
                link(dve.tensor_tensor(logits[:, t, :], bank[7][:, t * NE:(t + 1) * NE], rowv("b_router"), ALU.add))
                link(dve.max(top8[:, t, :], logits[:, t, :]))
                link(dve.max_index(top_i[:, t, :], top8[:, t, :], logits[:, t, :]))
                link(dve.tensor_copy(gates4[:, t, :], top8[:, t, 0:TOPK]))
                dve.tensor_scalar(ntop[:, t:t + 1], top8[:, t, 0:1], -1.0, None, ALU.mult).then_inc(top_ready, 1)
            link(dve.tensor_copy(top_f, top_i[:, :, 0:TOPK]))
            for t in range(TT):
                link(dve.tensor_tensor(chosen4[:, t], const("iota32").unsqueeze(1).broadcast_to([P, TOPK, NE]), wide(top_f[:, t, :], NE), ALU.is_equal))
                ins = dve.tensor_reduce(chosen[:, t, :], chosen4[:, t].rearrange("p k e -> p e k"), AX.X, ALU.add)
                if t == 0:
                    link(ins)
            ins.then_inc(chosen_ready, 1)
            dve.wait_ge(top_exp, 2)
            link(dve.reciprocal(gsum, gsum))
            for t in range(TT):
                link(dve.tensor_scalar(gates4[:, t, :], gates4[:, t, :], gsum[:, t:t + 1], None, ALU.mult))
                link(dve.tensor_tensor(chosen4[:, t], chosen4[:, t], wide(gates4[:, t, :], NE), ALU.mult))
                link(dve.memset(gate_of[:, t, NE * PASSES:COLS], 0.0))
                link(dve.memset(posm[:, t, NE * PASSES:COLS], -1.0))
                for b in range(PASSES):
                    ins = dve.tensor_reduce(gate_of[:, t, b * NE:(b + 1) * NE], chosen4[:, t].rearrange("p k e -> p e k"), AX.X, ALU.add)
                    if (t, b) != (TT - 1, PASSES - 1):
                        link(ins)
            ins.then_inc(chosen_ready, 1)
            dve.wait_ge(place_done, 1)
            for t in range(TT):
                link(dve.tensor_tensor(posm[:, t, 0:NE], bank[3][:, t * NE:(t + 1) * NE], chosen[:, t, :], ALU.mult))
                link(dve.tensor_scalar(posm[:, t, 0:NE], posm[:, t, 0:NE], -1.0, None, ALU.add))
                for b in range(1, PASSES):
                    link(dve.tensor_scalar(posm[:, t, b * NE:(b + 1) * NE], posm[:, t, 0:NE], float(-b * CAP), None, ALU.add))
            dve.wait_ge(place_done, 2)
            link(dve.tensor_reduce(n_iter_f[0:1, 0:1], bank[4][0:1, 0:NE], AX.X, ALU.max))
            link(dve.memset(n_iter_f[0:1, 1:2], float(NE)))
            for b in range(1, PASSES):
                link(dve.tensor_scalar(n_iter_f[0:1, 2:3], n_iter_f[0:1, 0:1], float(b * CAP), float(NE), ALU.is_gt, ALU.mult))
                link(dve.tensor_tensor(n_iter_f[0:1, 1:2], n_iter_f[0:1, 1:2], n_iter_f[0:1, 2:3], ALU.add))
            link(dve.tensor_scalar(n_iter_f[0:1, 2:3], n_iter_f[0:1, 1:2], -1.0, None, ALU.add))
            dve.tensor_copy(n_iter[0:1, 0:2], n_iter_f[0:1, 1:3]).then_inc(iter_ready, 1)
            dve.wait_ge(split_ready, 2)
            dve.tensor_tensor(h_part[:, 2], resid, h_part[:, 1], ALU.subtract).then_inc(split_ready, 1)

            def build_place(col):
                for t in range(TT):
                    ins = dve.tensor_scalar(place[:, t, :], const("iota2")[:, 0:CAP], posm[:, t, bass.ds(col, 1)], None, ALU.is_equal)
                ins.then_inc(place_ready, 1)

            def build_place_g(col):
                for t in range(TT):
                    ins = dve.tensor_scalar(place_g[:, t, :], const("iota2"), posm[:, t, bass.ds(col, 1)],
                                            gate_of[:, t, bass.ds(col, 1)], ALU.is_equal, ALU.mult)
                ins.then_inc(place_g_ready, 1)

            dve.memset(place_T, 0.0).then_inc(place_T_ready, 1)
            dve.memset(yy, 0.0).then_inc(y_ready, 1)
            build_place(0)
            build_place_g(0)
            dve.wait_ge(gather_done, 1)
            build_place(1)
            n = dve.value_load(n_iter[0:1, 0:1], min_val=NE, max_val=NE * PASSES)
            with dve.Fori(0, n) as it:
                now = dve.snap(it + 1)
                dve.wait_ge(slots_used, dve.snap(it * SLOTS + 8))
                dve.tensor_scalar(gt, bank[4][:, :], LIMIT, None, ALU.min).then_inc(gt_ready, 1)
                dve.tensor_scalar(uc, bank[5][:, :], LIMIT, -LIMIT, ALU.min, ALU.max).then_inc(uc_ready, 1)
                dve.wait_ge(uc_ready, now)
                dve.wait_ge(gt_ready, now)
                dve.scalar_tensor_tensor(out=vv, in0=uc, scalar=1.0, in1=gt, op0=ALU.add, op1=ALU.mult).then_inc(vv_ready, 1)
                dve.wait_ge(sg_ready, now)
                dve.wait_ge(vv_ready, now)
                dve.tensor_tensor(hid, vv, sg, ALU.mult).then_inc(hid_ready, 1)
                dve.wait_ge(place_T_done, now)
                dve.tensor_copy(place_T, bank[5][:, 0:T]).then_inc(place_T_ready, 1)
                build_place(it + 2)
                build_place_g(it + 1)
            dve.wait_ge(acc_done, 1)
            for t in range(TT):
                layer_norm(t, h, [bank[2 * t], bank[2 * t + 1]], None, rowv("ln2_g"), rowv("ln2_b"), x1_ready,
                           TT, resid)

            def rms_norm(to, base):
                dve.wait_ge(rms_std, base)
                link(dve.reciprocal(rms, rms))
                for t in range(TT):
                    dve.tensor_scalar(to[:, t, :], x1[:, t, :], rms[:, t:t + 1], None, ALU.mult).then_inc(hn_ready, 1)

            def scaled_T(base, g):
                for t in range(TT):
                    dve.wait_ge(hT_done, base + t + 1)
                    for b in range(2):
                        dve.tensor_tensor(hnT[:, 4 * b:4 * b + 4, t * P:(t + 1) * P],
                                          bank[4 + 2 * t + b][:, :].rearrange("p (k t) -> p k t", k=4),
                                          wide(col2(g)[:, 4 * b:4 * b + 4], P), ALU.mult).then_inc(hT_ready, 1)

            rms_norm(hn, 1)
            dve.wait_ge(small2_in, 96)
            scaled_T(2, "norm1_g_2")

            def mix_before(z, mu, n):
                link(dve.tensor_tensor(tmp[:, 0:n, 1:T], z[:, :, 0:T - 1], z[:, :, 1:T], ALU.subtract))
                link(dve.tensor_scalar(tmp[:, 0:n, 0:1], z[:, :, 0:1], -1.0, None, ALU.mult))
                for i in range(n):
                    ins = dve.scalar_tensor_tensor(out=z[:, i, :], in0=tmp[:, i, :], scalar=mu[:, i:i + 1], in1=z[:, i, :],
                                                   op0=ALU.mult, op1=ALU.add)
                    if i < n - 1:
                        link(ins)
                return ins

            link(dve.tensor_copy(pos_f, pos_i))
            link(dve.tensor_tensor(ang, const2("inv_freq").unsqueeze(1).broadcast_to([P, TT, ROT]), wide(pos_f, ROT), ALU.mult))
            link(dve.tensor_scalar(ang_n, ang, float(1 / (2 * np.pi)), 1.5 * 2.0 ** 23, ALU.mult, ALU.add))
            link(dve.tensor_scalar(ang_n, ang_n, -1.5 * 2.0 ** 23, None, ALU.add))
            link(dve.scalar_tensor_tensor(out=ang, in0=ang_n, scalar=-6.28125, in1=ang, op0=ALU.mult, op1=ALU.add))
            link(dve.scalar_tensor_tensor(out=ang, in0=ang_n, scalar=float(6.28125 - 2 * np.pi), in1=ang, op0=ALU.mult, op1=ALU.add))
            link(dve.tensor_scalar(ang, ang, 3.1415925, -3.1415925, ALU.min, ALU.max))
            link(dve.scalar_tensor_tensor(out=ang_n, in0=ang, scalar=-1.0, in1=ang, op0=ALU.mult, op1=ALU.max))
            dve.tensor_scalar(ang_n, ang_n, -1.0, float(np.pi / 2), ALU.mult, ALU.add).then_inc(ang_ready, 1)
            dve.wait_ge(z_raw, 2)
            link(mix_before(lora[:, 0:2, :], col2("mu_lora"), 2))
            link(dve.tensor_tensor(tmp[0:CH, 0, 1:T], lora[0:CH, 2, 0:T - 1], lora[0:CH, 2, 1:T], ALU.subtract))
            link(dve.tensor_scalar(tmp[0:CH, 0, 0:1], lora[0:CH, 2, 0:1], -1.0, None, ALU.mult))
            dve.scalar_tensor_tensor(out=lora[0:CH, 2, :], in0=tmp[0:CH, 0, :], scalar=col2("mu_lora")[0:CH, 2:3], in1=lora[0:CH, 2, :],
                                     op0=ALU.mult, op1=ALU.add).then_inc(lora_mixed, 1)
            dve.wait_ge(z_raw, 4)
            link(mix_before(zr, col2("mu_r"), NP2))
            dve.wait_ge(z_raw, 6)
            link(mix_before(zk, col2("mu_k"), NP2))
            link(dve.tensor_tensor(kk, zk, wide(col2("rwkv_k_k_2"), T), ALU.mult))
            dve.tensor_tensor(kk2, kk, kk, ALU.mult).then_inc(kk2_ready, 1)
            dve.wait_ge(z_raw, 8)
            mix_before(zv, col2("mu_v"), NP2).then_inc(zv_ready, 1)
            dve.wait_ge(zv_ready, 1)
            dve.wait_ge(sd_ready, 4)
            for i in range(NP2):
                link(dve.tensor_tensor_scan(cs[:, i, :], const2("chunk_start"), sd[:, i, :], 0.0, ALU.mult, ALU.add))
            dve.tensor_tensor(sd, cs, sd, ALU.subtract).then_inc(cs_ready, 1)
            dve.wait_ge(aa_ready, 4)
            dve.wait_ge(nrm_ready, 2)
            link(dve.tensor_scalar(nrm, nrm, 1e-12, None, ALU.max))
            link(dve.reciprocal(nrm, nrm))
            link(dve.tensor_tensor(kk, kk, nrm, ALU.mult))
            for i in range(NP2):
                link(dve.tensor_scalar(nrm[:, i, :], aa[:, i, :], -1.0, col2("rwkv_k_a_2")[:, i:i + 1], ALU.add, ALU.mult))
            link(dve.scalar_tensor_tensor(out=zk, in0=nrm, scalar=1.0, in1=zk, op0=ALU.add, op1=ALU.mult))
            for i in range(NP2):
                ins = dve.scalar_tensor_tensor(out=kk2[:, i, :], in0=zr[:, i, :], scalar=col2("rwkv_r_k_2")[:, i:i + 1], in1=zk[:, i, :],
                                               op0=ALU.mult, op1=ALU.mult)
            ins.then_inc(rk_ready, 1)
            dve.wait_ge(exp3_ready, 3)
            link(dve.tensor_tensor(ar[:, :, 1, :], zr, e_pos, ALU.mult))
            link(dve.scalar_tensor_tensor(out=ar[:, :, 0, :], in0=kk, scalar=-1.0, in1=e_before, op0=ALU.mult, op1=ALU.mult))
            link(dve.tensor_tensor(aa, aa, kk, ALU.mult))
            link(dve.tensor_tensor(b_hat, aa, e_neg, ALU.mult))
            dve.tensor_tensor(k_hat, zk, e_neg, ALU.mult).then_inc(hats_ready, 1)
            dve.wait_ge(bonus_done, 1)
            dve.tensor_copy(bonus, bank[6][:, 0:TT * NQ].rearrange("p (t h) -> p t h", t=TT)).then_inc(bonus_ready, 1)
            for t in range(TT):
                dve.wait_ge(nat_done, 4 + t + 1)
                dve.tensor_copy(x0[:, t, :, 0:HD], bank[t][:, :].rearrange("p (h k) -> p h k", h=NQ)).then_inc(nat_ready, 1)
            for t in range(TT):
                dve.wait_ge(nat_done, 6 + t + 1)
                dve.tensor_copy(vn[:, t, :], bank[6 + t][:, :]).then_inc(nat_ready, 1)
            dve.wait_ge(qkv2_raw, 4)
            dve.wait_ge(rows2_in, 16)
            heads = lambda a: a.rearrange("p w t (h d) -> p (w t h) d", d=HD)
            link(dve.tensor_tensor(sq2, qk2, qk2, ALU.mult))
            dve.tensor_reduce(ss_qk, heads(sq2), AX.X, ALU.add).then_inc(ss_ready, 1)
            dve.wait_ge(rs_ready, 1)
            link(dve.reciprocal(rs_qk, rs_qk))
            link(dve.tensor_tensor(heads(qk2), heads(qk2), wide(rs_qk, HD), ALU.mult))
            dve.wait_ge(trig_ready, 2)
            for w, g in enumerate(("q_norm_g_2", "k_norm_g_2")):
                a = qk2[:, w].rearrange("p t (h d) -> p (t h) d", d=HD)
                link(dve.tensor_tensor(a, a, row2(g).unsqueeze(1).broadcast_to([P, TT * NQ, HD]), ALU.mult))
                for t in range(TT):
                    at = qk2[:, w, t, :].rearrange("p (h d) -> p h d", d=HD)
                    lo, hi = at[:, :, 0:ROT], at[:, :, ROT:2 * ROT]
                    c8, s8 = (x[:, t, :].unsqueeze(1).broadcast_to([P, NQ, ROT]) for x in (cosv, sinv))
                    t0, t1 = rope_t[:, 0, 0:NQ, :], rope_t[:, 0, NQ:2 * NQ, :]
                    t2, t3 = rope_t[:, 1, 0:NQ, :], rope_t[:, 1, NQ:2 * NQ, :]
                    link(dve.tensor_tensor(t0, lo, c8, ALU.mult))
                    link(dve.tensor_tensor(t1, hi, s8, ALU.mult))
                    link(dve.tensor_tensor(t2, hi, c8, ALU.mult))
                    link(dve.tensor_tensor(t3, lo, s8, ALU.mult))
                    link(dve.tensor_tensor(lo, t0, t1, ALU.subtract))
                    ins = dve.tensor_tensor(hi, t2, t3, ALU.add)
                    if (w, t) != (1, TT - 1):
                        link(ins)
            ins.then_inc(qk2_ready, 1)

            def soft_max2(t, pr):
                o = t * NQ
                link(dve.tensor_reduce(nmax2[:, o:o + NQ], pr, AX.X, ALU.max))
                dve.tensor_scalar(nmax2[:, o:o + NQ], nmax2[:, o:o + NQ], -1.0, None, ALU.mult).then_inc(neg_max, 1)

            dve.wait_ge(scores_done, 3)
            for b in range(4):
                s3 = bank[4 + b][:, :].rearrange("p (m s) -> p m s", m=2)
                link(dve.tensor_scalar(prob2_1[:, 2 * b:2 * b + 2, 0:P], s3[:, :, 0:P], HD ** -0.5, None, ALU.mult))
                masked(prob2_1[:, 2 * b:2 * b + 2, P:T], s3[:, :, P:T], const("causal").unsqueeze(1).broadcast_to([P, 2, P]))
            soft_max2(0, prob2_1)
            dve.wait_ge(scores_done, 4)
            for half in range(2):
                masked(prob2_0[:, 4 * half:4 * half + 4, :], bank[half][:, :].rearrange("p (m s) -> p m s", m=4),
                       const("causal").unsqueeze(1).broadcast_to([P, 4, P]))
            soft_max2(1, prob2_0)
            for t, pr in enumerate((prob2_1, prob2_0)):
                o = t * NQ
                dve.wait_ge(exp_done, 18 + (t + 1) * NQ)
                link(dve.reciprocal(den2[:, o:o + NQ], den2[:, o:o + NQ]))
                dve.tensor_tensor(pr, pr, wide(den2[:, o:o + NQ], pr.shape[2]), ALU.mult).then_inc(prob_ready, 1)

            two = lambda a: a[:, :].rearrange("p (m w t) -> p m w t", m=2, w=2)
            over = lambda a, n: a.unsqueeze(1).broadcast_to([P, n] + list(a.shape[1:]))
            both = lambda n: const2_sb[:, const2_at[n][0]:const2_at[n][0] + T].rearrange("p (w t) -> p w t", w=2)
            MA_mask, NK_mask = both("subT_before"), both("chunkT_before")
            for tt in range(TT):
                for b in range(2):
                    B, Z = bank[4 * b:4 * b + 4], batch[b]
                    dve.wait_ge(rec_done, count(tensor_steps, "m", tt, b))
                    for half in range(2):
                        ins = dve.tensor_tensor(Z["Mb"][:, 2 * half:2 * half + 2, :], B[2 * half][:, 0:T].rearrange("p (m t) -> p m t", m=2),
                                                over(const2("sub_before"), 2), ALU.mult)
                    ins.then_inc(rec_ready, 1)
                for b in range(2):
                    B, Z = bank[4 * b:4 * b + 4], batch[b]
                    for half in range(2):
                        src, hd = two(B[2 * half + 1]), slice(2 * half, 2 * half + 2)
                        dve.tensor_tensor(Z["MA"][:, hd], src, over(MA_mask, 2), ALU.mult)
                        ins = dve.tensor_tensor(Z["MoT"][:, hd, :], src[:, :, 0, :], over(const2("off_subT"), 2), ALU.mult)
                    ins.then_inc(rec_ready, 1)
                for b in range(2):
                    B, Z = bank[4 * b:4 * b + 4], batch[b]
                    dve.wait_ge(rec_done, count(tensor_steps, "nk", tt, b))
                    for half in range(2):
                        src, hd = two(B[2 * half]), slice(2 * half, 2 * half + 2)
                        ins = dve.tensor_tensor(Z["NK"][:, hd], src, over(NK_mask, 2), ALU.mult)
                    ins.then_inc(rec_ready, 1)
                for b in range(2):
                    B, Z = bank[4 * b:4 * b + 4], batch[b]
                    dve.wait_ge(rec_done, count(tensor_steps, "p4", tt, b))
                    for half in range(2):
                        src, hd = two(B[half]), slice(2 * half, 2 * half + 2)
                        dve.tensor_copy(Z["MA"][:, hd, 0, :], src[:, :, 0, :])
                        ins = dve.tensor_tensor(Z["PU"][:, hd, 1, :], Z["PU"][:, hd, 1, :], src[:, :, 1, :], ALU.add)
                    ins.then_inc(rec_ready, 1)
                for done, which, before in (("p8", 0, "U2"), ("du", 1, "U4")):
                    for b in range(2):
                        B, Z = bank[4 * b:4 * b + 4], batch[b]
                        dve.wait_ge(rec_done, count(tensor_steps, done, tt, b))
                        dve.wait_ge(rec_ready, count(vector_steps, before, tt, b))
                        dve.tensor_tensor(Z["PU"][:, :, 1, :], Z["PU"][:, :, 1, :], B[which][:, :].rearrange("p (m t) -> p m t", m=4),
                                          ALU.add).then_inc(rec_ready, 1)
                for b in range(2):
                    B, Z = bank[4 * b:4 * b + 4], batch[b]
                    dve.wait_ge(rec_done, count(tensor_steps, "x3", tt, b))
                    dve.tensor_tensor(Z["X1"], Z["X1"], B[0][:, :].rearrange("p (m t) -> p m t", m=4), ALU.add).then_inc(rec_ready, 1)
                for b in range(2):
                    B = bank[4 * b:4 * b + 4]
                    dve.wait_ge(rec_done, count(tensor_steps, "rT", tt, b))
                    dve.tensor_tensor(rT[:, 2 * b:2 * b + 2, :], B[1][:, 0:T].rearrange("p (i t) -> p i t", i=2),
                                      ar[:, 2 * b:2 * b + 2, 1, tt * P:(tt + 1) * P], ALU.add).then_inc(rec_ready, 1)
                for b in range(2):
                    B = bank[4 * b:4 * b + 4]
                    dve.wait_ge(rec_done, count(tensor_steps, "fh", tt, b))
                    for c in range(4):
                        pr = slice(2 * b, 2 * b + 2)
                        dve.tensor_tensor(ft[:, c, pr, :], B[c][:, 0:P].rearrange("p (i k) -> p i k", i=2), over(const2("ident64"), 2), ALU.add)
                        ins = dve.tensor_copy(hs[:, c, pr, :], B[c][:, P:T].rearrange("p (i k) -> p i k", i=2))
                    ins.then_inc(rec_ready, 1)
                for c in range(4):
                    number = 4 * tt + c
                    if number == 7:
                        break
                    end = tt * P + (c + 1) * CH - 1
                    ecl = e_pos[:, :, end:end + 1].broadcast_to([P, NP2, HD])
                    if number == 0:
                        dve.wait_ge(rec_ready, count(vector_steps, "FH", 0, 1))
                        dve.tensor_tensor(state, hs[:, 0], ecl, ALU.mult).then_inc(st_ready, 1)
                        continue
                    dve.wait_ge(st_done, number)
                    link(dve.tensor_tensor(st_tmp, bank[0][:, 0:T].rearrange("p (i v) -> p i v", i=NP2), hs[:, c], ALU.add))
                    dve.tensor_tensor(state, st_tmp, ecl, ALU.mult).then_inc(st_ready, 1)
            dve.wait_ge(y2_ready, 4)
            y3 = y2.rearrange("p t (h d) -> p (t h) d", d=HD)
            q3 = sqy.rearrange("p t (h d) -> p (t h) d", d=HD)
            link(dve.tensor_reduce(y_sum, y3, AX.X, ALU.add))
            link(dve.tensor_scalar(y_sum, y_sum, 1.0 / HD, None, ALU.mult))
            link(dve.tensor_tensor(y3, y3, wide(y_sum, HD), ALU.subtract))
            link(dve.tensor_tensor(q3, y3, y3, ALU.mult))
            dve.tensor_reduce(y_sum2, q3, AX.X, ALU.add).then_inc(g_var, 1)
            link(dve.tensor_tensor(bv.rearrange("p t (h d) -> p (t h) d", d=HD), vn.rearrange("p t (h d) -> p (t h) d", d=HD),
                                   wide(bonus.rearrange("p t h -> p (t h)"), HD), ALU.mult))
            dve.wait_ge(g_stds, 2)
            link(dve.reciprocal(y_std, y_std))
            link(dve.tensor_tensor(y3, y3, wide(y_std, HD), ALU.mult))
            link(dve.tensor_tensor(y2, y2, over(row2("rwkv_ln_g_2"), TT), ALU.mult))
            link(dve.tensor_tensor(y2, y2, over(row2("rwkv_ln_b_2"), TT), ALU.add))
            link(dve.tensor_tensor(y2, y2, bv, ALU.add))
            dve.tensor_tensor(y2, y2, g_gate, ALU.mult).then_inc(ya_ready, 1)
            for n2 in range(2):
                for br, (sgx, f) in enumerate(((sga, "branch_a"), (sgb, "branch_b"))):
                    dve.wait_ge(w2_used, use_count(f, n2 + 1))
                    dve.wait_ge(sg_a, 4 * n2 + 2 * br + 2)
                    for t in range(TT):
                        ins = dve.tensor_tensor(sgx[:, t, :], sgx[:, t, :], bank[(6 if br == 0 else 2) + t][:, :], ALU.mult)
                        if br == 0:
                            if t == 1:
                                link(ins)
                            continue
                        link(ins)
                        ins = dve.tensor_tensor(mm[:, t, n2 * BANK:(n2 + 1) * BANK], sga[:, t, :], sgb[:, t, :], ALU.add)
                        if t == 1:
                            ins.then_inc(mm_ready, 1)
            for t in range(TT):
                for n2 in range(2):
                    dve.wait_ge(u_done, 2 * t + n2 + 1)
                    ins = dve.tensor_tensor(x1[:, t, n2 * BANK:(n2 + 1) * BANK], x1[:, t, n2 * BANK:(n2 + 1) * BANK],
                                            bank[2 * t + n2][:, :], ALU.add)
                ins.then_inc(x2_ready, 1)
            rms_norm(hn2, 2)
            scaled_T(6, "norm2_g_2")
            with dve.Fori(0, FT_N // 2) as it:
                now = dve.snap(it + 1)
                for i in range(2):
                    j = it * 2 + i
                    tap = lambda n: col2(n)[:, bass.ds(j, 1)]
                    a = bank[4 + i][:, 0:T]
                    dve.wait_ge(ffu_used[i], now)
                    dve.tensor_scalar(conv[:, i, :], a, tap("conv2"), tap("ffn_conv_b_2"), ALU.mult, ALU.add).then_inc(conv1[i], 1)
                    dve.wait_ge(conv1[i], now)
                    dve.scalar_tensor_tensor(out=conv[:, i, 1:T], in0=a[:, 0:T - 1], scalar=tap("conv1"), in1=conv[:, i, 1:T],
                                             op0=ALU.mult, op1=ALU.add).then_inc(conv2[i], 1)
                    dve.wait_ge(conv2[i], now)
                    dve.scalar_tensor_tensor(out=conv[:, i, 2:T], in0=a[:, 0:T - 2], scalar=tap("conv0"), in1=conv[:, i, 2:T],
                                             op0=ALU.mult, op1=ALU.add).then_inc(conv_ready[i], 1)
                    dve.wait_ge(gelu_ready[i], now)
                    dve.tensor_tensor(hid2[:, i, :], conv[:, i, :], bank[4 + i][:, T:2 * T], ALU.mult).then_inc(hid2_ready[i], 1)
            dve.wait_ge(ffn_done, 1)
            for n2 in range(2):
                dve.tensor_copy(out_sb[:, 1, n2 * BANK:(n2 + 1) * BANK], bank[2 + n2][:, :]).then_inc(out_ready[1], 1)

        @block.gpsimd
        def _(pool):
            for tt in range(TT):
                for b in range(2):
                    Z = batch[b]
                    pool.wait_ge(rec_ready, count(vector_steps, "MA", tt, b))
                    pool.tensor_tensor(Z["PU"][:, :, 1, :], Z["MA"][:, :, 0, :], ident.unsqueeze(1).broadcast_to([P, 4, P]),
                                       ALU.add).then_inc(one_added, 1)


def tiled(a, width):
    return np.ascontiguousarray(a.reshape(-1, P, width).transpose(1, 0, 2))


def arrange(inputs):
    i = {k: np.asarray(v) for k, v in inputs.items()}
    x = i["x"][0]
    heads = np.concatenate([np.r_[j * HD:(j + 1) * HD, (4 + j) * HD:(5 + j) * HD] for j in range(4)])
    order = np.concatenate([heads, np.arange(512, 1792)])
    w_in, b_in = i["w_in"][0][:, order], i["b_in"][0][order]
    row_of = {"b_in_vug": b_in[W_QK:]}
    rows = np.concatenate([row_of.get(n, i[n][0] if n in i else None) for n, _ in ROWS])
    columns = np.concatenate([b_in[:W_QK].reshape(5, P).T, i["b_spatial"][0].T], axis=1)
    w = i["w_in_2"][0]
    part = lambda lo, n: tiled(w[:, lo:lo + n], n).reshape(P, -1)
    lora_at, q_at, gate_at = 3 * C2, 3 * C2 + LORA, 6 * C2 + LORA
    mu = i["rwkv_mu_2"][0]
    mu_lora = np.pad(mu[lora_at:q_at], (0, 3 * P - LORA))
    vectors = {"mu_lora": mu_lora, "mu_r": mu[:C2], "mu_k": mu[C2:2 * C2], "mu_v": mu[2 * C2:3 * C2]}
    vectors |= {f"conv{j}": i["ffn_conv_w_2"][0][j] for j in range(3)}
    columns2 = [(vectors[n] if n in vectors else i[n][0]).reshape(-1, P).T for n, _ in COLUMNS2]
    up = i["w_ffn_up_2"][0].reshape(KD, P, 2, FT_N, P).transpose(3, 1, 2, 0, 4).reshape(FT_N, P, 2 * D)
    second = {
        "consts2": constants2(), "columns2": np.ascontiguousarray(np.concatenate(columns2, axis=1)),
        "rows2": np.concatenate([i[n][0] for n, _ in ROWS2]),
        "w_lora_up": np.concatenate([i["w_decay_up_2"][0], i["w_aaa_up_2"][0]]), "w_gate_up_2": i["w_gate_up_2"][0],
        "pos": np.ascontiguousarray(i["positions_2"].reshape(TT, P).T),
        "ffn_up": np.ascontiguousarray(up), "ffn_down": i["w_ffn_down_2"][0],
        "w2_lora": part(lora_at, LORA), "w2_r": part(0, C2), "w2_k": part(C2, C2), "w2_v": part(2 * C2, C2),
        "w2_q2": part(q_at, C2), "w2_k2": part(q_at + C2, C2), "w2_v2": part(q_at + 2 * C2, C2),
        "w2_branch_a": tiled(i["w_branch_a_2"][0], D).reshape(P, -1), "w2_branch_b": tiled(i["w_branch_b_2"][0], D).reshape(P, -1),
        "w2_out0": tiled(i["w_out_2"][0][:C2], D).reshape(P, -1), "w2_out1": tiled(i["w_out_2"][0][C2:], D).reshape(P, -1),
    }
    second |= {f"w2_gate_{'ab'[br]}{n}": part(gate_at + br * D + n * C2, C2) for br in range(2) for n in range(2)}
    return second | {
        "x": x, "xT": tiled(np.ascontiguousarray(x.T), T), "consts": constants(), "columns": np.ascontiguousarray(columns),
        "rows": rows, "w_in": tiled(w_in, 1792), "w_out": tiled(i["w_out"][0], D),
        "wsT": np.ascontiguousarray(i["w_spatial"][0].transpose(2, 0, 1)), "w_router": tiled(i["w_router"][0], NE),
        "w_gate": i["w_gate"][0], "w_up": i["w_up"][0], "w_down": i["w_down"][0], "b_down": i["b_down"][0],
        "b_gate_up": np.concatenate([i["b_gate"][0], i["b_up"][0]], axis=1),
    }


def kernel(**inputs):
    from concourse import bacc
    from concourse.bass_utils import run_bass_kernel_spmd

    nc = bacc.Bacc("TRN2", target_bir_lowering=False, num_devices=1)
    arrays = arrange(inputs)
    A = {n: nc.dram_tensor(f"in_{n}", a.shape, mybir.dt.from_np(a.dtype), kind="ExternalInput").ap() for n, a in arrays.items()}
    out = nc.dram_tensor("out", (T, D), F32, kind="ExternalOutput").ap()
    program(nc, A, out)
    r = run_bass_kernel_spmd(nc, [{f"in_{n}": a for n, a in arrays.items()}], core_ids=[0])
    return r.results[0]["out"].reshape(1, T, D)
```

```python
from contextlib import ExitStack

import numpy as np

import concourse.bass as bass
from concourse import mybir

F32 = mybir.dt.float32
F32R = mybir.dt.float32r
BF16 = mybir.dt.bfloat16
I32 = mybir.dt.int32
U32 = mybir.dt.uint32
ALU = mybir.AluOpType
ACT = mybir.ActivationFunctionType
AX = mybir.AxisListType

P = 128
T = 256
TT = T // P
D = 1024
KD = D // P
HD = 64
NQ = 8
G1 = 512
NG = 8
GD = G1 // NG
NE = 32
TOPK = 4
CAP = 64
PASSES = T // CAP
COLS = NE * PASSES + 2
BANK = 512
SLOT = 2048
SLOTS = 12
LN_EPS = 1e-5
ALPHA1 = 2.0 ** 0.25
LIMIT = 7.0
SWIGLU_ALPHA = 1.702
NEG = -1e30
W_QK, W_VUG = 640, 1152

ROWS = [("b_in_vug", W_VUG), ("ln_v_g", G1), ("ln_v_b", G1), ("b_router", NE), ("sinks", NQ),
        ("b_out", D), ("ln1_g", D), ("ln1_b", D), ("ln2_g", D), ("ln2_b", D)]
COLUMNS = [("b_in_qk", 5), ("b_s", NG)]
CONSTS = [("ident", P), ("iota2", P), ("iota32", NE), ("upto", P), ("ones", P), ("causal", P), ("before", P)]


KAPPA = float(np.exp(-0.5))
NP2 = 4
CH = 32
SUB = 16
C2 = 512
FT_N = 22
ROT = 8
NORM_EPS, GN_EPS, ROPE_THETA = 1e-6, 64e-5, 500000.0
WBUF = 4096
LORA = 288
LORA_W = 3 * P

ROWS2 = [("q_norm_g_2", HD), ("k_norm_g_2", HD), ("rwkv_ln_g_2", C2), ("rwkv_ln_b_2", C2)]
COLUMNS2 = [("mu_lora", 3), ("mu_r", NP2), ("mu_k", NP2), ("mu_v", NP2), ("decay_bias_2", NP2), ("aaa_bias_2", NP2),
            ("rwkv_k_k_2", NP2), ("rwkv_k_a_2", NP2), ("rwkv_r_k_2", NP2), ("norm1_g_2", KD), ("norm2_g_2", KD),
            ("conv0", FT_N), ("conv1", FT_N), ("conv2", FT_N), ("ffn_conv_b_2", FT_N)]
CONSTS2 = [("sub_before", P), ("subT_before", P), ("chunkT_upto", P), ("off_subT", P), ("chunkT_before", P), ("chunkT_upto2", P),
           ("head_ones", P), ("head_col", 2), ("chunk_start", T), ("ident64", HD), ("inv_freq", ROT)]


def offsets(parts):
    at, n = {}, 0
    for name, width in parts:
        at[name] = (n, width)
        n += width
    return at, n


def constants():
    i = np.arange(P)
    row, col = i[:, None], i[None, :]
    tab = {
        "ident": np.eye(P), "iota2": np.tile(col % CAP, (P, 1)), "iota32": np.tile(np.arange(NE), (P, 1)),
        "upto": row <= col, "ones": np.ones((P, P)),
        "causal": np.where(col <= row, 0.0, NEG), "before": np.where(col > row, 0.0, NEG),
    }
    return np.concatenate([np.asarray(tab[n], np.float32) for n, _ in CONSTS], axis=1)


def constants2():
    i = np.arange(P)
    row, col = i[:, None], i[None, :]
    chunk, sub = row // CH == col // CH, row // SUB == col // SUB
    t = np.arange(T)
    freq = np.float32(ROPE_THETA) ** (-np.arange(ROT, dtype=np.float32) / np.float32(ROT))
    tab = {
        "sub_before": sub & (col < row), "subT_before": sub & (row < col), "chunkT_upto": chunk & (row <= col),
        "off_subT": chunk & ~sub & (row < col), "chunkT_before": chunk & (row < col), "chunkT_upto2": chunk & (row <= col),
        "head_ones": row // HD == col // HD, "head_col": row // HD == np.arange(2)[None, :],
        "chunk_start": np.tile(t % CH != 0, (P, 1)), "ident64": row % HD == np.arange(HD)[None, :],
        "inv_freq": np.tile(freq, (P, 1)),
    }
    return np.concatenate([np.asarray(tab[n], np.float32) for n, _ in CONSTS2], axis=1)


def program(nc, A, out):
    ctx = ExitStack()
    with ctx:
        def sem(name):
            return ctx.enter_context(nc.semaphore(name))

        def area(name, floats):
            at = -(-nc.sbuf_base // 32) * 32
            full = ctx.enter_context(nc.sbuf_tensor(name, [P, floats], F32))
            return full, nc.alloc_sbuf_tensor_at(name + "_parts", [P, floats], F32R, offset=at)

        ring, ring_parts = area("ring", SLOTS * SLOT)
        work, work_parts = area("work", 27500)
        bank = [ctx.enter_context(nc.psum_tensor(f"bank{i}", [P, BANK], F32)) for i in range(8)]
        top = [0]

        def take(floats):
            a = work[:, top[0]:top[0] + floats]
            top[0] += floats
            assert top[0] <= 27500, top
            return a

        rows_at, rows_n = offsets(ROWS)
        cols_at, cols_n = offsets(COLUMNS)
        const_at, const_n = offsets(CONSTS)
        const_sb = take(const_n)
        cols_sb = take(cols_n)
        rows_sb = take(rows_n)
        const = lambda n: const_sb[:, const_at[n][0]:sum(const_at[n])]
        colv = lambda n: cols_sb[:, cols_at[n][0]:sum(cols_at[n])]
        rowv = lambda n: rows_sb[:, rows_at[n][0]:sum(rows_at[n])]
        ident = const("ident")
        tables_at = top[0]
        tables = take(2 * TT * COLS)
        posm = tables[:, 0:TT * COLS].rearrange("p (t e) -> p t e", t=TT)
        gate_of = tables[:, TT * COLS:].rearrange("p (t e) -> p t e", t=TT)
        small = take(320)
        small_at = [0]

        def little(*shape):
            n = int(np.prod(shape))
            a = small[:, small_at[0]:small_at[0] + n]
            small_at[0] += n
            assert small_at[0] <= 320
            return a if len(shape) == 1 else a.rearrange("p (a b) -> p a b", a=shape[0])

        eps1, eps2, eps3, n_iter_f = little(1), little(1), little(1), little(4)
        nmax, den, sink_e = little(TT * NQ), little(TT * NQ), little(TT * NQ)
        g_sum, g_sum2, g_std = little(TT * NG), little(TT * NG), little(TT * NG)
        logits, chosen = little(TT, NE), little(TT, NE)
        top8, top_i, top_f, gates4 = little(TT, 8), little(TT, 8).bitcast(U32), little(TT, TOPK), little(TT, TOPK)
        ntop, gsum, rstd, mv, stats = little(TT), little(TT), little(TT), little(TT, 2), little(2, 6)
        w_router = take(KD * NE).rearrange("p (k e) -> p k e", k=KD)
        n_iter = ctx.enter_context(nc.sbuf_tensor("n_iter", [1, 2], I32))

        xT = ring[:, 22528:24576].rearrange("p (k t) -> p k t", k=KD)
        w_in = ring[:, 0:KD * 1792].rearrange("p (k n) -> p k n", k=KD)
        w_out = ring[:, 14336:22528].rearrange("p (k n) -> p k n", k=KD)
        x_nat = take(TT * D).rearrange("p (t d) -> p t d", t=TT)
        r2_at = top[0]
        wsT_qkT = take(NG * P + 5 * T)
        wsT = wsT_qkT[:, 0:NG * P].rearrange("p (g t) -> p g t", g=NG)
        qkT = wsT_qkT[:, NG * P:].rearrange("p (i t) -> p i t", i=5)
        v_nat = take(TT * P).rearrange("p (t c) -> p t c", t=TT)
        ug = take(2 * TT * G1)
        u_nat = ug[:, 0:TT * G1].rearrange("p (t c) -> p t c", t=TT)
        g_nat = ug[:, TT * G1:].rearrange("p (t c) -> p t c", t=TT)
        prob = take(3 * 1024)
        prob0 = prob[:, 0:1024].rearrange("p (h s) -> p h s", h=NQ)
        prob1 = prob[:, 1024:3072].rearrange("p (h s) -> p h s", h=NQ)
        pT = take(3 * 1024).rearrange("p (j h t) -> p j h t", j=3, h=NQ)
        mixT_at = top[0]
        mixT = take(KD * T).rearrange("p (k t) -> p k t", k=KD)
        sq = take(TT * G1).rearrange("p (t c) -> p t c", t=TT)
        h = ug.rearrange("p (t d) -> p t d", t=TT)
        h_part = prob.bitcast(BF16).rearrange("p (i t d) -> p i t d", i=3, t=TT)
        hT = pT.rearrange("p j h t -> p (j h t)")[:, 0:2048].rearrange("p (k t) -> p k t", k=KD)
        resid = x_nat
        ln_tmp = sq.rearrange("p t c -> p (t c)")
        chosen4 = sq.rearrange("p t c -> p (t c)")[:, 0:TT * TOPK * NE].rearrange("p (t k e) -> p t k e", t=TT, k=TOPK)
        pool1 = mixT.rearrange("p k t -> p (k t)")
        gt, sg, uc, vv = (pool1[:, i * 512:(i + 1) * 512] for i in range(4))
        pool2 = rows_sb[:, rows_at["b_out"][0]:rows_at["b_out"][0] + 3072]
        hid, yy = pool2[:, 0:512], pool2[:, 512:1024]
        hidT = pool2[:, 1024:1536].rearrange("p (j c) -> p j c", j=4)
        x_e = pool2[:, 1536:2048].rearrange("p (k s) -> p k s", k=KD)
        place_g = pool2[:, 2048:2304].rearrange("p (t s) -> p t s", t=TT)
        place_T = pool2[:, 2304:2560]
        place = pool2[:, 2560:2624].bitcast(BF16).rearrange("p (t s) -> p t s", t=TT)
        gateT = pool2[0:NE, 2624:2880]
        b_down_area = take(D)
        b_down = b_down_area[0:NE, :]
        bias_row = wsT_qkT[0:1, 0:2 * D]

        consts_in, x_in, xT_in, mix_rows_in = sem("consts_in"), sem("x_in"), sem("xT_in"), sem("mix_rows_in")
        ln_rows_in, wsT_in = sem("ln_rows_in"), sem("wsT_in")
        w_in_in = [sem(f"w_in_in{i}") for i in range(4)]
        w_out_in = sem("w_out_in")
        router_in = sem("router_in")
        proj_done, qk_ready, v_ready, ug_biased, ug_gelu = (sem(n) for n in ("proj_done", "qk_ready", "v_ready", "ug_biased", "ug_gelu"))
        wsT_masked, g_normed, mixed_done, sgu_ready = (sem(n) for n in ("wsT_masked", "g_normed", "mixed_done", "sgu_ready"))
        scores_done, neg_max, exp_done, prob_ready = (sem(n) for n in ("scores_done", "neg_max", "exp_done", "prob_ready"))
        pT_done, pT_ready, attn_done, attn_ready, sguT_done, sguT_ready = (
            sem(n) for n in ("pT_done", "pT_ready", "attn_done", "attn_ready", "sguT_done", "sguT_ready"))
        mix_done, var_ready, std_ready, h_ready, hT_done, hT_ready = (
            sem(n) for n in ("mix_done", "var_ready", "std_ready", "h_ready", "hT_done", "hT_ready"))
        router_done, top_ready, top_exp, chosen_ready = (
            sem(n) for n in ("router_done", "top_ready", "top_exp", "chosen_ready"))
        iter_ready, gateT_ready, split_ready = (sem(n) for n in ("iter_ready", "gateT_ready", "split_ready"))
        slot_in = [sem(f"slot_in{i}") for i in range(SLOTS)]
        slots_used = sem("slots_used")
        bias_in, bias_free = sem("bias_in"), sem("bias_free")
        place_ready, place_g_ready, gather_done, x_e_ready = (sem(n) for n in ("place_ready", "place_g_ready", "gather_done", "x_e_ready"))
        gt_ready, sg_ready, uc_ready, vv_ready, hid_ready = (sem(n) for n in ("gt_ready", "sg_ready", "uc_ready", "vv_ready", "hid_ready"))
        hidT_done, hidT_ready, place_T_done, place_T_ready, y_ready = (
            sem(n) for n in ("hidT_done", "hidT_ready", "place_T_done", "place_T_ready", "y_ready"))
        acc_done, x1_ready, stored = (sem(n) for n in ("acc_done", "x1_ready", "stored"))
        rest_ready, g_var, g_stds = sem("rest_ready"), sem("g_var"), sem("g_stds")
        bonus_ready = sem("bonus_ready")
        dve_step = sem("dve_step")

        def views(a, *parts):
            n, got = 0, []
            for shape in parts:
                w = int(np.prod(shape))
                v = a[:, n:n + w]
                names = "abcd"[:len(shape)]
                if len(shape) > 1:
                    v = v.rearrange(f"p ({' '.join(names)}) -> p {' '.join(names)}", **dict(zip(names, shape)))
                got.append(v)
                n += w
            assert n <= a.shape[1], (n, a.shape)
            return got

        rows2_at, rows2_n = offsets(ROWS2)
        cols2_at, cols2_n = offsets(COLUMNS2)
        const2_at, const2_n = offsets(CONSTS2)
        kept = pT.rearrange("p j h t -> p (j h t)")
        const2_sb, cols2_sb, rows2_sb, w_lora_up, pos_f = views(kept, (const2_n,), (cols2_n,), (rows2_n,), (C2,), (TT,))
        pos_i = pos_f.bitcast(I32)
        const2 = lambda n: const2_sb[:, const2_at[n][0]:sum(const2_at[n])]
        col2 = lambda n: cols2_sb[:, cols2_at[n][0]:sum(cols2_at[n])]
        row2 = lambda n: rows2_sb[:, rows2_at[n][0]:sum(rows2_at[n])]
        w_gate_up = views(sq.rearrange("p t c -> p (t c)"), (2, C2))[0]
        r1 = rows_sb
        r2 = work[:, r2_at:r2_at + 7680]
        rt = ring[:, 4 * WBUF:4 * WBUF + 8192]
        x1 = resid
        hnT = views(mixT.rearrange("p k t -> p (k t)"), (KD, T))[0]
        hn = views(r2, (TT, D))[0]
        zr, zk, zv, lora, tmp, sd, aa = views(r1, (NP2, T), (NP2, T), (NP2, T), (3, T), (NP2, T), (NP2, T), (NP2, T))
        cs = tmp
        small2 = r1[:, 6912:rows_n]
        (ss, rms, ss_qk, rs_qk, cosv, sinv, ang, ang_n, nmax2, den2, bonus, y_sum, y_sum2, y_std) = views(
            small2, (TT,), (TT,), (2 * TT * NQ,), (2 * TT * NQ,), (TT, ROT), (TT, ROT), (TT, ROT), (TT, ROT),
            (TT * NQ,), (TT * NQ,), (TT, NQ), (TT * NQ,), (TT * NQ,), (TT * NQ,))
        ar, b_hat, k_hat, e_pos, g_gate, ybT = views(r2, (NP2, 2, T), (NP2, T), (NP2, T), (NP2, T), (TT, C2), (NP2, T))
        qk2, _, qkT2, prob_2 = views(rt, (2, TT, C2), (1024,), (2, NP2, T), (3072,))
        pT2 = views(rt, (3, NQ, P))[0]
        sq2 = views(rt[:, 5120:7168], (2, TT, C2))[0]
        rope_t = views(rt[:, 7168:7680], (2, TT * NQ, ROT))[0]
        prob2_0, prob2_1 = views(prob_2, (NQ, P), (NQ, T))
        v2 = views(b_down_area, (TT, C2))[0]
        _, e_neg, e_before, kk, kk2, nrm = views(rt, (3072,), (NP2, T), (NP2, T), (NP2, T), (NP2, T), (NP2, T))
        x0, = views(r1, (TT, NQ, P))
        vn, bn, kn = views(r1[:, 3840:6912], (TT, C2), (TT, C2), (TT, C2))
        batch = []
        for b, a in enumerate((rt, ring[:, 2 * WBUF:4 * WBUF])):
            names = "Mb MA MoT NK P2 PU X1".split()
            parts = [(4, P), (4, 2, P), (4, P), (4, 2, P), (4, P), (4, 2, P), (4, P)]
            batch.append(dict(zip(names, views(a, *parts))))
        ft, hs, rT = views(rt[:, 5120:8192], (4, NP2, HD), (4, NP2, HD), (NP2, P))
        y2, state, st_tmp = views(ring[:, 2 * WBUF + 5120:4 * WBUF], (TT, C2), (NP2, HD), (NP2, HD))
        sqy, bv = views(r1, (TT, C2), (TT, C2))
        yaT = views(r2, (NP2, T))[0]
        gate_at = {"gate_a0": sq.rearrange("p t c -> p (t c)"), "gate_b0": r1[:, 2048:3072], "gate_a1": ring[:, 4096:5120], "gate_b1": ring[:, 5120:6144]}
        gate = {f: views(a, (TT, BANK))[0] for f, a in gate_at.items()}
        mm, = views(r1[:, 3840:5888], (TT, D))
        mT, = views(r1, (KD, T))
        hn2 = views(r1, (TT, D))[0]
        conv, hid2 = views(r2[:, 1024:2048], (2, T), (2, T))
        hid2_hi, hid2_lo = views(work_parts[:, r2_at + 2048:r2_at + 3072], (2, T), (2, T))
        out_sb = views(r1[:, 2048:4096], (TT, D))[0]

        hnT_rest = views(work_parts[:, mixT_at:mixT_at + KD * T], (KD, T))[0]
        hnT_hi, hnT_hi2 = ([work_parts[:, at + k * T:at + (k + 1) * T] for k, at in enumerate(starts)] for starts in (
            [r2_at + 6144] * 6 + [tables_at - 6 * T] * 2, [r2_at + 4096] * KD))

        FILLS = ["lora", "r", "k", "v", "q2", "k2", "v2", "gate_a0", "gate_b0", "gate_a1", "gate_b1"]
        HALVES = [(f, half) for f in FILLS for half in range(2)]
        HBUF = WBUF // 2

        def half_width(f):
            return KD // 2 * (LORA_W if f == "lora" else C2)

        def half_view(n, of=ring, base=0):
            at = base + n % 4 * HBUF
            return of[:, at:at + half_width(HALVES[n][0])]

        def rest_of(n):
            return half_view(n, ring_parts)

        def upper_of(n):
            return half_view(n, ring_parts, 4 * HBUF)

        def used_count(f):
            return 2 * FILLS.index(f) + 2

        tail_at = {"branch_b": ring[:, 0:WBUF], "branch_a": ring[:, 2 * WBUF:3 * WBUF], "out0": ring[:, 4 * WBUF:5 * WBUF], "out1": ring[:, 5 * WBUF:6 * WBUF]}
        tail = {f: a.rearrange("p (k n) -> p k n", k=4) for f, a in tail_at.items()}
        FF = 3 * D
        ff_land = [ring[:, 3 * WBUF:3 * WBUF + FF], ring[:, 0:FF]]
        ff_hi = [ring_parts[:, at:at + FF] for at in (2 * WBUF, 4 * WBUF)]
        ff_rest = [ring_parts[:, at:at + FF] for at in (FF, 4 * WBUF + FF)]

        small2_in = sem("small2_in")
        half_in, half_used = [sem(f"half_in{b}") for b in range(4)], sem("half_used")
        half_upper, half_rest = sem("half_upper"), sem("half_rest")
        x_upper, x_rest, branch_done = sem("x_upper"), sem("x_rest"), sem("branch_done")
        tail_in = {f: sem(f"{f}_in") for f in ("branch_b", "branch_a", "out")}
        sq_done, rms_std, hn_ready = (sem(n) for n in ("sq_done", "rms_std", "hn_ready"))
        z_raw, lora_mixed, lora_ready, kk2_ready, cs_ready, exp3_ready = (
            sem(n) for n in ("z_raw", "lora_mixed", "lora_ready", "kk2_ready", "cs_ready", "exp3_ready"))
        lora_up_done, lora_up_ready, nrm_done, nrm_ready = (
            sem(n) for n in ("lora_up_done", "lora_up_ready", "nrm_done", "nrm_ready"))
        rk_ready, bonus_done, hats_ready, nat_done, nat_ready = (sem(n) for n in ("rk_ready", "bonus_done", "hats_ready", "nat_done", "nat_ready"))
        qkv2_raw, ang_ready, trig_ready, ss_ready, rs_ready, qk2_ready, qkT2_done, qkT2_ready = (
            sem(n) for n in ("qkv2_raw", "ang_ready", "trig_ready", "ss_ready", "rs_ready", "qk2_ready", "qkT2_done", "qkT2_ready"))
        tensor_steps = ["m", "nk", "p2", "nv", "p4", "p8", "du", "x1", "x2", "x3", "rT", "fh"]
        scalar_steps = ["P2", "x0", "P4", "P8", "X1", "X2"]
        vector_steps = ["Mb", "MA", "NK", "U2", "U4", "U8", "X3", "rT", "FH"]
        rec_done, rec_copied, rec_ready = sem("rec_done"), sem("rec_copied"), sem("rec_ready")
        one_added, st_done, st_ready, y2_done, y2_ready = (sem(n) for n in ("one_added", "st_done", "st_ready", "y2_done", "y2_ready"))

        def count(steps, step, tt, b):
            return (tt * len(steps) + steps.index(step)) * 2 + b + 1

        ya_ready = sem("ya_ready")
        u_done, gate_ready, mm_ready = (sem(n) for n in ("u_done", "gate_ready", "mm_ready"))
        ff_in, ff_upper, up_rest, down_rest, ffu_used, ffd_used = (
            [sem(f"{n}{i}") for i in range(2)] for n in ("ff_in", "ff_upper", "up_rest", "down_rest", "ffu_used", "ffd_used"))
        hidden_step, conv_ready, gelu_ready, hid2_ready = (
            [sem(f"{n}{i}") for i in range(2)] for n in ("hidden_step", "conv_ready", "gelu_ready", "hid2_ready"))
        ffn_done, out_ready = sem("ffn_done"), [sem(f"out_ready{t}") for t in range(TT)]

        block = ctx.enter_context(nc.Block())

        def expert_slot(e, j):
            which, c = (("w_gate", "w_up")[j % 2], j // 2) if j < 8 else ("w_down", j - 8)
            return A[which][bass.ds(e, 1), c * 256:(c + 1) * 256, :].rearrange("o (k p) n -> p (o k) n", p=P)

        def slot_view(j):
            return ring[:, j * SLOT:(j + 1) * SLOT].rearrange("p (k n) -> p k n", k=2)

        @block.sync
        def _(sp):
            sp.dma_start(xT, A["xT"]).then_inc(xT_in, 16)
            sp.dma_start(const_sb, A["consts"]).then_inc(consts_in, 16)
            sp.dma_start(cols_sb, A["columns"]).then_inc(consts_in, 16)
            for i in range(4):
                sp.dma_start(w_in[:, 2 * i:2 * i + 2, :], A["w_in"][:, 2 * i:2 * i + 2, :]).then_inc(w_in_in[i], 16)
            mix_n = rows_at["b_out"][0]
            sp.dma_start(rows_sb[:, 0:mix_n], A["rows"][0:mix_n].partition_broadcast(P)).then_inc(mix_rows_in, 16)
            sp.dma_start(wsT, A["wsT"]).then_inc(wsT_in, 16)
            for i in range(4):
                sp.dma_start(w_out[:, 2 * i:2 * i + 2, :], A["w_out"][:, 2 * i:2 * i + 2, :]).then_inc(w_out_in, 16)
            sp.dma_start(x_nat, A["x"].rearrange("(t p) d -> p t d", p=P)).then_inc(x_in, 16)
            sp.dma_start(rows_sb[:, mix_n:rows_n], A["rows"][mix_n:rows_n].partition_broadcast(P)).then_inc(ln_rows_in, 16)
            sp.dma_start(b_down, A["b_down"]).then_inc(ln_rows_in, 16)
            sp.wait_ge(proj_done, 7)
            for j in range(SLOTS):
                if j == 7:
                    sp.wait_ge(mix_done, 4)
                    sp.dma_start(bias_row, A["b_gate_up"][0:1, :]).then_inc(bias_in, 16)
                sp.dma_start(slot_view(j), expert_slot(0, j)).then_inc(slot_in[j], 16)
            sp.wait_ge(iter_ready, 1)
            sp.dma_start(const2_sb, A["consts2"]).then_inc(small2_in, 16)
            sp.dma_start(cols2_sb, A["columns2"]).then_inc(small2_in, 16)
            sp.dma_start(w_lora_up, A["w_lora_up"]).then_inc(small2_in, 16)
            sp.dma_start(w_gate_up[:, 0, :], A["w_gate_up_2"][0:P, :]).then_inc(small2_in, 16)
            sp.dma_start(w_gate_up[0:CH, 1, :], A["w_gate_up_2"][P:, :]).then_inc(small2_in, 16)
            sp.dma_start(pos_i, A["pos"]).then_inc(small2_in, 16)
            sp.dma_start(rows2_sb, A["rows2"].partition_broadcast(P)).then_inc(small2_in, 16)
            n = sp.value_load(n_iter[0:1, 0:1], min_val=NE, max_val=NE * PASSES)
            n_rest = sp.value_load(n_iter[0:1, 1:2], min_val=NE - 1, max_val=NE * PASSES - 1)
            with sp.Fori(1, n) as it:
                e = it % NE
                sp.wait_ge(bias_free, it)
                sp.dma_start(bias_row, A["b_gate_up"][bass.ds(e, 1), :]).then_inc(bias_in, 16)
                for j in range(SLOTS):
                    sp.wait_ge(slots_used, sp.snap(it * SLOTS - (SLOTS - j - 1)))
                    sp.dma_start(slot_view(j), expert_slot(e, j)).then_inc(slot_in[j], 16)
            for n2, (f, half) in enumerate(HALVES):
                if n2 < 4:
                    sp.wait_ge(slots_used, sp.snap(n_rest * SLOTS + n2 + 1))
                else:
                    sp.wait_ge(half_used, n2 - 3)
                w = half_width(f)
                sp.dma_start(half_view(n2), A[f"w2_{f}"][:, half * w:(half + 1) * w]).then_inc(half_in[n2 % 4], 16)
            sp.wait_ge(half_used, len(HALVES))
            sp.dma_start(tail_at["branch_b"], A["w2_branch_b"]).then_inc(tail_in["branch_b"], 16)
            sp.wait_ge(y2_ready, 4)
            for f in ("branch_a", "out0", "out1"):
                sp.dma_start(tail_at[f], A[f"w2_{f}"]).then_inc(tail_in[f.rstrip("01")], 16)

            def ff_load(i, j):
                sp.dma_start(ff_land[i][:, 0:2 * D], A["ffn_up"][bass.ds(j, 1), :, :].rearrange("o p n -> p (o n)")).then_inc(ff_in[i], 16)
                sp.dma_start(ff_land[i][:, 2 * D:FF], A["ffn_down"][bass.ds(j * P, P), :]).then_inc(ff_in[i], 16)

            sp.wait_ge(sguT_done, 2)
            ff_load(0, 0)
            sp.wait_ge(branch_done, 2)
            ff_load(1, 1)
            with sp.Fori(1, FT_N // 2) as it:
                for i in range(2):
                    sp.wait_ge(up_rest[i], it)
                    sp.wait_ge(down_rest[i], it)
                    ff_load(i, it * 2 + i)
            for t in range(TT):
                sp.wait_ge(out_ready[t], 2)
                sp.dma_start(out[t * P:(t + 1) * P, :], out_sb[:, t, :]).then_inc(stored, 16)
            sp.wait_ge(stored, 32)

        @block.tensor
        def _(pe):
            pe.wait_ge(xT_in, 16)
            for k in range(KD):
                first, last = k == 0, k == KD - 1
                if k % 2 == 0:
                    pe.wait_ge(w_in_in[k // 2], 16)
                for i in range(5):
                    ins = pe.matmul(bank[i // 2][:, (i % 2) * T:(i % 2 + 1) * T], w_in[:, k, i * P:(i + 1) * P], xT[:, k, :],
                                    start=first and i % 2 == 0, stop=last, skip_group_check=True)
                if last:
                    ins.then_inc(proj_done, 1)
                for c in range(3):
                    for t in range(TT):
                        to = bank[2][:, T + t * P:T + (t + 1) * P] if c == 0 else bank[3 + 2 * (c - 1) + t][:, :]
                        lo = W_QK + (0 if c == 0 else P + (c - 1) * G1)
                        ins = pe.matmul(to, xT[:, k, t * P:(t + 1) * P], w_in[:, k, lo:lo + (P if c == 0 else G1)],
                                        start=first and c > 0, stop=last, skip_group_check=True)
                        if last:
                            ins.then_inc(proj_done, 1)
            pe.wait_ge(qk_ready, 5)
            pe.wait_ge(v_ready, 2)
            s1_bank = [0, 1, 2, 7]
            for i in range(4):
                for half in range(2):
                    lo = half * HD
                    ins = pe.matmul(bank[s1_bank[2 * half + i // 2]][:, (i % 2) * T:(i % 2 + 1) * T],
                                    qkT[lo:lo + HD, i, P:T], qkT[lo:lo + HD, 4, :],
                                    start=i % 2 == 0, stop=True, skip_group_check=True)
            ins.then_inc(scores_done, 1)
            pe.wait_ge(ug_biased, 2)
            for i in range(4):
                for half in range(2):
                    lo = half * HD
                    ins = pe.matmul(bank[3 + half][:, i * P:(i + 1) * P], qkT[lo:lo + HD, i, 0:P], qkT[lo:lo + HD, 4, 0:P],
                                    start=i == 0, stop=True, skip_group_check=True)
            ins.then_inc(scores_done, 1)
            pe.wait_ge(ug_biased, 4)
            pe.wait_ge(wsT_masked, 1)
            pe.wait_ge(g_normed, 1)
            for g in range(NG):
                ins = pe.matmul(bank[5 + g // 4][:, (g % 4) * P:(g % 4 + 1) * P].rearrange("p (c d) -> p c d", c=TT),
                                wsT[:, g, :], g_nat[:, :, g * GD:(g + 1) * GD],
                                start=g % 4 == 0, stop=True, skip_group_check=True)
            ins.then_inc(mixed_done, 1)
            pe.wait_ge(prob_ready, 2)
            t_bank = [[3, 4], [0, 1], [2, 7]]
            for j in range(3):
                for hh in range(NQ):
                    src = prob0[:, hh, :] if j == 0 else prob1[:, hh, (j - 1) * P:j * P]
                    ins = pe.transpose(bank[t_bank[j][hh // 4]][:, (hh % 4) * P:(hh % 4 + 1) * P], src, ident)
                ins.then_inc(pT_done, 1)
            pe.wait_ge(sgu_ready, 1)
            for c in range(4):
                for t in range(TT):
                    ins = pe.transpose(bank[5 + c // 2][:, (c % 2) * T + t * P:(c % 2) * T + (t + 1) * P],
                                       u_nat[:, t, c * P:(c + 1) * P], ident)
            ins.then_inc(sguT_done, 1)
            pe.wait_ge(pT_ready, 3)
            for hh in range(NQ):
                kv = hh // 4 * HD
                half = hh % 2 * HD
                for t in range(TT):
                    to = bank[3 + hh // 4][half:half + HD, (hh // 2 % 2) * T + t * P:(hh // 2 % 2) * T + (t + 1) * P]
                    fresh = hh // 2 % 2 == 0 and t == 0
                    if t == 0:
                        ins = pe.matmul(to, v_nat[:, 0, kv:kv + HD], pT[:, 0, hh, :], start=fresh, stop=True, skip_group_check=True)
                    else:
                        pe.matmul(to, v_nat[:, 0, kv:kv + HD], pT[:, 1, hh, :], start=False, stop=False, skip_group_check=True)
                        ins = pe.matmul(to, v_nat[:, 1, kv:kv + HD], pT[:, 2, hh, :], start=False, stop=True, skip_group_check=True)
            ins.then_inc(attn_done, 1)
            pe.wait_ge(attn_ready, 2)
            pe.wait_ge(sguT_ready, 2)
            pe.wait_ge(w_out_in, 4 * 16)
            mix_bank = [[0, 1], [2, 7]]
            for t in range(TT):
                for n in range(2):
                    for k in range(KD):
                        ins = pe.matmul(bank[mix_bank[t][n]][:, :], mixT[:, k, t * P:(t + 1) * P], w_out[:, k, n * BANK:(n + 1) * BANK],
                                        start=k == 0, stop=k == KD - 1)
                    ins.then_inc(mix_done, 1)
            for t in range(TT):
                pe.wait_ge(h_ready, t + 1)
                for k in range(KD):
                    ins = pe.transpose(bank[3 + 2 * t + k // 4][:, (k % 4) * P:(k % 4 + 1) * P], h[:, t, k * P:(k + 1) * P], ident)
                ins.then_inc(hT_done, 1)
            pe.wait_ge(router_in, 16)
            pe.wait_ge(hT_ready, 4)
            for t in range(TT):
                for k in range(KD):
                    ins = pe.matmul(bank[7][:, t * NE:(t + 1) * NE], hT[:, k, t * P:(t + 1) * P], w_router[:, k, :],
                                    start=k == 0, stop=k == KD - 1, skip_group_check=True)
            ins.then_inc(router_done, 1)
            pe.wait_ge(chosen_ready, 1)
            m0, m1 = chosen[:, 0, :], chosen[:, 1, :]
            pe.matmul(bank[3][:, 0:NE], const("upto"), m0, start=True, stop=True, skip_group_check=True)
            pe.matmul(bank[3][:, NE:2 * NE], const("ones"), m0, start=False, stop=False, skip_group_check=True)
            pe.matmul(bank[3][:, NE:2 * NE], const("upto"), m1, start=False, stop=True, skip_group_check=True).then_inc(router_done, 1)
            pe.matmul(bank[4][0:1, 0:NE], const("ones")[:, 0:1], m0, start=True, stop=False)
            pe.matmul(bank[4][0:1, 0:NE], const("ones")[:, 0:1], m1, start=False, stop=True).then_inc(router_done, 1)
            pe.wait_ge(chosen_ready, 2)
            for t in range(TT):
                ins = pe.transpose(bank[5][0:NE, t * P:(t + 1) * P], gate_of[:, t, 0:NE], ident)
            ins.then_inc(router_done, 1)
            pe.wait_ge(gateT_ready, 1)
            pe.wait_ge(ln_rows_in, 32)
            pe.wait_ge(iter_ready, 1)
            for t in range(TT):
                for n in range(2):
                    pe.matmul(bank[2 * t + n][:, :], gateT[:, t * P:(t + 1) * P], b_down[:, n * BANK:(n + 1) * BANK],
                              start=True, stop=False, skip_group_check=True)

            gate_bank, up_bank, x_bank, y_bank = bank[4], bank[5], bank[6], bank[7]

            def gather():
                for k in range(KD):
                    for n, (t, part) in enumerate((t, part) for t in range(TT) for part in range(3)):
                        ins = pe.matmul(x_bank[:, k * CAP:(k + 1) * CAP], h_part[:, part, t, k * P:(k + 1) * P], place[:, t, :],
                                        start=n == 0, stop=n == 5, skip_group_check=True)
                ins.then_inc(gather_done, 1)

            def scatter(stop):
                for t in range(TT):
                    for n in range(2):
                        lo = n * CAP
                        ins = pe.matmul(bank[2 * t + n][:, :], place_T[lo:lo + CAP, t * P:(t + 1) * P], yy[lo:lo + CAP, :],
                                        start=False, stop=stop, skip_group_check=True)
                return ins

            pe.wait_ge(split_ready, 3)
            pe.wait_ge(place_ready, 1)
            gather()
            n = pe.value_load(n_iter[0:1, 0:1], min_val=NE, max_val=NE * PASSES)
            with pe.Fori(0, n) as it:
                now, ahead, landed = pe.snap(it + 1), pe.snap(it + 2), pe.snap(it * 16 + 16)
                pe.wait_ge(x_e_ready, now)
                pe.wait_ge(place_T_ready, now)
                pe.wait_ge(bias_in, landed)
                for b, to in enumerate((gate_bank, up_bank)):
                    for n2 in range(2):
                        ins = pe.matmul(to[n2 * CAP:(n2 + 1) * CAP, :], const("ones")[0:1, 0:CAP],
                                        bias_row[:, b * D + n2 * BANK:b * D + (n2 + 1) * BANK], start=True, stop=False)
                ins.then_inc(bias_free, 1)
                for j in range(8):
                    to = (gate_bank, up_bank)[j % 2]
                    pe.wait_ge(slot_in[j], landed)
                    for kk in range(2):
                        for n2 in range(2):
                            ins = pe.matmul(to[n2 * CAP:(n2 + 1) * CAP, :], x_e[:, j // 2 * 2 + kk, :],
                                            slot_view(j)[:, kk, n2 * BANK:(n2 + 1) * BANK],
                                            start=False, stop=j >= 6 and kk == 1)
                    ins.then_inc(slots_used, 1)
                pe.wait_ge(place_ready, ahead)
                gather()
                pe.wait_ge(y_ready, now)
                scatter(False)
                pe.wait_ge(hid_ready, now)
                for j in range(4):
                    ins = pe.transpose(gate_bank[:, j * P:(j + 1) * P], hid[:, j * P:(j + 1) * P], ident)
                ins.then_inc(hidT_done, 1)
                pe.wait_ge(place_g_ready, now)
                for t in range(TT):
                    ins = pe.transpose(up_bank[:, t * P:(t + 1) * P], place_g[:, t, :], ident)
                ins.then_inc(place_T_done, 1)
                pe.wait_ge(hidT_ready, now)
                for j in range(4):
                    pe.wait_ge(slot_in[8 + j], landed)
                    for kk in range(2):
                        k = 2 * j + kk
                        for n2 in range(2):
                            ins = pe.matmul(y_bank[n2 * CAP:(n2 + 1) * CAP, :], hidT[:, k % 4, k // 4 * CAP:(k // 4 + 1) * CAP],
                                            slot_view(8 + j)[:, kk, n2 * BANK:(n2 + 1) * BANK], start=k == 0, stop=k == 7)
                    ins.then_inc(slots_used, 1)
            pe.wait_ge(y_ready, pe.snap(n + 1))
            pe.wait_ge(place_T_ready, pe.snap(n + 1))
            scatter(True).then_inc(acc_done, 1)

            def transpose_hn(src, before):
                for t in range(TT):
                    pe.wait_ge(hn_ready, before + t + 1)
                    for k in range(KD):
                        ins = pe.transpose(bank[4 + 2 * t + k // 4][:, (k % 4) * P:(k % 4 + 1) * P], src[:, t, k * P:(k + 1) * P], ident)
                    ins.then_inc(hT_done, 1)

            transpose_hn(hn, 0)
            pe.wait_ge(x_rest, 4)

            def three_passes(to, left, right, start, stop):
                pe.matmul(to, left[0], right[0], start=start, stop=False, skip_group_check=True)
                pe.matmul(to, left[0], right[1], start=False, stop=False, skip_group_check=True)
                return pe.matmul(to, left[1], right[0], start=False, stop=stop, skip_group_check=True)

            def halves(f):
                for half in range(2):
                    n2 = 2 * FILLS.index(f) + half
                    pe.wait_ge(half_rest, n2 + 1)
                    yield half, [a.rearrange("p (k n) -> p k n", k=KD // 2) for a in (upper_of(n2), rest_of(n2))]

            def project_T(f, pair):
                for half, w in halves(f):
                    for i in range(w[0].shape[2] // P):
                        for k in range(KD // 2):
                            kx = half * (KD // 2) + k
                            ins = three_passes(bank[2 * pair + i // 2][:, (i % 2) * T:(i % 2 + 1) * T], [a[:, k, i * P:(i + 1) * P] for a in w],
                                               (hnT_hi[kx], hnT_rest[:, kx, :]), kx == 0 and i % 2 == 0, kx == KD - 1)
                    ins.then_inc(half_used, 1)

            def project(f, pair):
                for half, w in halves(f):
                    for t in range(TT):
                        for k in range(KD // 2):
                            kx = half * (KD // 2) + k
                            ins = three_passes(bank[2 * pair + t][:, :], [a[:, t * P:(t + 1) * P] for a in (hnT_hi[kx], hnT_rest[:, kx, :])],
                                               [a[:, k, :] for a in w], kx == 0, kx == KD - 1)
                    ins.then_inc(half_used, 1)

            for n2, f in enumerate(("lora", "r", "k", "v")):
                project_T(f, (n2 + 3) % 4)
            pe.wait_ge(small2_in, 112)
            pe.wait_ge(lora_ready, 1)
            for i in range(NP2):
                ins = pe.matmul(bank[6 + i // 2][:, (i % 2) * T:(i % 2 + 1) * T], w_lora_up[0:HD, i * P:(i + 1) * P], lora[0:HD, 0, :],
                                start=True, stop=True, skip_group_check=True)
            ins.then_inc(lora_up_done, 1)
            pe.wait_ge(z_raw, 4)
            for i in range(NP2):
                ins = pe.matmul(bank[i // 2][:, (i % 2) * T:(i % 2 + 1) * T], w_lora_up[HD:P, i * P:(i + 1) * P], lora[HD:P, 0, :],
                                start=True, stop=True, skip_group_check=True)
            ins.then_inc(lora_up_done, 1)
            pe.wait_ge(z_raw, 6)
            pe.wait_ge(lora_ready, 3)
            for t in range(TT):
                pe.matmul(bank[2 + t][:, :], lora[:, 1, t * P:(t + 1) * P], w_gate_up[:, 0, :], start=True, stop=False)
                ins = pe.matmul(bank[2 + t][:, :], lora[0:CH, 2, t * P:(t + 1) * P], w_gate_up[0:CH, 1, :], start=False, stop=True)
            ins.then_inc(lora_up_done, 1)
            pe.wait_ge(z_raw, 8)
            project("q2", 2)
            pe.wait_ge(kk2_ready, 1)
            pe.wait_ge(lora_up_ready, 4)
            for b in range(2):
                ins = pe.matmul(bank[6 + b][:, :].rearrange("p (i t) -> p i t", i=2), const2("head_ones"), kk2[:, 2 * b:2 * b + 2, :],
                                start=True, stop=True)
            ins.then_inc(nrm_done, 1)
            pe.wait_ge(lora_up_ready, 8)
            project("k2", 0)
            pe.wait_ge(lora_up_ready, 10)
            project("v2", 1)
            pe.wait_ge(qkv2_raw, 2)
            project("gate_a0", 2)
            pe.wait_ge(rk_ready, 1)
            pe.wait_ge(nrm_ready, 2)
            for t in range(TT):
                for i in range(NP2):
                    ins = pe.matmul(bank[6][:, t * NQ + 2 * i:t * NQ + 2 * i + 2], kk2[:, i, t * P:(t + 1) * P], const2("head_col"),
                                    start=t == 0 and i == 0, stop=True, skip_group_check=True)
            ins.then_inc(bonus_done, 1)
            pe.wait_ge(hats_ready, 1)
            pe.wait_ge(qkv2_raw, 6)
            for y in (1, 2, 0, 3):
                if y == 2:
                    pe.wait_ge(gate_ready, 2)
                if y == 3:
                    pe.wait_ge(bonus_ready, 1)
                for t in range(TT):
                    for i in range(NP2):
                        src = (ar[:, i, 0, :], b_hat[:, i, :], k_hat[:, i, :], zv[:, i, :])[y][:, t * P:(t + 1) * P]
                        ins = pe.transpose(bank[2 * y + t][:, i * P:(i + 1) * P], src, ident)
                    ins.then_inc(nat_done, 1)

            pe.wait_ge(nat_ready, 8)
            project("gate_b0", 1)
            pe.wait_ge(qk2_ready, 1)
            for w in range(2):
                for i in range(NP2):
                    for t in range(TT):
                        ins = pe.transpose(bank[4 * w + i // 2][:, (i % 2) * T + t * P:(i % 2) * T + (t + 1) * P],
                                           qk2[:, w, t, i * P:(i + 1) * P], ident)
            ins.then_inc(qkT2_done, 1)
            project("gate_a1", 3)
            pe.wait_ge(qkT2_ready, 4)
            for i in range(NP2):
                for half in range(2):
                    lo = half * HD
                    ins = pe.matmul(bank[4 * half + i // 2][:, (i % 2) * T:(i % 2 + 1) * T], qkT2[lo:lo + HD, 0, i, P:T],
                                    qkT2[lo:lo + HD, 1, i, :], start=i % 2 == 0, stop=True, skip_group_check=True)
            ins.then_inc(scores_done, 1)
            pe.wait_ge(gate_ready, 4)
            for i in range(NP2):
                for half in range(2):
                    lo = half * HD
                    ins = pe.matmul(bank[2 + half][:, i * P:(i + 1) * P], qkT2[lo:lo + HD, 0, i, 0:P], qkT2[lo:lo + HD, 1, i, 0:P],
                                    start=i == 0, stop=True, skip_group_check=True)
            ins.then_inc(scores_done, 1)
            pe.wait_ge(gate_ready, 6)
            project("gate_b1", 3)
            pe.wait_ge(prob_ready, 4)
            for j in range(3):
                for m in range(NQ):
                    src = prob2_0[:, m, :] if j == 0 else prob2_1[:, m, (j - 1) * P:j * P]
                    ins = pe.transpose(bank[2 * j + m // 4][:, (m % 4) * P:(m % 4 + 1) * P], src, ident)
                ins.then_inc(pT_done, 1)
            pe.wait_ge(pT_ready, 6)
            pe.wait_ge(gate_ready, 8)
            for m in range(NQ):
                half, i = m // 4, m % 4
                hh = 2 * i + half
                for t in range(TT):
                    to = bank[6 + i // 2][half * HD:(half + 1) * HD, (i % 2) * T + t * P:(i % 2) * T + (t + 1) * P]
                    for j in ([0] if t == 0 else [1, 2]):
                        ins = pe.matmul(to, v2[:, max(j - 1, 0), hh * HD:(hh + 1) * HD], pT2[:, j, m, :],
                                        start=i % 2 == 0 and j == 0, stop=j != 1, skip_group_check=True)
            ins.then_inc(attn_done, 1)

            def head(b, m):
                half, i = m // 2, 2 * b + m % 2
                return 2 * i + half, i, half * HD

            pe.wait_ge(attn_ready, 4)
            for tt in range(TT):
                cols = slice(tt * P, (tt + 1) * P)
                if tt > 0:
                    pe.wait_ge(y2_ready, 2 * tt)
                    pe.wait_ge(st_ready, 4 * tt)
                for b in range(2):
                    B = bank[4 * b:4 * b + 4]
                    for m in range(4):
                        hh, i, lo = head(b, m)
                        pe.matmul(B[2 * (m // 2)][:, (m % 2) * P:(m % 2 + 1) * P], ar[lo:lo + HD, i, 0, cols], b_hat[lo:lo + HD, i, cols],
                                  start=m % 2 == 0, stop=True, skip_group_check=True)
                        ins = pe.matmul(B[2 * (m // 2) + 1][:, (m % 2) * T:(m % 2 + 1) * T].rearrange("p (w t) -> p w t", w=2),
                                        b_hat[lo:lo + HD, i, cols], ar[lo:lo + HD, i, :, cols],
                                        start=m % 2 == 0, stop=True, skip_group_check=True)
                    ins.then_inc(rec_done, 1)
                for b in range(2):
                    B = bank[4 * b:4 * b + 4]
                    pe.wait_ge(rec_ready, count(vector_steps, "Mb", tt, b))
                    for m in range(4):
                        hh, i, lo = head(b, m)
                        ins = pe.matmul(B[2 * (m // 2)][:, (m % 2) * T:(m % 2 + 1) * T].rearrange("p (w t) -> p w t", w=2),
                                        k_hat[lo:lo + HD, i, cols], ar[lo:lo + HD, i, :, cols],
                                        start=m % 2 == 0, stop=True, skip_group_check=True)
                    ins.then_inc(rec_done, 1)
                for b in range(2):
                    B, Z = bank[4 * b:4 * b + 4], batch[b]
                    pe.wait_ge(rec_ready, count(vector_steps, "MA", tt, b))
                    for m in range(4):
                        c = slice(m * P, (m + 1) * P)
                        pe.matmul(B[1][:, c], Z["MA"][:, m, 0, :], Z["Mb"][:, m, :], start=m == 0, stop=True, skip_group_check=True)
                        ins = pe.matmul(B[3][:, c], Z["Mb"][:, m, :], Z["MA"][:, m, 0, :], start=m == 0, stop=True, skip_group_check=True)
                    ins.then_inc(rec_done, 1)
                for b in range(2):
                    B, Z = bank[4 * b:4 * b + 4], batch[b]
                    pe.wait_ge(rec_ready, count(vector_steps, "NK", tt, b))
                    for m in range(4):
                        hh, i, lo = head(b, m)
                        ins = pe.matmul(B[2][:, m * HD:(m + 1) * HD], Z["NK"][:, m, 0, :], vn[:, tt, hh * HD:(hh + 1) * HD],
                                        start=m == 0, stop=True, skip_group_check=True)
                    ins.then_inc(rec_done, 1)
                for b in range(2):
                    B, Z = bank[4 * b:4 * b + 4], batch[b]
                    pe.wait_ge(rec_copied, count(scalar_steps, "P2", tt, b))
                    pe.wait_ge(one_added, 2 * tt + b + 1)
                    for m in range(4):
                        pe.matmul(B[m // 2][:, (m % 2) * T:(m % 2 + 1) * T].rearrange("p (w t) -> p w t", w=2), Z["P2"][:, m, :], Z["PU"][:, m],
                                  start=m % 2 == 0, stop=True, skip_group_check=True)
                        ins = pe.matmul(B[3][:, m * P:(m + 1) * P], Z["PU"][:, m, 0, :], Z["P2"][:, m, :],
                                        start=m == 0, stop=True, skip_group_check=True)
                    ins.then_inc(rec_done, 1)
                for b in range(2):
                    B, Z = bank[4 * b:4 * b + 4], batch[b]
                    pe.wait_ge(rec_copied, count(scalar_steps, "P4", tt, b))
                    pe.wait_ge(rec_ready, count(vector_steps, "U2", tt, b))
                    pe.wait_ge(rec_copied, count(scalar_steps, "x0", tt, b))
                    for m in range(4):
                        c = slice(m * P, (m + 1) * P)
                        pe.matmul(B[2][:, c], Z["MA"][:, m, 0, :], Z["Mb"][:, m, :], start=m == 0, stop=True, skip_group_check=True)
                        ins = pe.matmul(B[0][:, c], Z["Mb"][:, m, :], Z["PU"][:, m, 1, :], start=m == 0, stop=True, skip_group_check=True)
                    ins.then_inc(rec_done, 1)
                for b in range(2):
                    B, Z = bank[4 * b:4 * b + 4], batch[b]
                    pe.wait_ge(rec_copied, count(scalar_steps, "P8", tt, b))
                    pe.wait_ge(rec_ready, count(vector_steps, "U4", tt, b))
                    for m in range(4):
                        ins = pe.matmul(B[1][:, m * P:(m + 1) * P], Z["P2"][:, m, :], Z["PU"][:, m, 1, :],
                                        start=m == 0, stop=True, skip_group_check=True)
                    ins.then_inc(rec_done, 1)
                for b in range(2):
                    B, Z = bank[4 * b:4 * b + 4], batch[b]
                    pe.wait_ge(rec_ready, count(vector_steps, "U8", tt, b))
                    for m in range(4):
                        ins = pe.matmul(B[3][:, m * P:(m + 1) * P], Z["PU"][:, m, 1, :], x0[:, tt, head(b, m)[0], :],
                                        start=m == 0, stop=True, skip_group_check=True)
                    ins.then_inc(rec_done, 1)
                for b in range(2):
                    B, Z = bank[4 * b:4 * b + 4], batch[b]
                    pe.wait_ge(rec_copied, count(scalar_steps, "X1", tt, b))
                    for m in range(4):
                        ins = pe.matmul(B[2][:, m * P:(m + 1) * P], Z["MoT"][:, m, :], Z["X1"][:, m, :],
                                        start=m == 0, stop=True, skip_group_check=True)
                    ins.then_inc(rec_done, 1)
                for b in range(2):
                    B, Z = bank[4 * b:4 * b + 4], batch[b]
                    pe.wait_ge(rec_copied, count(scalar_steps, "X2", tt, b))
                    for m in range(4):
                        ins = pe.matmul(B[0][:, m * P:(m + 1) * P], Z["PU"][:, m, 1, :], Z["Mb"][:, m, :],
                                        start=m == 0, stop=True, skip_group_check=True)
                    ins.then_inc(rec_done, 1)
                for b in range(2):
                    B, Z = bank[4 * b:4 * b + 4], batch[b]
                    pe.wait_ge(rec_ready, count(vector_steps, "X3", tt, b))
                    for m in range(4):
                        hh, i, lo = head(b, m)
                        ins = pe.matmul(B[1][lo:lo + HD, (m % 2) * P:(m % 2 + 1) * P], Z["X1"][:, m, 0:HD], Z["MA"][:, m, 1, :],
                                        start=m % 2 == 0, stop=True, skip_group_check=True)
                    ins.then_inc(rec_done, 1)
                for b in range(2):
                    B, Z = bank[4 * b:4 * b + 4], batch[b]
                    pe.wait_ge(rec_ready, count(vector_steps, "rT", tt, b))
                    for c in range(4):
                        rows = slice(c * CH, (c + 1) * CH)
                        for m in range(4):
                            hh, i, lo = head(b, m)
                            hc = slice(hh * HD, (hh + 1) * HD)
                            o = (m % 2) * HD
                            pe.matmul(B[c][lo:lo + HD, o:o + HD], Z["X1"][rows, m, 0:HD], bn[rows, tt, hc],
                                      start=m % 2 == 0, stop=True, skip_group_check=True)
                            pe.matmul(B[c][lo:lo + HD, P + o:P + o + HD], bn[rows, tt, hc], Z["X1"][rows, m, HD:P],
                                      start=False, stop=False, skip_group_check=True)
                            ins = pe.matmul(B[c][lo:lo + HD, P + o:P + o + HD], kn[rows, tt, hc], vn[rows, tt, hc],
                                            start=False, stop=True, skip_group_check=True)
                    ins.then_inc(rec_done, 1)
                pe.wait_ge(rec_ready, count(vector_steps, "FH", tt, 1))
                for b in range(2):
                    Z = batch[b]
                    for m in range(4):
                        hh, i, lo = head(b, m)
                        y_to = bank[2 + 4 * (m // 2)][:, i * HD:(i + 1) * HD]
                        pe.matmul(y_to, Z["MA"][:, m, 1, :], Z["X1"][:, m, HD:P], start=b == 0 and m % 2 == 0, stop=False, skip_group_check=True)
                        pe.matmul(y_to, Z["NK"][:, m, 1, :], vn[:, tt, hh * HD:(hh + 1) * HD], start=False, stop=False, skip_group_check=True)
                for c in range(4):
                    rows = slice(c * CH, (c + 1) * CH)
                    number = 4 * tt + c
                    if number == 0:
                        continue
                    pe.wait_ge(st_ready, number)
                    for i in range(NP2):
                        for half in range(2):
                            lo = half * HD
                            ins = pe.matmul(bank[2 + 4 * half][rows, i * HD:(i + 1) * HD], rT[lo:lo + HD, i, rows], state[lo:lo + HD, i, :],
                                            start=False, stop=True, skip_group_check=True)
                    if c == 3:
                        ins.then_inc(y2_done, 1)
                    if number < 2 * 4 - 1:
                        for i in range(NP2):
                            for half in range(2):
                                lo = half * HD
                                ins = pe.matmul(bank[0][lo:lo + HD, i * HD:(i + 1) * HD], ft[lo:lo + HD, c, i, :], state[lo:lo + HD, i, :],
                                                start=i == 0, stop=True, skip_group_check=True)
                        ins.then_inc(st_done, 1)
            def branch(f, yT, to):
                pe.wait_ge(tail_in[f], 16)
                for n2 in range(2):
                    for t in range(TT):
                        for k in range(NP2):
                            ins = pe.matmul(bank[to[n2] + t][:, :], yT[:, k, t * P:(t + 1) * P], tail[f][:, k, n2 * BANK:(n2 + 1) * BANK],
                                            start=k == 0, stop=k == NP2 - 1)
                    ins.then_inc(branch_done, 1)

            pe.wait_ge(st_ready, 7)
            branch("branch_b", ybT, (0, 4))
            pe.wait_ge(ya_ready, 1)
            for i in range(NP2):
                for t in range(TT):
                    ins = pe.transpose(bank[2 + i // 2][:, (i % 2) * T + t * P:(i % 2) * T + (t + 1) * P], y2[:, t, i * P:(i + 1) * P], ident)
            ins.then_inc(sguT_done, 1)
            pe.wait_ge(sguT_ready, 4)
            branch("branch_a", yaT, (6, 2))
            pe.wait_ge(mm_ready, 2)
            for t in range(TT):
                for k in range(KD):
                    ins = pe.transpose(bank[4 + 2 * t + k // 4][:, (k % 4) * P:(k % 4 + 1) * P], mm[:, t, k * P:(k + 1) * P], ident)
                ins.then_inc(hT_done, 1)
            pe.wait_ge(hT_ready, 12)
            pe.wait_ge(tail_in["out"], 32)
            for t in range(TT):
                for n2 in range(2):
                    for k in range(KD):
                        ins = pe.matmul(bank[2 * t + n2][:, :], mT[:, k, t * P:(t + 1) * P],
                                        tail["out0" if k < 4 else "out1"][:, k % 4, n2 * BANK:(n2 + 1) * BANK], start=k == 0, stop=k == KD - 1)
                    ins.then_inc(u_done, 1)
            transpose_hn(hn2, TT)
            pe.wait_ge(x_rest, 8)
            for t in range(TT):
                for n2 in range(2):
                    pe.matmul(bank[2 * t + n2][:, :], ident, x1[:, t, n2 * BANK:(n2 + 1) * BANK], start=True, stop=False, skip_group_check=True)

            def ffn_up(i, use):
                pe.wait_ge(up_rest[i], use)
                w = [a[i][:, 0:2 * D].rearrange("p (c k n) -> p c k n", c=2, k=KD) for a in (ff_hi, ff_rest)]
                for c in range(2):
                    for k in range(KD):
                        ins = three_passes(bank[4 + i][:, c * T:(c + 1) * T], [a[:, c, k, :] for a in w], (hnT_hi2[k], hnT_rest[:, k, :]),
                                           c == 0 and k == 0, k == KD - 1)
                ins.then_inc(ffu_used[i], 1)

            def ffn_down(i, use, last=False):
                pe.wait_ge(down_rest[i], use)
                pe.wait_ge(hid2_ready[i], use)
                w = [a[i][:, 2 * D:FF] for a in (ff_hi, ff_rest)]
                for t in range(TT):
                    for n2 in range(2):
                        ins = three_passes(bank[2 * t + n2][:, :], [a[:, i, t * P:(t + 1) * P] for a in (hid2_hi, hid2_lo)],
                                           [a[:, n2 * BANK:(n2 + 1) * BANK] for a in w], False, last)
                ins.then_inc(ffn_done if last else ffd_used[i], 1)

            ffn_up(0, 1)
            with pe.Fori(0, FT_N // 2 - 1) as it:
                now, ahead = pe.snap(it + 1), pe.snap(it + 2)
                ffn_up(1, now)
                ffn_down(0, now)
                ffn_up(0, ahead)
                ffn_down(1, now)
            ffn_up(1, FT_N // 2)
            ffn_down(0, FT_N // 2)
            ffn_down(1, FT_N // 2, last=True)

        @block.scalar
        def _(act):
            act.dma_start(w_router, A["w_router"]).then_inc(router_in, 16)
            act.wait_ge(consts_in, 32)
            act.wait_ge(proj_done, 1)
            for i in range(4):
                act.activation(qkT[:, i, :], bank[i // 2][:, (i % 2) * T:(i % 2 + 1) * T], ACT.Identity,
                               bias=colv("b_in_qk")[:, i:i + 1]).then_inc(qk_ready, 1)
            for i, a in enumerate((g_nat, u_nat)):
                act.wait_ge(ug_biased, 2 * (2 - i))
                act.activation(a, a, ACT.Gelu_apprx_tanh).then_inc(ug_gelu, 1)
            act.wait_ge(g_var, 1)
            act.activation(g_std, g_sum2, ACT.Sqrt, bias=eps1, scale=1.0 / GD).then_inc(g_stds, 1)
            act.wait_ge(neg_max, 1)
            for t, pr in enumerate((prob1, prob0)):
                act.wait_ge(neg_max, t + 1)
                for hh in range(NQ):
                    act.activation(pr[:, hh, :], pr[:, hh, :], ACT.Exp, bias=nmax[:, t * NQ + hh:t * NQ + hh + 1],
                                   accum_out=den[:, t * NQ + hh:t * NQ + hh + 1]).then_inc(exp_done, 1)
                act.activation(sink_e[:, t * NQ:(t + 1) * NQ], sink_e[:, t * NQ:(t + 1) * NQ], ACT.Exp).then_inc(exp_done, 1)
            t_bank = [[3, 4], [0, 1], [2, 7]]
            for j in range(3):
                act.wait_ge(pT_done, j + 1)
                for b in range(2):
                    ins = act.copy(pT[:, j, 4 * b:4 * b + 4, :], bank[t_bank[j][b]][:, :].rearrange("p (h t) -> p h t", h=4))
                ins.then_inc(pT_ready, 1)
            act.wait_ge(attn_done, 1)
            for b in range(2):
                act.copy(mixT[:, 2 * b:2 * b + 2, :], bank[3 + b][:, :].rearrange("p (k t) -> p k t", k=2)).then_inc(attn_ready, 1)
            for t in range(TT):
                act.wait_ge(var_ready, t + 1)
                act.activation(rstd[:, t:t + 1], mv[:, t, 1:2], ACT.Sqrt, bias=eps1).then_inc(std_ready, 1)
            for t in range(TT):
                act.wait_ge(hT_done, t + 1)
                for b in range(2):
                    act.copy(hT[:, 4 * b:4 * b + 4, t * P:(t + 1) * P],
                             bank[3 + 2 * t + b][:, :].rearrange("p (k t) -> p k t", k=4)).then_inc(hT_ready, 1)
            act.copy(h_part[:, 0], h).then_inc(split_ready, 1)
            act.wait_ge(top_ready, 2)
            for t in range(TT):
                act.activation(gates4[:, t, :], gates4[:, t, :], ACT.Exp, bias=ntop[:, t:t + 1],
                               accum_out=gsum[:, t:t + 1]).then_inc(top_exp, 1)
            act.wait_ge(router_done, 4)
            act.copy(gateT, bank[5][0:NE, 0:T]).then_inc(gateT_ready, 1)
            act.wait_ge(rest_ready, 1)
            act.copy(h_part[:, 1], resid).then_inc(split_ready, 1)
            act.wait_ge(gather_done, 1)
            act.copy(x_e, bank[6][:, :].rearrange("p (k s) -> p k s", k=KD)).then_inc(x_e_ready, 1)
            act.wait_ge(iter_ready, 1)
            n = act.value_load(n_iter[0:1, 0:1], min_val=NE, max_val=NE * PASSES)
            with act.Fori(0, n) as it:
                now, ahead = act.snap(it + 1), act.snap(it + 2)
                act.wait_ge(gt_ready, now)
                act.activation(sg, gt, ACT.Sigmoid, scale=SWIGLU_ALPHA).then_inc(sg_ready, 1)
                act.wait_ge(gather_done, ahead)
                act.copy(x_e, bank[6][:, :].rearrange("p (k s) -> p k s", k=KD)).then_inc(x_e_ready, 1)
                act.wait_ge(hidT_done, now)
                act.copy(hidT, bank[4][:, :].rearrange("p (j c) -> p j c", j=4)).then_inc(hidT_ready, 1)
                act.wait_ge(slots_used, act.snap(it * SLOTS + SLOTS))
                act.copy(yy, bank[7][:, :]).then_inc(y_ready, 1)
            for n2 in range(2):
                act.wait_ge(half_in[n2], 16)
                act.copy(upper_of(n2), half_view(n2)).then_inc(half_upper, 1)
            for t in range(TT):
                act.wait_ge(var_ready, TT + t + 1)
                act.activation(rstd[:, t:t + 1], mv[:, t, 1:2], ACT.Sqrt, bias=eps1).then_inc(std_ready, 1)

            def upper(f):
                for half in range(2):
                    n2 = 2 * FILLS.index(f) + half
                    act.wait_ge(half_in[n2 % 4], 16 * (n2 // 4 + 1))
                    act.copy(upper_of(n2), half_view(n2)).then_inc(half_upper, 1)

            def upper_x(to, before):
                for t in range(TT):
                    cols = slice(t * P, (t + 1) * P)
                    for b in range(2):
                        act.wait_ge(hT_ready, before + 2 * t + b + 1)
                        for k in range(4 * b, 4 * b + 4):
                            ins = act.copy(to[k][:, cols], hnT[:, k, cols])
                        ins.then_inc(x_upper, 1)

            def root_mean_square(before, scratch):
                act.wait_ge(x1_ready, before + TT)
                for t in range(TT):
                    act.activation(scratch[:, t, :], x1[:, t, :], ACT.Square, accum_out=ss[:, t:t + 1]).then_inc(sq_done, 1)
                act.wait_ge(sq_done, before + TT)
                act.activation(rms, ss, ACT.Sqrt, bias=eps2, scale=1.0 / D).then_inc(rms_std, 1)

            root_mean_square(0, hn)
            upper("r")
            upper_x(hnT_hi, 4)
            act.wait_ge(half_used, used_count("lora"))
            act.copy(lora[:, 0:2, :], bank[6][:, :].rearrange("p (i t) -> p i t", i=2)).then_inc(z_raw, 1)
            act.copy(lora[0:CH, 2, :], bank[7][0:CH, 0:T]).then_inc(z_raw, 1)
            upper("k")
            act.wait_ge(lora_mixed, 1)
            act.activation(lora[0:HD, 0, :], lora[0:HD, 0, :], ACT.Tanh).then_inc(lora_ready, 1)
            act.activation(lora[:, 1, :], lora[:, 1, :], ACT.Sigmoid).then_inc(lora_ready, 1)
            act.activation(lora[0:CH, 2, :], lora[0:CH, 2, :], ACT.Sigmoid).then_inc(lora_ready, 1)
            for n2, (f, z, after_next) in enumerate((("r", zr, "v"), ("k", zk, "q2"), ("v", zv, None))):
                act.wait_ge(half_used, used_count(f))
                for b in range(2):
                    act.copy(z[:, 2 * b:2 * b + 2, :], bank[2 * n2 + b][:, :].rearrange("p (i t) -> p i t", i=2)).then_inc(z_raw, 1)
                if after_next:
                    upper(after_next)
            act.wait_ge(lora_up_done, 1)
            for i in range(NP2):
                act.activation(sd[:, i, :], bank[6 + i // 2][:, (i % 2) * T:(i % 2 + 1) * T], ACT.Sigmoid,
                               bias=col2("decay_bias_2")[:, i:i + 1]).then_inc(lora_up_ready, 1)
            act.wait_ge(lora_up_done, 2)
            for i in range(NP2):
                act.activation(aa[:, i, :], bank[i // 2][:, (i % 2) * T:(i % 2 + 1) * T], ACT.Sigmoid,
                               bias=col2("aaa_bias_2")[:, i:i + 1]).then_inc(lora_up_ready, 1)
            act.wait_ge(lora_up_done, 3)
            for t in range(TT):
                act.copy(g_gate[:, t, :], bank[2 + t][:, :]).then_inc(lora_up_ready, 1)
            upper("k2")
            act.wait_ge(cs_ready, 1)
            act.activation(e_pos, cs, ACT.Exp, scale=-KAPPA).then_inc(exp3_ready, 1)
            act.activation(e_neg, cs, ACT.Exp, scale=KAPPA).then_inc(exp3_ready, 1)
            act.activation(e_before, sd, ACT.Exp, scale=-KAPPA).then_inc(exp3_ready, 1)
            act.wait_ge(nrm_done, 1)
            for b in range(2):
                act.activation(nrm[:, 2 * b:2 * b + 2, :], bank[6 + b][:, :].rearrange("p (i t) -> p i t", i=2), ACT.Sqrt).then_inc(nrm_ready, 1)
            for w, (f, pair, after_next) in enumerate((("q2", 2, "v2"), ("k2", 0, "gate_a0"))):
                act.wait_ge(half_used, used_count(f))
                for t in range(TT):
                    act.copy(qk2[:, w, t, :], bank[2 * pair + t][:, :]).then_inc(qkv2_raw, 1)
                upper(after_next)
            act.wait_ge(half_used, used_count("v2"))
            for t in range(TT):
                act.copy(v2[:, t, :], bank[2 + t][:, :]).then_inc(qkv2_raw, 1)
            upper("gate_b0")

            def gates(f, pair):
                act.wait_ge(half_used, used_count(f))
                for t in range(TT):
                    act.activation(gate[f][:, t, :], bank[2 * pair + t][:, :], ACT.Sigmoid).then_inc(gate_ready, 1)

            gates("gate_a0", 2)
            upper("gate_a1")
            for n2, to in enumerate((bn, kn)):
                for t in range(TT):
                    act.wait_ge(nat_done, 2 * n2 + t + 1)
                    act.copy(to[:, t, :], bank[2 * (n2 + 1) + t][:, :]).then_inc(nat_ready, 1)
            act.wait_ge(ang_ready, 1)
            act.activation(sinv, ang, ACT.Sin).then_inc(trig_ready, 1)
            act.activation(cosv, ang_n, ACT.Sin).then_inc(trig_ready, 1)
            act.wait_ge(ss_ready, 1)
            act.activation(rs_qk, ss_qk, ACT.Sqrt, bias=eps2, scale=1.0 / HD).then_inc(rs_ready, 1)
            gates("gate_b0", 1)
            upper("gate_b1")
            act.wait_ge(qkT2_done, 1)
            for w in range(2):
                for b in range(2):
                    act.copy(qkT2[:, w, 2 * b:2 * b + 2, :], bank[4 * w + b][:, :].rearrange("p (i t) -> p i t", i=2)).then_inc(qkT2_ready, 1)
            gates("gate_a1", 3)
            for t, pr in enumerate((prob2_1, prob2_0)):
                act.wait_ge(neg_max, 2 + t + 1)
                for m in range(NQ):
                    o = t * NQ + m
                    act.activation(pr[:, m, :], pr[:, m, :], ACT.Exp, bias=nmax2[:, o:o + 1], accum_out=den2[:, o:o + 1]).then_inc(exp_done, 1)
            gates("gate_b1", 3)
            for j in range(3):
                act.wait_ge(pT_done, 3 + j + 1)
                for b in range(2):
                    ins = act.copy(pT2[:, j, 4 * b:4 * b + 4, :], bank[2 * j + b][:, :].rearrange("p (h t) -> p h t", h=4))
                ins.then_inc(pT_ready, 1)
            act.wait_ge(attn_done, 2)
            for b in range(2):
                act.copy(ybT[:, 2 * b:2 * b + 2, :], bank[6 + b][:, :].rearrange("p (i t) -> p i t", i=2)).then_inc(attn_ready, 1)
            four = lambda a: a[:, :].rearrange("p (m t) -> p m t", m=4)
            for tt in range(TT):
                for b in range(2):
                    B, Z = bank[4 * b:4 * b + 4], batch[b]
                    act.wait_ge(rec_done, count(tensor_steps, "p2", tt, b))
                    act.copy(Z["P2"], four(B[1]))
                    act.copy(Z["PU"][:, :, 0, :], four(B[3])).then_inc(rec_copied, 1)
                for b in range(2):
                    B = bank[4 * b:4 * b + 4]
                    act.wait_ge(rec_done, count(tensor_steps, "nv", tt, b))
                    for half in range(2):
                        ins = act.copy(x0[:, tt, 4 * b + half:4 * b + half + 3:2, HD:P],
                                       B[2][:, half * P:(half + 1) * P].rearrange("p (m v) -> p m v", m=2))
                    ins.then_inc(rec_copied, 1)
                for b in range(2):
                    B, Z = bank[4 * b:4 * b + 4], batch[b]
                    act.wait_ge(rec_done, count(tensor_steps, "p4", tt, b))
                    act.copy(Z["Mb"], four(B[3])).then_inc(rec_copied, 1)
                for b in range(2):
                    B, Z = bank[4 * b:4 * b + 4], batch[b]
                    act.wait_ge(rec_done, count(tensor_steps, "p8", tt, b))
                    act.copy(Z["P2"], four(B[2])).then_inc(rec_copied, 1)
                for b in range(2):
                    B, Z = bank[4 * b:4 * b + 4], batch[b]
                    act.wait_ge(rec_done, count(tensor_steps, "x1", tt, b))
                    act.copy(Z["X1"], four(B[3])).then_inc(rec_copied, 1)
                for b in range(2):
                    B, Z = bank[4 * b:4 * b + 4], batch[b]
                    act.wait_ge(rec_done, count(tensor_steps, "x2", tt, b))
                    act.copy(Z["Mb"], four(B[2])).then_inc(rec_copied, 1)
                act.wait_ge(y2_done, tt + 1)
                for half in range(2):
                    act.copy(y2[:, tt, :].rearrange("p (i h v) -> p i h v", i=NP2, h=2)[:, :, half, :],
                             bank[2 + 4 * half][:, 0:T].rearrange("p (i v) -> p i v", i=NP2)).then_inc(y2_ready, 1)
            act.wait_ge(g_var, 2)
            act.activation(y_std, y_sum2, ACT.Sqrt, bias=eps3, scale=1.0 / HD).then_inc(g_stds, 1)
            act.wait_ge(sguT_done, 2)
            for b in range(2):
                act.copy(yaT[:, 2 * b:2 * b + 2, :], bank[2 + b][:, :].rearrange("p (i t) -> p i t", i=2)).then_inc(sguT_ready, 1)

            def ff_part(i, use, cols):
                act.wait_ge(ff_in[i], use * 32)
                act.copy(ff_hi[i][:, cols], ff_land[i][:, cols]).then_inc(ff_upper[i], 1)

            up_cols, down_cols = slice(0, 2 * D), slice(2 * D, FF)
            for t in range(TT):
                act.wait_ge(hT_done, 4 + t + 1)
                for b in range(2):
                    act.copy(mT[:, 4 * b:4 * b + 4, t * P:(t + 1) * P], bank[4 + 2 * t + b][:, :].rearrange("p (k t) -> p k t", k=4)).then_inc(hT_ready, 1)
            act.wait_ge(branch_done, 4)
            ff_part(0, 1, up_cols)
            ff_part(0, 1, down_cols)
            root_mean_square(TT, hn2)
            ff_part(1, 1, up_cols)
            ff_part(1, 1, down_cols)
            upper_x(hnT_hi2, 12)

            def gelu(i, use):
                act.wait_ge(conv_ready[i], use)
                act.activation(conv[:, i, :], conv[:, i, :], ACT.Gelu).then_inc(gelu_ready[i], 1)

            def next_part(i, now, cols):
                act.wait_ge(ffu_used[i] if cols is up_cols else ffd_used[i], now)
                ff_part(i, act.snap(now + 1), cols)

            with act.Fori(0, FT_N // 2 - 1) as it:
                now = act.snap(it + 1)
                gelu(0, now)
                next_part(0, now, up_cols)
                gelu(1, now)
                next_part(0, now, down_cols)
                next_part(1, now, up_cols)
                next_part(1, now, down_cols)
            for i in range(2):
                gelu(i, FT_N // 2)
            act.wait_ge(ffn_done, 1)
            for n2 in range(2):
                act.copy(out_sb[:, 0, n2 * BANK:(n2 + 1) * BANK], bank[n2][:, :]).then_inc(out_ready[0], 1)

        @block.vector
        def _(dve):
            step = [0]

            def link(ins):
                step[0] += 1
                ins.then_inc(dve_step, 1)
                dve.wait_ge(dve_step, step[0])

            def wide(a, n):
                return a.unsqueeze(len(a.shape)).broadcast_to(list(a.shape) + [n])

            link(dve.memset(eps1, LN_EPS))
            link(dve.memset(eps2, NORM_EPS))
            link(dve.memset(eps3, GN_EPS))
            dve.wait_ge(consts_in, 32)
            dve.wait_ge(wsT_in, 16)
            dve.tensor_tensor(wsT, wsT, const("upto").unsqueeze(1).broadcast_to([P, NG, P]), ALU.mult).then_inc(wsT_masked, 1)
            dve.wait_ge(mix_rows_in, 16)
            b_vug = rowv("b_in_vug")
            dve.wait_ge(proj_done, 3)
            dve.tensor_scalar(qkT[:, 4, :], bank[2][:, 0:T], colv("b_in_qk")[:, 4:5], None, ALU.add).then_inc(qk_ready, 1)
            for t in range(TT):
                dve.tensor_tensor(v_nat[:, t, :], bank[2][:, T + t * P:T + (t + 1) * P], b_vug[:, 0:P], ALU.add).then_inc(v_ready, 1)
            for c, a in enumerate((u_nat, g_nat)):
                for t in range(TT):
                    dve.wait_ge(proj_done, 4 + 2 * c + t)
                    dve.tensor_tensor(a[:, t, :], bank[3 + 2 * c + t][:, :], b_vug[:, P + c * G1:P + (c + 1) * G1],
                                      ALU.add).then_inc(ug_biased, 1)
            def masked(to, frm, masks):
                link(dve.scalar_tensor_tensor(out=to, in0=frm, scalar=HD ** -0.5, in1=masks, op0=ALU.mult, op1=ALU.add))

            def soft_max(t, pr):
                o = t * NQ
                link(dve.tensor_reduce(nmax[:, o:o + NQ], pr, AX.X, ALU.max))
                link(dve.tensor_tensor(nmax[:, o:o + NQ], nmax[:, o:o + NQ], rowv("sinks"), ALU.max))
                link(dve.tensor_tensor(sink_e[:, o:o + NQ], rowv("sinks"), nmax[:, o:o + NQ], ALU.subtract))
                dve.tensor_scalar(nmax[:, o:o + NQ], nmax[:, o:o + NQ], -1.0, None, ALU.mult).then_inc(neg_max, 1)

            dve.wait_ge(scores_done, 1)
            for b, nb in enumerate((0, 1, 2, 7)):
                for q in range(2):
                    o = q * T
                    hh = 2 * b + q
                    masked(prob1[:, hh, 0:P], bank[nb][:, o:o + P], const("before"))
                    masked(prob1[:, hh, P:T], bank[nb][:, o + P:o + T], const("causal"))
            soft_max(0, prob1)
            g3 = g_nat.rearrange("p t (g d) -> p (t g) d", d=GD)
            sq3 = sq.rearrange("p t (g d) -> p (t g) d", d=GD)
            dve.wait_ge(ug_gelu, 1)
            link(dve.tensor_reduce(g_sum, g3, AX.X, ALU.add))
            link(dve.tensor_scalar(g_sum, g_sum, 1.0 / GD, None, ALU.mult))
            link(dve.tensor_tensor(g3, g3, wide(g_sum, GD), ALU.subtract))
            link(dve.tensor_tensor(sq3, g3, g3, ALU.mult))
            dve.tensor_reduce(g_sum2, sq3, AX.X, ALU.add).then_inc(g_var, 1)
            dve.wait_ge(scores_done, 2)
            for half in range(2):
                masked(prob0[:, 4 * half:4 * half + 4, :], bank[3 + half][:, :].rearrange("p (h s) -> p h s", h=4),
                       const("causal").unsqueeze(1).broadcast_to([P, 4, P]))
            soft_max(1, prob0)
            dve.wait_ge(g_stds, 1)
            link(dve.reciprocal(g_sum2, g_std))
            link(dve.tensor_tensor(g3, g3, wide(g_sum2, GD), ALU.mult))
            link(dve.tensor_tensor(g_nat, g_nat, rowv("ln_v_g").unsqueeze(1).broadcast_to([P, TT, G1]), ALU.mult))
            dve.tensor_tensor(g_nat, g_nat, rowv("ln_v_b").unsqueeze(1).broadcast_to([P, TT, G1]), ALU.add).then_inc(g_normed, 1)
            for t, pr in enumerate((prob1, prob0)):
                o = t * NQ
                dve.wait_ge(exp_done, (t + 1) * (NQ + 1))
                link(dve.tensor_tensor(den[:, o:o + NQ], den[:, o:o + NQ], sink_e[:, o:o + NQ], ALU.add))
                link(dve.reciprocal(den[:, o:o + NQ], den[:, o:o + NQ]))
                dve.tensor_tensor(pr, pr, wide(den[:, o:o + NQ], pr.shape[2]), ALU.mult).then_inc(prob_ready, 1)
            dve.wait_ge(mixed_done, 1)
            dve.wait_ge(ug_gelu, 2)
            for b in range(2):
                m4 = bank[5 + b][:, :].rearrange("p (g c d) -> p c g d", g=4, c=TT)
                s4 = sq[:, :, b * T:(b + 1) * T].rearrange("p c (g d) -> p c g d", g=4)
                for c in range(TT):
                    link(dve.tensor_tensor(s4[:, c], m4[:, c], wide(colv("b_s")[:, 4 * b:4 * b + 4], GD), ALU.add))
            dve.tensor_tensor(u_nat, u_nat, sq, ALU.mult).then_inc(sgu_ready, 1)
            dve.wait_ge(sguT_done, 1)
            for b in range(2):
                dve.tensor_copy(mixT[:, 4 + 2 * b:6 + 2 * b, :], bank[5 + b][:, :].rearrange("p (k t) -> p k t", k=2)).then_inc(sguT_ready, 1)

            def layer_norm(t, src, frm_banks, add_row, g, b, done, before, to):
                for n in range(2):
                    cols = slice(n * BANK, (n + 1) * BANK)
                    if add_row is not None:
                        dve.wait_ge(mix_done, 2 * t + n + 1)
                        link(dve.tensor_tensor(ln_tmp[:, cols], frm_banks[n][:, :], add_row[:, cols], ALU.add))
                        link(dve.scalar_tensor_tensor(out=resid[:, t, cols], in0=src[:, t, cols], scalar=ALPHA1, in1=ln_tmp[:, cols],
                                                      op0=ALU.mult, op1=ALU.add))
                    else:
                        link(dve.scalar_tensor_tensor(out=resid[:, t, cols], in0=src[:, t, cols], scalar=ALPHA1, in1=frm_banks[n][:, :],
                                                      op0=ALU.mult, op1=ALU.add))
                    link(dve.bn_stats(stats[:, n, :], resid[:, t, cols]))
                dve.bn_aggr(mv[:, t, :], stats.rearrange("p n s -> p (n s)")).then_inc(var_ready, 1)
                dve.wait_ge(std_ready, before + t + 1)
                link(dve.reciprocal(rstd[:, t:t + 1], rstd[:, t:t + 1]))
                link(dve.tensor_scalar(resid[:, t, :], resid[:, t, :], mv[:, t, 0:1], rstd[:, t:t + 1], ALU.subtract, ALU.mult))
                link(dve.tensor_tensor(resid[:, t, :], resid[:, t, :], g, ALU.mult))
                dve.tensor_tensor(to[:, t, :], resid[:, t, :], b, ALU.add).then_inc(done, 1)

            dve.wait_ge(x_in, 16)
            dve.wait_ge(ln_rows_in, 32)
            mix_bank = [[0, 1], [2, 7]]
            for t in range(TT):
                layer_norm(t, x_nat, [bank[i] for i in mix_bank[t]], rowv("b_out"), rowv("ln1_g"), rowv("ln1_b"), h_ready,
                           0, h)
            dve.wait_ge(split_ready, 1)
            dve.tensor_tensor(resid, h, h_part[:, 0], ALU.subtract).then_inc(rest_ready, 1)
            dve.wait_ge(router_done, 1)
            for t in range(TT):
                link(dve.tensor_tensor(logits[:, t, :], bank[7][:, t * NE:(t + 1) * NE], rowv("b_router"), ALU.add))
                link(dve.max(top8[:, t, :], logits[:, t, :]))
                link(dve.max_index(top_i[:, t, :], top8[:, t, :], logits[:, t, :]))
                link(dve.tensor_copy(gates4[:, t, :], top8[:, t, 0:TOPK]))
                dve.tensor_scalar(ntop[:, t:t + 1], top8[:, t, 0:1], -1.0, None, ALU.mult).then_inc(top_ready, 1)
            link(dve.tensor_copy(top_f, top_i[:, :, 0:TOPK]))
            for t in range(TT):
                link(dve.tensor_tensor(chosen4[:, t], const("iota32").unsqueeze(1).broadcast_to([P, TOPK, NE]), wide(top_f[:, t, :], NE), ALU.is_equal))
                ins = dve.tensor_reduce(chosen[:, t, :], chosen4[:, t].rearrange("p k e -> p e k"), AX.X, ALU.add)
                if t == 0:
                    link(ins)
            ins.then_inc(chosen_ready, 1)
            dve.wait_ge(top_exp, 2)
            link(dve.reciprocal(gsum, gsum))
            for t in range(TT):
                link(dve.tensor_scalar(gates4[:, t, :], gates4[:, t, :], gsum[:, t:t + 1], None, ALU.mult))
                link(dve.tensor_tensor(chosen4[:, t], chosen4[:, t], wide(gates4[:, t, :], NE), ALU.mult))
                link(dve.memset(gate_of[:, t, NE * PASSES:COLS], 0.0))
                link(dve.memset(posm[:, t, NE * PASSES:COLS], -1.0))
                for b in range(PASSES):
                    ins = dve.tensor_reduce(gate_of[:, t, b * NE:(b + 1) * NE], chosen4[:, t].rearrange("p k e -> p e k"), AX.X, ALU.add)
                    if (t, b) != (TT - 1, PASSES - 1):
                        link(ins)
            ins.then_inc(chosen_ready, 1)
            dve.wait_ge(router_done, 2)
            for t in range(TT):
                link(dve.tensor_tensor(posm[:, t, 0:NE], bank[3][:, t * NE:(t + 1) * NE], chosen[:, t, :], ALU.mult))
                link(dve.tensor_scalar(posm[:, t, 0:NE], posm[:, t, 0:NE], -1.0, None, ALU.add))
                for b in range(1, PASSES):
                    link(dve.tensor_scalar(posm[:, t, b * NE:(b + 1) * NE], posm[:, t, 0:NE], float(-b * CAP), None, ALU.add))
            dve.wait_ge(router_done, 3)
            link(dve.tensor_reduce(n_iter_f[0:1, 0:1], bank[4][0:1, 0:NE], AX.X, ALU.max))
            link(dve.memset(n_iter_f[0:1, 1:2], float(NE)))
            for b in range(1, PASSES):
                link(dve.tensor_scalar(n_iter_f[0:1, 2:3], n_iter_f[0:1, 0:1], float(b * CAP), float(NE), ALU.is_gt, ALU.mult))
                link(dve.tensor_tensor(n_iter_f[0:1, 1:2], n_iter_f[0:1, 1:2], n_iter_f[0:1, 2:3], ALU.add))
            link(dve.tensor_scalar(n_iter_f[0:1, 2:3], n_iter_f[0:1, 1:2], -1.0, None, ALU.add))
            dve.tensor_copy(n_iter[0:1, 0:2], n_iter_f[0:1, 1:3]).then_inc(iter_ready, 1)
            dve.wait_ge(split_ready, 2)
            dve.tensor_tensor(h_part[:, 2], resid, h_part[:, 1], ALU.subtract).then_inc(split_ready, 1)

            def build_place(col):
                for t in range(TT):
                    ins = dve.tensor_scalar(place[:, t, :], const("iota2")[:, 0:CAP], posm[:, t, bass.ds(col, 1)], None, ALU.is_equal)
                ins.then_inc(place_ready, 1)

            def build_place_g(col):
                for t in range(TT):
                    ins = dve.tensor_scalar(place_g[:, t, :], const("iota2"), posm[:, t, bass.ds(col, 1)],
                                            gate_of[:, t, bass.ds(col, 1)], ALU.is_equal, ALU.mult)
                ins.then_inc(place_g_ready, 1)

            dve.memset(place_T, 0.0).then_inc(place_T_ready, 1)
            dve.memset(yy, 0.0).then_inc(y_ready, 1)
            build_place(0)
            build_place_g(0)
            dve.wait_ge(gather_done, 1)
            build_place(1)
            n = dve.value_load(n_iter[0:1, 0:1], min_val=NE, max_val=NE * PASSES)
            with dve.Fori(0, n) as it:
                now = dve.snap(it + 1)
                dve.wait_ge(slots_used, dve.snap(it * SLOTS + 8))
                dve.tensor_scalar(gt, bank[4][:, :], LIMIT, None, ALU.min).then_inc(gt_ready, 1)
                dve.tensor_scalar(uc, bank[5][:, :], LIMIT, -LIMIT, ALU.min, ALU.max).then_inc(uc_ready, 1)
                dve.wait_ge(uc_ready, now)
                dve.wait_ge(gt_ready, now)
                dve.scalar_tensor_tensor(out=vv, in0=uc, scalar=1.0, in1=gt, op0=ALU.add, op1=ALU.mult).then_inc(vv_ready, 1)
                dve.wait_ge(sg_ready, now)
                dve.wait_ge(vv_ready, now)
                dve.tensor_tensor(hid, vv, sg, ALU.mult).then_inc(hid_ready, 1)
                dve.wait_ge(place_T_done, now)
                dve.tensor_copy(place_T, bank[5][:, 0:T]).then_inc(place_T_ready, 1)
                build_place(it + 2)
                build_place_g(it + 1)
            dve.wait_ge(acc_done, 1)
            for t in range(TT):
                layer_norm(t, h, [bank[2 * t], bank[2 * t + 1]], None, rowv("ln2_g"), rowv("ln2_b"), x1_ready,
                           TT, resid)

            def rms_norm(to, base):
                dve.wait_ge(rms_std, base)
                link(dve.reciprocal(rms, rms))
                for t in range(TT):
                    dve.tensor_scalar(to[:, t, :], x1[:, t, :], rms[:, t:t + 1], None, ALU.mult).then_inc(hn_ready, 1)

            def scaled_T(base, g, hi, before_rest):
                for t in range(TT):
                    dve.wait_ge(hT_done, base + t + 1)
                    for b in range(2):
                        dve.tensor_tensor(hnT[:, 4 * b:4 * b + 4, t * P:(t + 1) * P],
                                          bank[4 + 2 * t + b][:, :].rearrange("p (k t) -> p k t", k=4),
                                          wide(col2(g)[:, 4 * b:4 * b + 4], P), ALU.mult).then_inc(hT_ready, 1)
                for t in range(TT):
                    cols = slice(t * P, (t + 1) * P)
                    for b in range(2):
                        dve.wait_ge(x_upper, before_rest + 2 * t + b + 1)
                        for k in range(4 * b, 4 * b + 4):
                            ins = dve.tensor_tensor(hnT_rest[:, k, cols], hnT[:, k, cols], hi[k][:, cols].bitcast(F32), ALU.subtract)
                        ins.then_inc(x_rest, 1)

            rms_norm(hn, 1)
            dve.wait_ge(small2_in, 112)
            scaled_T(2, "norm1_g_2", hnT_hi, 0)

            def mix_before(z, mu, n):
                link(dve.tensor_tensor(tmp[:, 0:n, 1:T], z[:, :, 0:T - 1], z[:, :, 1:T], ALU.subtract))
                link(dve.tensor_scalar(tmp[:, 0:n, 0:1], z[:, :, 0:1], -1.0, None, ALU.mult))
                for i in range(n):
                    ins = dve.scalar_tensor_tensor(out=z[:, i, :], in0=tmp[:, i, :], scalar=mu[:, i:i + 1], in1=z[:, i, :],
                                                   op0=ALU.mult, op1=ALU.add)
                    if i < n - 1:
                        link(ins)
                return ins

            link(dve.tensor_copy(pos_f, pos_i))
            link(dve.tensor_tensor(ang, const2("inv_freq").unsqueeze(1).broadcast_to([P, TT, ROT]), wide(pos_f, ROT), ALU.mult))
            link(dve.tensor_scalar(ang_n, ang, float(1 / (2 * np.pi)), 1.5 * 2.0 ** 23, ALU.mult, ALU.add))
            link(dve.tensor_scalar(ang_n, ang_n, -1.5 * 2.0 ** 23, None, ALU.add))
            link(dve.scalar_tensor_tensor(out=ang, in0=ang_n, scalar=-6.28125, in1=ang, op0=ALU.mult, op1=ALU.add))
            link(dve.scalar_tensor_tensor(out=ang, in0=ang_n, scalar=float(6.28125 - 2 * np.pi), in1=ang, op0=ALU.mult, op1=ALU.add))
            link(dve.tensor_scalar(ang, ang, 3.1415925, -3.1415925, ALU.min, ALU.max))
            link(dve.scalar_tensor_tensor(out=ang_n, in0=ang, scalar=-1.0, in1=ang, op0=ALU.mult, op1=ALU.max))
            dve.tensor_scalar(ang_n, ang_n, -1.0, float(np.pi / 2), ALU.mult, ALU.add).then_inc(ang_ready, 1)
            dve.wait_ge(z_raw, 2)
            link(mix_before(lora[:, 0:2, :], col2("mu_lora"), 2))
            link(dve.tensor_tensor(tmp[0:CH, 0, 1:T], lora[0:CH, 2, 0:T - 1], lora[0:CH, 2, 1:T], ALU.subtract))
            link(dve.tensor_scalar(tmp[0:CH, 0, 0:1], lora[0:CH, 2, 0:1], -1.0, None, ALU.mult))
            dve.scalar_tensor_tensor(out=lora[0:CH, 2, :], in0=tmp[0:CH, 0, :], scalar=col2("mu_lora")[0:CH, 2:3], in1=lora[0:CH, 2, :],
                                     op0=ALU.mult, op1=ALU.add).then_inc(lora_mixed, 1)
            dve.wait_ge(z_raw, 4)
            link(mix_before(zr, col2("mu_r"), NP2))
            dve.wait_ge(z_raw, 6)
            link(mix_before(zk, col2("mu_k"), NP2))
            link(dve.tensor_tensor(kk, zk, wide(col2("rwkv_k_k_2"), T), ALU.mult))
            dve.tensor_tensor(kk2, kk, kk, ALU.mult).then_inc(kk2_ready, 1)
            dve.wait_ge(z_raw, 8)
            link(mix_before(zv, col2("mu_v"), NP2))
            dve.wait_ge(lora_up_ready, 4)
            for i in range(NP2):
                link(dve.tensor_tensor_scan(cs[:, i, :], const2("chunk_start"), sd[:, i, :], 0.0, ALU.mult, ALU.add))
            dve.tensor_tensor(sd, cs, sd, ALU.subtract).then_inc(cs_ready, 1)
            dve.wait_ge(lora_up_ready, 8)
            dve.wait_ge(nrm_ready, 2)
            link(dve.tensor_scalar(nrm, nrm, 1e-12, None, ALU.max))
            link(dve.reciprocal(nrm, nrm))
            link(dve.tensor_tensor(kk, kk, nrm, ALU.mult))
            for i in range(NP2):
                link(dve.tensor_scalar(nrm[:, i, :], aa[:, i, :], -1.0, col2("rwkv_k_a_2")[:, i:i + 1], ALU.add, ALU.mult))
            link(dve.scalar_tensor_tensor(out=zk, in0=nrm, scalar=1.0, in1=zk, op0=ALU.add, op1=ALU.mult))
            for i in range(NP2):
                ins = dve.scalar_tensor_tensor(out=kk2[:, i, :], in0=zr[:, i, :], scalar=col2("rwkv_r_k_2")[:, i:i + 1], in1=zk[:, i, :],
                                               op0=ALU.mult, op1=ALU.mult)
            ins.then_inc(rk_ready, 1)
            dve.wait_ge(exp3_ready, 3)
            link(dve.tensor_tensor(ar[:, :, 1, :], zr, e_pos, ALU.mult))
            link(dve.scalar_tensor_tensor(out=ar[:, :, 0, :], in0=kk, scalar=-1.0, in1=e_before, op0=ALU.mult, op1=ALU.mult))
            link(dve.tensor_tensor(aa, aa, kk, ALU.mult))
            link(dve.tensor_tensor(b_hat, aa, e_neg, ALU.mult))
            dve.tensor_tensor(k_hat, zk, e_neg, ALU.mult).then_inc(hats_ready, 1)
            dve.wait_ge(bonus_done, 1)
            dve.tensor_copy(bonus, bank[6][:, 0:TT * NQ].rearrange("p (t h) -> p t h", t=TT)).then_inc(bonus_ready, 1)
            for t in range(TT):
                dve.wait_ge(nat_done, 4 + t + 1)
                dve.tensor_copy(x0[:, t, :, 0:HD], bank[t][:, :].rearrange("p (h k) -> p h k", h=NQ)).then_inc(nat_ready, 1)
            for t in range(TT):
                dve.wait_ge(nat_done, 6 + t + 1)
                dve.tensor_copy(vn[:, t, :], bank[6 + t][:, :]).then_inc(nat_ready, 1)
            dve.wait_ge(qkv2_raw, 4)
            dve.wait_ge(small2_in, 112)
            heads = lambda a: a.rearrange("p w t (h d) -> p (w t h) d", d=HD)
            link(dve.tensor_tensor(sq2, qk2, qk2, ALU.mult))
            dve.tensor_reduce(ss_qk, heads(sq2), AX.X, ALU.add).then_inc(ss_ready, 1)
            dve.wait_ge(rs_ready, 1)
            link(dve.reciprocal(rs_qk, rs_qk))
            link(dve.tensor_tensor(heads(qk2), heads(qk2), wide(rs_qk, HD), ALU.mult))
            dve.wait_ge(trig_ready, 2)
            for w, g in enumerate(("q_norm_g_2", "k_norm_g_2")):
                a = qk2[:, w].rearrange("p t (h d) -> p (t h) d", d=HD)
                link(dve.tensor_tensor(a, a, row2(g).unsqueeze(1).broadcast_to([P, TT * NQ, HD]), ALU.mult))
                for t in range(TT):
                    at = qk2[:, w, t, :].rearrange("p (h d) -> p h d", d=HD)
                    lo, hi = at[:, :, 0:ROT], at[:, :, ROT:2 * ROT]
                    c8, s8 = (x[:, t, :].unsqueeze(1).broadcast_to([P, NQ, ROT]) for x in (cosv, sinv))
                    t0, t1 = rope_t[:, 0, 0:NQ, :], rope_t[:, 0, NQ:2 * NQ, :]
                    t2, t3 = rope_t[:, 1, 0:NQ, :], rope_t[:, 1, NQ:2 * NQ, :]
                    link(dve.tensor_tensor(t0, lo, c8, ALU.mult))
                    link(dve.tensor_tensor(t1, hi, s8, ALU.mult))
                    link(dve.tensor_tensor(t2, hi, c8, ALU.mult))
                    link(dve.tensor_tensor(t3, lo, s8, ALU.mult))
                    link(dve.tensor_tensor(lo, t0, t1, ALU.subtract))
                    ins = dve.tensor_tensor(hi, t2, t3, ALU.add)
                    if (w, t) != (1, TT - 1):
                        link(ins)
            ins.then_inc(qk2_ready, 1)

            def soft_max2(t, pr):
                o = t * NQ
                link(dve.tensor_reduce(nmax2[:, o:o + NQ], pr, AX.X, ALU.max))
                dve.tensor_scalar(nmax2[:, o:o + NQ], nmax2[:, o:o + NQ], -1.0, None, ALU.mult).then_inc(neg_max, 1)

            dve.wait_ge(scores_done, 3)
            for b in range(4):
                s3 = bank[(0, 1, 4, 5)[b]][:, :].rearrange("p (m s) -> p m s", m=2)
                link(dve.tensor_scalar(prob2_1[:, 2 * b:2 * b + 2, 0:P], s3[:, :, 0:P], HD ** -0.5, None, ALU.mult))
                masked(prob2_1[:, 2 * b:2 * b + 2, P:T], s3[:, :, P:T], const("causal").unsqueeze(1).broadcast_to([P, 2, P]))
            soft_max2(0, prob2_1)
            dve.wait_ge(scores_done, 4)
            for half in range(2):
                masked(prob2_0[:, 4 * half:4 * half + 4, :], bank[2 + half][:, :].rearrange("p (m s) -> p m s", m=4),
                       const("causal").unsqueeze(1).broadcast_to([P, 4, P]))
            soft_max2(1, prob2_0)
            for t, pr in enumerate((prob2_1, prob2_0)):
                o = t * NQ
                dve.wait_ge(exp_done, 18 + (t + 1) * NQ)
                link(dve.reciprocal(den2[:, o:o + NQ], den2[:, o:o + NQ]))
                dve.tensor_tensor(pr, pr, wide(den2[:, o:o + NQ], pr.shape[2]), ALU.mult).then_inc(prob_ready, 1)

            two = lambda a: a[:, :].rearrange("p (m w t) -> p m w t", m=2, w=2)
            over = lambda a, n: a.unsqueeze(1).broadcast_to([P, n] + list(a.shape[1:]))
            both = lambda n: const2_sb[:, const2_at[n][0]:const2_at[n][0] + T].rearrange("p (w t) -> p w t", w=2)
            MA_mask, NK_mask = both("subT_before"), both("chunkT_before")
            for tt in range(TT):
                for b in range(2):
                    B, Z = bank[4 * b:4 * b + 4], batch[b]
                    dve.wait_ge(rec_done, count(tensor_steps, "m", tt, b))
                    for half in range(2):
                        ins = dve.tensor_tensor(Z["Mb"][:, 2 * half:2 * half + 2, :], B[2 * half][:, 0:T].rearrange("p (m t) -> p m t", m=2),
                                                over(const2("sub_before"), 2), ALU.mult)
                    ins.then_inc(rec_ready, 1)
                for b in range(2):
                    B, Z = bank[4 * b:4 * b + 4], batch[b]
                    for half in range(2):
                        src, hd = two(B[2 * half + 1]), slice(2 * half, 2 * half + 2)
                        dve.tensor_tensor(Z["MA"][:, hd], src, over(MA_mask, 2), ALU.mult)
                        ins = dve.tensor_tensor(Z["MoT"][:, hd, :], src[:, :, 0, :], over(const2("off_subT"), 2), ALU.mult)
                    ins.then_inc(rec_ready, 1)
                for b in range(2):
                    B, Z = bank[4 * b:4 * b + 4], batch[b]
                    dve.wait_ge(rec_done, count(tensor_steps, "nk", tt, b))
                    for half in range(2):
                        src, hd = two(B[2 * half]), slice(2 * half, 2 * half + 2)
                        ins = dve.tensor_tensor(Z["NK"][:, hd], src, over(NK_mask, 2), ALU.mult)
                    ins.then_inc(rec_ready, 1)
                for b in range(2):
                    B, Z = bank[4 * b:4 * b + 4], batch[b]
                    dve.wait_ge(rec_done, count(tensor_steps, "p4", tt, b))
                    for half in range(2):
                        src, hd = two(B[half]), slice(2 * half, 2 * half + 2)
                        dve.tensor_copy(Z["MA"][:, hd, 0, :], src[:, :, 0, :])
                        ins = dve.tensor_tensor(Z["PU"][:, hd, 1, :], Z["PU"][:, hd, 1, :], src[:, :, 1, :], ALU.add)
                    ins.then_inc(rec_ready, 1)
                for done, which, before in (("p8", 0, "U2"), ("du", 1, "U4")):
                    for b in range(2):
                        B, Z = bank[4 * b:4 * b + 4], batch[b]
                        dve.wait_ge(rec_done, count(tensor_steps, done, tt, b))
                        dve.wait_ge(rec_ready, count(vector_steps, before, tt, b))
                        dve.tensor_tensor(Z["PU"][:, :, 1, :], Z["PU"][:, :, 1, :], B[which][:, :].rearrange("p (m t) -> p m t", m=4),
                                          ALU.add).then_inc(rec_ready, 1)
                for b in range(2):
                    B, Z = bank[4 * b:4 * b + 4], batch[b]
                    dve.wait_ge(rec_done, count(tensor_steps, "x3", tt, b))
                    dve.tensor_tensor(Z["X1"], Z["X1"], B[0][:, :].rearrange("p (m t) -> p m t", m=4), ALU.add).then_inc(rec_ready, 1)
                for b in range(2):
                    B = bank[4 * b:4 * b + 4]
                    dve.wait_ge(rec_done, count(tensor_steps, "rT", tt, b))
                    dve.tensor_tensor(rT[:, 2 * b:2 * b + 2, :], B[1][:, 0:T].rearrange("p (i t) -> p i t", i=2),
                                      ar[:, 2 * b:2 * b + 2, 1, tt * P:(tt + 1) * P], ALU.add).then_inc(rec_ready, 1)
                for b in range(2):
                    B = bank[4 * b:4 * b + 4]
                    dve.wait_ge(rec_done, count(tensor_steps, "fh", tt, b))
                    for c in range(4):
                        pr = slice(2 * b, 2 * b + 2)
                        dve.tensor_tensor(ft[:, c, pr, :], B[c][:, 0:P].rearrange("p (i k) -> p i k", i=2), over(const2("ident64"), 2), ALU.add)
                        ins = dve.tensor_copy(hs[:, c, pr, :], B[c][:, P:T].rearrange("p (i k) -> p i k", i=2))
                    ins.then_inc(rec_ready, 1)
                for c in range(4):
                    number = 4 * tt + c
                    if number == 7:
                        break
                    end = tt * P + (c + 1) * CH - 1
                    ecl = e_pos[:, :, end:end + 1].broadcast_to([P, NP2, HD])
                    if number == 0:
                        dve.wait_ge(rec_ready, count(vector_steps, "FH", 0, 1))
                        dve.tensor_tensor(state, hs[:, 0], ecl, ALU.mult).then_inc(st_ready, 1)
                        continue
                    dve.wait_ge(st_done, number)
                    link(dve.tensor_tensor(st_tmp, bank[0][:, 0:T].rearrange("p (i v) -> p i v", i=NP2), hs[:, c], ALU.add))
                    dve.tensor_tensor(state, st_tmp, ecl, ALU.mult).then_inc(st_ready, 1)
            dve.wait_ge(y2_ready, 4)
            y3 = y2.rearrange("p t (h d) -> p (t h) d", d=HD)
            q3 = sqy.rearrange("p t (h d) -> p (t h) d", d=HD)
            link(dve.tensor_reduce(y_sum, y3, AX.X, ALU.add))
            link(dve.tensor_scalar(y_sum, y_sum, 1.0 / HD, None, ALU.mult))
            link(dve.tensor_tensor(y3, y3, wide(y_sum, HD), ALU.subtract))
            link(dve.tensor_tensor(q3, y3, y3, ALU.mult))
            dve.tensor_reduce(y_sum2, q3, AX.X, ALU.add).then_inc(g_var, 1)
            link(dve.tensor_tensor(bv.rearrange("p t (h d) -> p (t h) d", d=HD), vn.rearrange("p t (h d) -> p (t h) d", d=HD),
                                   wide(bonus.rearrange("p t h -> p (t h)"), HD), ALU.mult))
            dve.wait_ge(g_stds, 2)
            link(dve.reciprocal(y_std, y_std))
            link(dve.tensor_tensor(y3, y3, wide(y_std, HD), ALU.mult))
            link(dve.tensor_tensor(y2, y2, over(row2("rwkv_ln_g_2"), TT), ALU.mult))
            link(dve.tensor_tensor(y2, y2, over(row2("rwkv_ln_b_2"), TT), ALU.add))
            link(dve.tensor_tensor(y2, y2, bv, ALU.add))
            dve.tensor_tensor(y2, y2, g_gate, ALU.mult).then_inc(ya_ready, 1)
            for n2 in range(2):
                g_a, g_b = gate[f"gate_a{n2}"], gate[f"gate_b{n2}"]
                dve.wait_ge(branch_done, n2 + 1)
                for t in range(TT):
                    link(dve.tensor_tensor(g_b[:, t, :], g_b[:, t, :], bank[4 * n2 + t][:, :], ALU.mult))
                dve.wait_ge(branch_done, 3 + n2)
                for t in range(TT):
                    link(dve.tensor_tensor(g_a[:, t, :], g_a[:, t, :], bank[(6, 2)[n2] + t][:, :], ALU.mult))
                    ins = dve.tensor_tensor(mm[:, t, n2 * BANK:(n2 + 1) * BANK], g_a[:, t, :], g_b[:, t, :], ALU.add)
                ins.then_inc(mm_ready, 1)
            dve.wait_ge(ff_upper[0], 1)
            dve.wait_ge(mm_ready, 2)
            dve.tensor_tensor(ff_rest[0][:, 0:2 * D], ff_land[0][:, 0:2 * D], ff_hi[0][:, 0:2 * D].bitcast(F32), ALU.subtract).then_inc(up_rest[0], 1)
            for t in range(TT):
                for n2 in range(2):
                    dve.wait_ge(u_done, 2 * t + n2 + 1)
                    ins = dve.tensor_tensor(x1[:, t, n2 * BANK:(n2 + 1) * BANK], x1[:, t, n2 * BANK:(n2 + 1) * BANK],
                                            bank[2 * t + n2][:, :], ALU.add)
                ins.then_inc(x1_ready, 1)
            rms_norm(hn2, 2)
            scaled_T(6, "norm2_g_2", hnT_hi2, 4)
            def up_part(i, use):
                dve.wait_ge(ff_upper[i], dve.snap(use * 2 - 1) if not isinstance(use, int) else 2 * use - 1)
                dve.tensor_tensor(ff_rest[i][:, 0:2 * D], ff_land[i][:, 0:2 * D], ff_hi[i][:, 0:2 * D].bitcast(F32), ALU.subtract).then_inc(up_rest[i], 1)

            def convolve(i, now, j):
                tap = lambda n: col2(n)[:, bass.ds(j, 1)]
                a = bank[4 + i][:, 0:T]
                dve.wait_ge(ffu_used[i], now)
                dve.tensor_scalar(conv[:, i, :], a, tap("conv2"), tap("ffn_conv_b_2"), ALU.mult, ALU.add).then_inc(hidden_step[i], 1)
                dve.wait_ge(hidden_step[i], dve.snap(now * 4 - 3))
                dve.scalar_tensor_tensor(out=conv[:, i, 1:T], in0=a[:, 0:T - 1], scalar=tap("conv1"), in1=conv[:, i, 1:T],
                                         op0=ALU.mult, op1=ALU.add).then_inc(hidden_step[i], 1)
                dve.wait_ge(hidden_step[i], dve.snap(now * 4 - 2))
                dve.scalar_tensor_tensor(out=conv[:, i, 2:T], in0=a[:, 0:T - 2], scalar=tap("conv0"), in1=conv[:, i, 2:T],
                                         op0=ALU.mult, op1=ALU.add).then_inc(conv_ready[i], 1)

            def hidden(i, now):
                dve.wait_ge(gelu_ready[i], now)
                dve.tensor_tensor(hid2[:, i, :], conv[:, i, :], bank[4 + i][:, T:2 * T], ALU.mult).then_inc(hidden_step[i], 1)
                dve.wait_ge(hidden_step[i], dve.snap(now * 4 - 1))
                dve.tensor_copy(hid2_hi[:, i, :], hid2[:, i, :]).then_inc(hidden_step[i], 1)
                dve.wait_ge(hidden_step[i], dve.snap(now * 4))
                dve.tensor_tensor(hid2_lo[:, i, :], hid2[:, i, :], hid2_hi[:, i, :].bitcast(F32), ALU.subtract).then_inc(hid2_ready[i], 1)

            up_part(1, 1)
            with dve.Fori(0, FT_N // 2 - 1) as it:
                now = dve.snap(it + 1)
                for i in range(2):
                    convolve(i, now, it * 2 + i)
                    hidden(i, now)
                    up_part(i, it + 2)
            for i in range(2):
                convolve(i, FT_N // 2, FT_N - 2 + i)
                hidden(i, FT_N // 2)
            dve.wait_ge(ffn_done, 1)
            for n2 in range(2):
                dve.tensor_copy(out_sb[:, 1, n2 * BANK:(n2 + 1) * BANK], bank[2 + n2][:, :]).then_inc(out_ready[1], 1)

        @block.gpsimd
        def _(pool):
            for n2 in range(len(HALVES)):
                pool.wait_ge(half_upper, n2 + 1)
                pool.tensor_tensor(rest_of(n2), half_view(n2), upper_of(n2).bitcast(F32), ALU.subtract).then_inc(half_rest, 1)
            for tt in range(TT):
                for b in range(2):
                    Z = batch[b]
                    pool.wait_ge(rec_ready, count(vector_steps, "MA", tt, b))
                    pool.tensor_tensor(Z["PU"][:, :, 1, :], Z["MA"][:, :, 0, :], ident.unsqueeze(1).broadcast_to([P, 4, P]),
                                       ALU.add).then_inc(one_added, 1)

            def down_part(i, upper):
                pool.wait_ge(ff_upper[i], upper)
                pool.tensor_tensor(ff_rest[i][:, 2 * D:FF], ff_land[i][:, 2 * D:FF], ff_hi[i][:, 2 * D:FF].bitcast(F32), ALU.subtract).then_inc(down_rest[i], 1)

            pool.wait_ge(mm_ready, 2)
            for i in range(2):
                down_part(i, 2)
            with pool.Fori(1, FT_N // 2) as it:
                for i in range(2):
                    down_part(i, pool.snap(it * 2 + 2))


def tiled(a, width):
    return np.ascontiguousarray(a.reshape(-1, P, width).transpose(1, 0, 2))


def arrange(inputs):
    i = {k: np.asarray(v) for k, v in inputs.items()}
    x = i["x"][0]
    heads = np.concatenate([np.r_[j * HD:(j + 1) * HD, (4 + j) * HD:(5 + j) * HD] for j in range(4)])
    order = np.concatenate([heads, np.arange(512, 1792)])
    w_in, b_in = i["w_in"][0][:, order], i["b_in"][0][order]
    row_of = {"b_in_vug": b_in[W_QK:]}
    rows = np.concatenate([row_of.get(n, i[n][0] if n in i else None) for n, _ in ROWS])
    columns = np.concatenate([b_in[:W_QK].reshape(5, P).T, i["b_spatial"][0].T], axis=1)
    w = i["w_in_2"][0]
    part = lambda lo, n: tiled(w[:, lo:lo + n], n).reshape(P, -1)
    lora_at, q_at, gates_at = 3 * C2, 3 * C2 + LORA, 6 * C2 + LORA
    mu = i["rwkv_mu_2"][0]
    mu_lora = np.pad(mu[lora_at:q_at], (0, 3 * P - LORA))
    vectors = {"mu_lora": mu_lora, "mu_r": mu[:C2], "mu_k": mu[C2:2 * C2], "mu_v": mu[2 * C2:3 * C2]}
    vectors |= {f"conv{j}": i["ffn_conv_w_2"][0][j] for j in range(3)}
    columns2 = [(vectors[n] if n in vectors else i[n][0]).reshape(-1, P).T for n, _ in COLUMNS2]
    up = i["w_ffn_up_2"][0].reshape(KD, P, 2, FT_N, P).transpose(3, 1, 2, 0, 4).reshape(FT_N, P, 2 * D)
    second = {
        "consts2": constants2(), "columns2": np.ascontiguousarray(np.concatenate(columns2, axis=1)),
        "rows2": np.concatenate([i[n][0] for n, _ in ROWS2]),
        "w_lora_up": np.concatenate([i["w_decay_up_2"][0], i["w_aaa_up_2"][0]]), "w_gate_up_2": i["w_gate_up_2"][0],
        "pos": np.ascontiguousarray(i["positions_2"].reshape(TT, P).T),
        "ffn_up": np.ascontiguousarray(up), "ffn_down": i["w_ffn_down_2"][0],
        "w2_lora": tiled(np.pad(w[:, lora_at:q_at], ((0, 0), (0, LORA_W - LORA))), LORA_W).reshape(P, -1), "w2_r": part(0, C2), "w2_k": part(C2, C2), "w2_v": part(2 * C2, C2),
        "w2_q2": part(q_at, C2), "w2_k2": part(q_at + C2, C2), "w2_v2": part(q_at + 2 * C2, C2),
        "w2_branch_a": tiled(i["w_branch_a_2"][0], D).reshape(P, -1), "w2_branch_b": tiled(i["w_branch_b_2"][0], D).reshape(P, -1),
        "w2_out0": tiled(i["w_out_2"][0][:C2], D).reshape(P, -1), "w2_out1": tiled(i["w_out_2"][0][C2:], D).reshape(P, -1),
    }
    second |= {f"w2_gate_{'ab'[br]}{n}": part(gates_at + br * D + n * C2, C2) for br in range(2) for n in range(2)}
    return second | {
        "x": x, "xT": tiled(np.ascontiguousarray(x.T), T), "consts": constants(), "columns": np.ascontiguousarray(columns),
        "rows": rows, "w_in": tiled(w_in, 1792), "w_out": tiled(i["w_out"][0], D),
        "wsT": np.ascontiguousarray(i["w_spatial"][0].transpose(2, 0, 1)), "w_router": tiled(i["w_router"][0], NE),
        "w_gate": i["w_gate"][0], "w_up": i["w_up"][0], "w_down": i["w_down"][0], "b_down": i["b_down"][0],
        "b_gate_up": np.concatenate([i["b_gate"][0], i["b_up"][0]], axis=1),
    }


def kernel(**inputs):
    from concourse import bacc
    from concourse.bass_utils import run_bass_kernel_spmd

    nc = bacc.Bacc("TRN2", target_bir_lowering=False, num_devices=1)
    arrays = arrange(inputs)
    A = {n: nc.dram_tensor(f"in_{n}", a.shape, mybir.dt.from_np(a.dtype), kind="ExternalInput").ap() for n, a in arrays.items()}
    out = nc.dram_tensor("out", (T, D), F32, kind="ExternalOutput").ap()
    program(nc, A, out)
    r = run_bass_kernel_spmd(nc, [{f"in_{n}": a for n, a in arrays.items()}], core_ids=[0])
    return r.results[0]["out"].reshape(1, T, D)
```

```python
from contextlib import ExitStack

import numpy as np

import concourse.bass as bass
from concourse import mybir

F32 = mybir.dt.float32
F32R = mybir.dt.float32r
BF16 = mybir.dt.bfloat16
I32 = mybir.dt.int32
U32 = mybir.dt.uint32
ALU = mybir.AluOpType
ACT = mybir.ActivationFunctionType
AX = mybir.AxisListType

P = 128
T = 256
TT = T // P
D = 1024
KD = D // P
HD = 64
NQ = 8
G1 = 512
NG = 8
GD = G1 // NG
NE = 32
TOPK = 4
CAP = 64
PASSES = T // CAP
COLS = NE * PASSES + 2
BANK = 512
SLOT = 2048
SLOTS = 12
LN_EPS = 1e-5
ALPHA1 = 2.0 ** 0.25
LIMIT = 7.0
SWIGLU_ALPHA = 1.702
NEG = -1e30
W_QK, W_QKV, W_VUG = 640, 768, 1152

ROWS = [("b_in_vug", W_VUG), ("ln_v_g", G1), ("ln_v_b", G1), ("b_router", NE), ("sinks", NQ),
        ("b_out", D), ("ln1_g", D), ("ln1_b", D), ("ln2_g", D), ("ln2_b", D)]
COLUMNS = [("b_in_qk", 5), ("b_s", NG)]
CONSTS = [("ident", P), ("iota2", P), ("iota32", NE), ("upto", P), ("ones", P), ("causal", P), ("before", P), ("thresholds", PASSES)]


KAPPA = float(np.exp(-0.5))
NP2 = 4
CH = 32
SUB = 16
C2 = 512
FT_N = 22
ROT = 8
NORM_EPS, GN_EPS, ROPE_THETA = 1e-6, 64e-5, 500000.0
WBUF = 4096
LORA = 288
LORA_W = 3 * P

ROWS2 = [("q_norm_g_2", HD), ("k_norm_g_2", HD), ("rwkv_ln_g_2", C2), ("rwkv_ln_b_2", C2)]
COLUMNS2 = [("mu_lora", 3), ("mu_r", NP2), ("mu_k", NP2), ("mu_v", NP2), ("decay_bias_2", NP2), ("aaa_bias_2", NP2),
            ("rwkv_k_k_2", NP2), ("rwkv_k_a_2", NP2), ("rwkv_r_k_2", NP2), ("norm1_g_2", KD), ("norm2_g_2", KD),
            ("conv0", FT_N), ("conv1", FT_N), ("conv2", FT_N), ("ffn_conv_b_2", FT_N)]
CONSTS2 = [("sub_before", P), ("subT_before", P), ("chunkT_upto", P), ("off_subT", P), ("chunkT_before", P), ("chunkT_upto2", P),
           ("head_ones", P), ("head_col", 2), ("chunk_start", T), ("ident64", HD), ("inv_freq", ROT)]


def offsets(parts):
    at, n = {}, 0
    for name, width in parts:
        at[name] = (n, width)
        n += width
    return at, n


def constants():
    i = np.arange(P)
    row, col = i[:, None], i[None, :]
    tab = {
        "ident": np.eye(P), "iota2": np.tile(col % CAP + 1, (P, 1)), "iota32": np.tile(np.arange(NE), (P, 1)),
        "upto": row <= col, "ones": np.ones((P, P)),
        "causal": np.where(col <= row, 0.0, NEG), "before": np.where(col > row, 0.0, NEG),
        "thresholds": np.tile(np.arange(PASSES) * CAP - (np.arange(PASSES) == 0), (P, 1)),
    }
    return np.concatenate([np.asarray(tab[n], np.float32) for n, _ in CONSTS], axis=1)


def constants2():
    i = np.arange(P)
    row, col = i[:, None], i[None, :]
    chunk, sub = row // CH == col // CH, row // SUB == col // SUB
    t = np.arange(T)
    freq = np.float32(ROPE_THETA) ** (-np.arange(ROT, dtype=np.float32) / np.float32(ROT))
    tab = {
        "sub_before": sub & (col < row), "subT_before": sub & (row < col), "chunkT_upto": chunk & (row <= col),
        "off_subT": chunk & ~sub & (row < col), "chunkT_before": chunk & (row < col), "chunkT_upto2": chunk & (row <= col),
        "head_ones": row // HD == col // HD, "head_col": row // HD == np.arange(2)[None, :],
        "chunk_start": np.tile(t % CH != 0, (P, 1)), "ident64": row % HD == np.arange(HD)[None, :],
        "inv_freq": np.tile(freq, (P, 1)),
    }
    return np.concatenate([np.asarray(tab[n], np.float32) for n, _ in CONSTS2], axis=1)


def program(nc, A, out):
    ctx = ExitStack()
    with ctx:
        def sem(name):
            return ctx.enter_context(nc.semaphore(name))

        def area(name, floats):
            at = -(-nc.sbuf_base // 32) * 32
            full = ctx.enter_context(nc.sbuf_tensor(name, [P, floats], F32))
            return full, nc.alloc_sbuf_tensor_at(name + "_parts", [P, floats], F32R, offset=at)

        ring, ring_parts = area("ring", SLOTS * SLOT)
        work, work_parts = area("work", 27500)
        bank = [ctx.enter_context(nc.psum_tensor(f"bank{i}", [P, BANK], F32)) for i in range(8)]
        top = [0]

        def take(floats):
            a = work[:, top[0]:top[0] + floats]
            top[0] += floats
            assert top[0] <= 27500, top
            return a

        rows_at, rows_n = offsets(ROWS)
        cols_at, cols_n = offsets(COLUMNS)
        const_at, const_n = offsets(CONSTS)
        const_sb = take(const_n)
        cols_sb = take(cols_n)
        rows_sb = take(rows_n)
        const = lambda n: const_sb[:, const_at[n][0]:sum(const_at[n])]
        colv = lambda n: cols_sb[:, cols_at[n][0]:sum(cols_at[n])]
        rowv = lambda n: rows_sb[:, rows_at[n][0]:sum(rows_at[n])]
        ident = const("ident")
        tables_at = top[0]
        tables = take(2 * TT * COLS)
        posm = tables[:, 0:TT * COLS].rearrange("p (t e) -> p t e", t=TT)
        gate_of = tables[:, TT * COLS:].rearrange("p (t e) -> p t e", t=TT)
        small = take(320)
        small_at = [0]

        def little(*shape):
            n = int(np.prod(shape))
            a = small[:, small_at[0]:small_at[0] + n]
            small_at[0] += n
            assert small_at[0] <= 320
            return a if len(shape) == 1 else a.rearrange("p (a b) -> p a b", a=shape[0])

        eps1, eps2, eps3, n_iter_f = little(1), little(1), little(1), little(4)
        passes = little(PASSES)[0:1, :]
        nmax, den, sink_e = little(TT * NQ), little(TT * NQ), little(TT * NQ)
        g_sum, g_sum2, g_std = little(TT * NG), little(TT * NG), little(TT * NG)
        logits, chosen = little(TT, NE), little(TT, NE)
        top8, top_i, top_f, gates4 = little(TT, 8), little(TT, 8).bitcast(U32), little(TT, TOPK), little(TT, TOPK)
        ntop, gsum, rstd, mv, stats = little(TT), little(TT), little(TT), little(TT, 2), little(2, 6)
        ss1, rms1 = little(TT), little(TT)
        w_router = take(KD * NE).rearrange("p (k e) -> p k e", k=KD)
        n_iter = ctx.enter_context(nc.sbuf_tensor("n_iter", [1, 2], I32))

        xT = ring[:, 22528:24576].rearrange("p (k t) -> p k t", k=KD)
        w_in = ring[:, 0:KD * 1792].rearrange("p (k n) -> p k n", k=KD)
        w_out = ring[:, 14336:22528].rearrange("p (k n) -> p k n", k=KD)
        x_nat = take(TT * D).rearrange("p (t d) -> p t d", t=TT)
        r2_at = top[0]
        wsT_qkT = take(NG * P + 5 * T)
        wsT = wsT_qkT[:, 0:NG * P].rearrange("p (g t) -> p g t", g=NG)
        qkT = wsT_qkT[:, NG * P:].rearrange("p (i t) -> p i t", i=5)
        v_nat = take(TT * P).rearrange("p (t c) -> p t c", t=TT)
        ug = take(2 * TT * G1)
        u_nat = ug[:, 0:TT * G1].rearrange("p (t c) -> p t c", t=TT)
        g_nat = ug[:, TT * G1:].rearrange("p (t c) -> p t c", t=TT)
        prob = take(3 * 1024)
        prob0 = prob[:, 0:1024].rearrange("p (h s) -> p h s", h=NQ)
        prob1 = prob[:, 1024:3072].rearrange("p (h s) -> p h s", h=NQ)
        pT = take(3 * 1024).rearrange("p (j h t) -> p j h t", j=3, h=NQ)
        mixT_at = top[0]
        mixT = take(KD * T).rearrange("p (k t) -> p k t", k=KD)
        sq = take(TT * G1).rearrange("p (t c) -> p t c", t=TT)
        h = ug.rearrange("p (t d) -> p t d", t=TT)
        h_part = prob.bitcast(BF16).rearrange("p (i t d) -> p i t d", i=3, t=TT)
        hT = pT.rearrange("p j h t -> p (j h t)")[:, 0:2048].rearrange("p (k t) -> p k t", k=KD)
        resid = x_nat
        chosen4 = sq.rearrange("p t c -> p (t c)")[:, 0:TT * TOPK * NE].rearrange("p (t k e) -> p t k e", t=TT, k=TOPK)
        pool1 = mixT.rearrange("p k t -> p (k t)")
        gt, sg, uc, vv = (pool1[:, i * 512:(i + 1) * 512] for i in range(4))
        pool2 = rows_sb[:, rows_at["b_out"][0]:rows_at["b_out"][0] + 3072]
        hid, yy = pool2[:, 0:512], pool2[:, 512:1024]
        hidT = pool2[:, 1024:1536].rearrange("p (j c) -> p j c", j=4)
        x_e = pool2[:, 1536:2048].rearrange("p (k s) -> p k s", k=KD)
        place_g = pool2[:, 2048:2304].rearrange("p (t s) -> p t s", t=TT)
        place_T = pool2[:, 2304:2560]
        place = pool2[:, 2560:2624].bitcast(BF16).rearrange("p (t s) -> p t s", t=TT)
        alpha_ident = take(P)
        b_down_area = take(D)
        down_bias_row = b_down_area[0:1, :]
        bias_row = wsT_qkT[0:1, 0:2 * D]

        consts_in, w_g_in, w_u_in = sem("consts_in"), sem("w_g_in"), sem("w_u_in")
        ln_rows_in, wsT_in = sem("ln_rows_in"), sem("wsT_in")
        w_in_in = [sem(f"w_in_in{i}") for i in range(4)]
        w_out_in = sem("w_out_in")
        router_in = sem("router_in")
        proj_done, qk_ready, v_ready, ug_biased, ug_gelu = (sem(n) for n in ("proj_done", "qk_ready", "v_ready", "ug_biased", "ug_gelu"))
        wsT_masked, g_normed, mixed_done, sgu_ready = (sem(n) for n in ("wsT_masked", "g_normed", "mixed_done", "sgu_ready"))
        scores_done, neg_max, exp_done, prob_ready = (sem(n) for n in ("scores_done", "neg_max", "exp_done", "prob_ready"))
        pT_done, pT_ready, attn_done, attn_ready, sguT_done, sguT_ready = (
            sem(n) for n in ("pT_done", "pT_ready", "attn_done", "attn_ready", "sguT_done", "sguT_ready"))
        mix_done, var_ready, std_ready, h_ready, hT_done, hT_ready = (
            sem(n) for n in ("mix_done", "var_ready", "std_ready", "h_ready", "hT_done", "hT_ready"))
        router_done, top_ready, top_exp, chosen_ready = (
            sem(n) for n in ("router_done", "top_ready", "top_exp", "chosen_ready"))
        iter_ready, split_ready = sem("iter_ready"), sem("split_ready")
        slot_in = [sem(f"slot_in{i}") for i in range(SLOTS)]
        slots_used = sem("slots_used")
        bias_in, bias_free, down_bias_in = sem("bias_in"), sem("bias_free"), sem("down_bias_in")
        place_ready, place_g_ready, gather_done, x_e_ready = (sem(n) for n in ("place_ready", "place_g_ready", "gather_done", "x_e_ready"))
        gt_ready, sg_ready, uc_ready, vv_ready, hid_ready = (sem(n) for n in ("gt_ready", "sg_ready", "uc_ready", "vv_ready", "hid_ready"))
        hidT_done, hidT_ready, place_T_done, place_T_ready, y_ready = (
            sem(n) for n in ("hidT_done", "hidT_ready", "place_T_done", "place_T_ready", "y_ready"))
        acc_done, x1_ready, stored = (sem(n) for n in ("acc_done", "x1_ready", "stored"))
        rest_ready, g_var, g_stds = sem("rest_ready"), sem("g_var"), sem("g_stds")
        bonus_ready = sem("bonus_ready")
        dve_step = sem("dve_step")

        def views(a, *parts):
            n, got = 0, []
            for shape in parts:
                w = int(np.prod(shape))
                v = a[:, n:n + w]
                names = "abcd"[:len(shape)]
                if len(shape) > 1:
                    v = v.rearrange(f"p ({' '.join(names)}) -> p {' '.join(names)}", **dict(zip(names, shape)))
                got.append(v)
                n += w
            assert n <= a.shape[1], (n, a.shape)
            return got

        rows2_at, rows2_n = offsets(ROWS2)
        cols2_at, cols2_n = offsets(COLUMNS2)
        const2_at, const2_n = offsets(CONSTS2)
        kept = pT.rearrange("p j h t -> p (j h t)")
        const2_sb, cols2_sb, rows2_sb, w_lora_up, pos_f = views(kept, (const2_n,), (cols2_n,), (rows2_n,), (C2,), (TT,))
        pos_i = pos_f.bitcast(I32)
        const2 = lambda n: const2_sb[:, const2_at[n][0]:sum(const2_at[n])]
        col2 = lambda n: cols2_sb[:, cols2_at[n][0]:sum(cols2_at[n])]
        row2 = lambda n: rows2_sb[:, rows2_at[n][0]:sum(rows2_at[n])]
        w_gate_up = views(sq.rearrange("p t c -> p (t c)"), (2, C2))[0]
        r1 = rows_sb
        r2 = work[:, r2_at:r2_at + 7680]
        rt = ring[:, 4 * WBUF:4 * WBUF + 8192]
        x1 = resid
        hnT = views(mixT.rearrange("p k t -> p (k t)"), (KD, T))[0]
        squares = views(r2, (D,))[0]
        rms_diag = views(r2[:, 3072:], (TT, P))[0]
        zr, zk, zv, lora, tmp, sd, aa = views(r1, (NP2, T), (NP2, T), (NP2, T), (3, T), (NP2, T), (NP2, T), (NP2, T))
        cs = tmp
        small2 = r1[:, 6912:rows_n]
        (ss2, ms2, rms2, ss_qk, rs_qk, cosv, sinv, ang, ang_n, nmax2, den2, bonus, y_sum, y_sum2, y_std) = views(
            small2, (TT, 2), (TT,), (TT,), (2 * TT * NQ,), (2 * TT * NQ,), (TT, ROT), (TT, ROT), (TT, ROT), (TT, ROT),
            (TT * NQ,), (TT * NQ,), (TT, NQ), (TT * NQ,), (TT * NQ,), (TT * NQ,))
        ar, b_hat, k_hat, e_pos, g_gate, ybT = views(r2, (NP2, 2, T), (NP2, T), (NP2, T), (NP2, T), (TT, C2), (NP2, T))
        qk2, _, qkT2, prob_2 = views(rt, (2, TT, C2), (1024,), (2, NP2, T), (3072,))
        pT2 = views(rt, (3, NQ, P))[0]
        sq2 = views(rt[:, 3072:5120], (2, TT, C2))[0]
        rope_t = rt[:, 7168:7680].rearrange("p (x t h r) -> p x t h r", x=4, t=TT, h=NQ)
        prob2_0, prob2_1 = views(prob_2, (NQ, P), (NQ, T))
        v2 = views(b_down_area, (TT, C2))[0]
        _, e_neg, e_before, kk, kk2, nrm = views(rt, (3072,), (NP2, T), (NP2, T), (NP2, T), (NP2, T), (NP2, T))
        x0, = views(r1, (TT, NQ, P))
        vn, bn, kn = views(r1[:, 3840:6912], (TT, C2), (TT, C2), (TT, C2))
        batch = []
        for b, a in enumerate((rt, ring[:, 2 * WBUF:4 * WBUF])):
            names = "Mb MA MoT NK P2 PU X1".split()
            parts = [(4, P), (4, 2, P), (4, P), (4, 2, P), (4, P), (4, 2, P), (4, P)]
            batch.append(dict(zip(names, views(a, *parts))))
        ft, hs, rT = views(rt[:, 5120:8192], (4, NP2, HD), (4, NP2, HD), (NP2, P))
        y2, state = views(ring[:, 2 * WBUF + 5120:4 * WBUF], (TT, C2), (2, NP2, HD))
        ar_of = [views(ring[:, at:at + 2048], (NP2, 2, T))[0] for at in (6144, 0)]
        sqy, bv = views(r1, (TT, C2), (TT, C2))
        yaT = views(r2, (NP2, T))[0]
        gate_at = {"gate_a0": sq.rearrange("p t c -> p (t c)"), "gate_b0": r1[:, 2048:3072], "gate_a1": ring[:, 4096:5120], "gate_b1": ring[:, 5120:6144]}
        gate = {f: views(a, (TT, BANK))[0] for f, a in gate_at.items()}
        mm, = views(r1[:, 3840:5888], (TT, D))
        mT, = views(r1, (KD, T))
        hn2 = views(r1[:, 2048:4096], (TT, D))[0]
        conv, hid2 = views(r2[:, 1024:2048], (2, T), (2, T))
        squares2 = views(r2[:, 1024:], (TT, D))[0]
        hid2_hi, hid2_lo = views(work_parts[:, r2_at + 2048:r2_at + 3072], (2, T), (2, T))
        out_sb = views(r1[:, 2048:4096], (TT, D))[0]

        hnT_rest = views(work_parts[:, mixT_at:mixT_at + KD * T], (KD, T))[0]
        hi_runs = [[(range(0, 6), views(work_parts[:, r2_at + 6144:], (6, T))[0]), (range(6, KD), views(work_parts[:, tables_at:], (2, T))[0])],
                   [(range(0, KD), views(work_parts[:, r2_at + 4096:], (KD, T))[0])]]
        hnT_hi, hnT_hi2 = ([a[:, k - run[0], :] for run, a in runs for k in run] for runs in hi_runs)

        def hi_parts(n2, b, cols):
            for run, a in hi_runs[n2]:
                ks = [k for k in run if k // 4 == b]
                if ks:
                    yield slice(ks[0], ks[-1] + 1), a[:, ks[0] - run[0]:ks[-1] + 1 - run[0], cols]


        FILLS = ["lora", "r", "k", "v", "q2", "k2", "v2", "gate_a0", "gate_b0", "gate_a1", "gate_b1"]
        HALVES = [(f, half) for f in FILLS for half in range(2)]
        HBUF = WBUF // 2

        def half_width(f):
            return KD // 2 * (LORA_W if f == "lora" else C2)

        def half_view(n, of=ring, base=0):
            at = base + n % 4 * HBUF
            return of[:, at:at + half_width(HALVES[n][0])]

        def rest_of(n):
            return half_view(n, ring_parts)

        def upper_of(n):
            return half_view(n, ring_parts, 4 * HBUF)

        def used_count(f):
            return 2 * FILLS.index(f) + 2

        tail_at = {"branch_b": ring[:, 0:WBUF], "branch_a": ring[:, 2 * WBUF:3 * WBUF], "out0": ring[:, 4 * WBUF:5 * WBUF], "out1": ring[:, 5 * WBUF:6 * WBUF]}
        tail = {f: a.rearrange("p (k n) -> p k n", k=4) for f, a in tail_at.items()}
        FF = 3 * D
        ff_land = [ring[:, 3 * WBUF:3 * WBUF + FF], ring[:, 0:FF]]
        ff_hi = [ring_parts[:, at:at + FF] for at in (2 * WBUF, 4 * WBUF)]
        ff_rest = [ring_parts[:, at:at + FF] for at in (FF, 4 * WBUF + FF)]

        small2_in = sem("small2_in")
        half_in, half_used = [sem(f"half_in{b}") for b in range(4)], sem("half_used")
        half_upper, half_rest = sem("half_upper"), sem("half_rest")
        x_upper, x_rest, branch_done = sem("x_upper"), sem("x_rest"), sem("branch_done")
        tail_in = {f: sem(f"{f}_in") for f in ("branch_b", "branch_a", "out")}
        sq_done, rms_std, hn_ready = (sem(n) for n in ("sq_done", "rms_std", "hn_ready"))
        z_raw, lora_mixed, lora_ready, kk2_ready, cs_ready, exp3_ready = (
            sem(n) for n in ("z_raw", "lora_mixed", "lora_ready", "kk2_ready", "cs_ready", "exp3_ready"))
        lora_up_done, lora_up_ready, nrm_done, nrm_ready = (
            sem(n) for n in ("lora_up_done", "lora_up_ready", "nrm_done", "nrm_ready"))
        rk_ready, bonus_done, hats_ready, nat_done, av_ready, bk_ready = (
            sem(n) for n in ("rk_ready", "bonus_done", "hats_ready", "nat_done", "av_ready", "bk_ready"))
        qkv2_raw, ang_ready, trig_ready, ss_ready, rs_ready, qk2_ready, qkT2_done, qkT2_ready = (
            sem(n) for n in ("qkv2_raw", "ang_ready", "trig_ready", "ss_ready", "rs_ready", "qk2_ready", "qkT2_done", "qkT2_ready"))
        tensor_steps = ["m", "nk", "p2", "nv", "p4", "p8", "du", "x1", "x2", "x3", "rT", "fh"]
        scalar_steps = ["P2", "x0", "P4", "P8", "X1", "X2"]
        vector_steps = ["Mb", "MA", "NK", "U2", "U4", "U8", "X3", "rT", "FH"]
        rec_done, rec_copied, rec_ready = sem("rec_done"), sem("rec_copied"), sem("rec_ready")
        pool_ready, st_done, st_ready, y2_done, y2_ready = (
            sem(n) for n in ("pool_ready", "st_done", "st_ready", "y2_done", "y2_ready"))

        CHUNKS = TT * P // CH

        def passed_on(tt, from_start=False):
            return range(0 if from_start or tt else 1, P // CH - (tt == TT - 1))

        def count(steps, step, tt, b):
            return (tt * len(steps) + steps.index(step)) * 2 + b + 1

        ya_ready = sem("ya_ready")
        u_done, gate_ready, mm_ready, rms_ready = (sem(n) for n in ("u_done", "gate_ready", "mm_ready", "rms_ready"))
        ff_in, ff_upper, up_rest, down_rest, ffu_used, ffd_used = (
            [sem(f"{n}{i}") for i in range(2)] for n in ("ff_in", "ff_upper", "up_rest", "down_rest", "ffu_used", "ffd_used"))
        hidden_step, conv_ready, gelu_ready, hid2_ready = (
            [sem(f"{n}{i}") for i in range(2)] for n in ("hidden_step", "conv_ready", "gelu_ready", "hid2_ready"))
        ffn_done, out_ready = sem("ffn_done"), [sem(f"out_ready{t}") for t in range(TT)]

        block = ctx.enter_context(nc.Block())

        def expert_slot(e, j):
            which, c = (("w_gate", "w_up")[j % 2], j // 2) if j < 8 else ("w_down", j - 8)
            return A[which][bass.ds(e, 1), c * 256:(c + 1) * 256, :].rearrange("o (k p) n -> p (o k) n", p=P)

        def slot_view(j):
            return ring[:, j * SLOT:(j + 1) * SLOT].rearrange("p (k n) -> p k n", k=2)

        @block.sync
        def _(sp):
            for i in range(4):
                sp.dma_start(xT[:, 2 * i:2 * i + 2, :], A["xT"][:, 2 * i:2 * i + 2, :]).then_inc(w_in_in[i], 16)
                sp.dma_start(w_in[:, 2 * i:2 * i + 2, 0:W_QKV], A["w_in"][:, 2 * i:2 * i + 2, 0:W_QKV]).then_inc(w_in_in[i], 16)
            sp.dma_start(const_sb, A["consts"]).then_inc(consts_in, 16)
            sp.dma_start(cols_sb, A["columns"]).then_inc(consts_in, 16)
            mix_n = rows_at["b_out"][0]
            sp.dma_start(rows_sb[:, 0:mix_n], A["rows"][0:mix_n].partition_broadcast(P)).then_inc(consts_in, 16)
            sp.dma_start(w_in[:, :, W_QKV + G1:], A["w_in"][:, :, W_QKV + G1:]).then_inc(w_g_in, 16)
            sp.dma_start(wsT, A["wsT"]).then_inc(wsT_in, 16)
            sp.dma_start(w_in[:, :, W_QKV:W_QKV + G1], A["w_in"][:, :, W_QKV:W_QKV + G1]).then_inc(w_u_in, 16)
            for i in range(4):
                sp.dma_start(w_out[:, 2 * i:2 * i + 2, :], A["w_out"][:, 2 * i:2 * i + 2, :]).then_inc(w_out_in, 16)
            sp.dma_start(x_nat, A["x"].rearrange("(t p) d -> p t d", p=P)).then_inc(ln_rows_in, 16)
            sp.dma_start(rows_sb[:, mix_n:rows_n], A["rows"][mix_n:rows_n].partition_broadcast(P)).then_inc(ln_rows_in, 16)
            sp.dma_start(down_bias_row, A["b_down"][0:1, :]).then_inc(down_bias_in, 16)
            sp.wait_ge(proj_done, 6)
            for j in range(SLOTS):
                if j == 7:
                    sp.wait_ge(mix_done, 4)
                    sp.dma_start(bias_row, A["b_gate_up"][0:1, :]).then_inc(bias_in, 16)
                sp.dma_start(slot_view(j), expert_slot(0, j)).then_inc(slot_in[j], 16)
            sp.wait_ge(iter_ready, 1)
            sp.dma_start(const2_sb, A["consts2"]).then_inc(small2_in, 16)
            sp.dma_start(cols2_sb, A["columns2"]).then_inc(small2_in, 16)
            sp.dma_start(w_lora_up, A["w_lora_up"]).then_inc(small2_in, 16)
            sp.wait_ge(chosen_ready, 2)
            sp.dma_start(w_gate_up[:, 0, :], A["w_gate_up_2"][0:P, :]).then_inc(small2_in, 16)
            sp.dma_start(w_gate_up[0:CH, 1, :], A["w_gate_up_2"][P:, :]).then_inc(small2_in, 16)
            sp.dma_start(pos_i, A["pos"]).then_inc(small2_in, 16)
            sp.dma_start(rows2_sb, A["rows2"].partition_broadcast(P)).then_inc(small2_in, 16)
            n = sp.value_load(n_iter[0:1, 0:1], min_val=NE, max_val=NE * PASSES)
            n_rest = sp.value_load(n_iter[0:1, 1:2], min_val=NE - 1, max_val=NE * PASSES - 1)
            with sp.Fori(1, n) as it:
                e = it % NE
                sp.wait_ge(bias_free, it)
                sp.dma_start(bias_row, A["b_gate_up"][bass.ds(e, 1), :]).then_inc(bias_in, 16)
                for j in range(SLOTS):
                    sp.wait_ge(slots_used, sp.snap(it * SLOTS - (SLOTS - j - 1)))
                    if j == 8:
                        sp.dma_start(down_bias_row, A["b_down"][bass.ds(e, 1), :]).then_inc(down_bias_in, 16)
                    sp.dma_start(slot_view(j), expert_slot(e, j)).then_inc(slot_in[j], 16)
            for n2, (f, half) in enumerate(HALVES):
                if n2 < 4:
                    sp.wait_ge(slots_used, sp.snap(n_rest * SLOTS + n2 + 1))
                else:
                    sp.wait_ge(half_used, n2 - 3)
                w = half_width(f)
                sp.dma_start(half_view(n2), A[f"w2_{f}"][:, half * w:(half + 1) * w]).then_inc(half_in[n2 % 4], 16)
            sp.wait_ge(rec_done, count(tensor_steps, "nk", 1, 1))
            sp.dma_start(tail_at["branch_b"], A["w2_branch_b"]).then_inc(tail_in["branch_b"], 16)
            sp.wait_ge(y2_ready, 4)
            for f in ("branch_a", "out0", "out1"):
                sp.dma_start(tail_at[f], A[f"w2_{f}"]).then_inc(tail_in[f.rstrip("01")], 16)

            def ff_load(i, j):
                sp.dma_start(ff_land[i][:, 0:2 * D], A["ffn_up"][bass.ds(j, 1), :, :].rearrange("o p n -> p (o n)")).then_inc(ff_in[i], 16)
                sp.dma_start(ff_land[i][:, 2 * D:FF], A["ffn_down"][bass.ds(j * P, P), :]).then_inc(ff_in[i], 16)

            sp.wait_ge(sguT_done, 2)
            ff_load(0, 0)
            sp.wait_ge(branch_done, 2)
            ff_load(1, 1)
            with sp.Fori(1, FT_N // 2) as it:
                for i in range(2):
                    sp.wait_ge(up_rest[i], it)
                    sp.wait_ge(down_rest[i], it)
                    ff_load(i, it * 2 + i)
            for t in range(TT):
                sp.wait_ge(out_ready[t], 2)
                sp.dma_start(out[t * P:(t + 1) * P, :], out_sb[:, t, :]).then_inc(stored, 16)
            sp.wait_ge(stored, 32)

        @block.tensor
        def _(pe):
            for k in range(KD):
                first, last = k == 0, k == KD - 1
                if k % 2 == 0:
                    pe.wait_ge(w_in_in[k // 2], 32)
                for i in range(5):
                    ins = pe.matmul(bank[i // 2][:, (i % 2) * T:(i % 2 + 1) * T], w_in[:, k, i * P:(i + 1) * P], xT[:, k, :],
                                    start=first and i % 2 == 0, stop=last, skip_group_check=True)
                if last:
                    ins.then_inc(proj_done, 1)
                for t in range(TT):
                    ins = pe.matmul(bank[2][:, T + t * P:T + (t + 1) * P], xT[:, k, t * P:(t + 1) * P], w_in[:, k, W_QK:W_QKV],
                                    start=False, stop=last, skip_group_check=True)
            ins.then_inc(proj_done, 1)
            pe.wait_ge(qk_ready, 5)
            s1_bank = [0, 1, 3, 4]
            for i in range(4):
                for half in range(2):
                    lo = half * HD
                    ins = pe.matmul(bank[s1_bank[2 * half + i // 2]][:, (i % 2) * T:(i % 2 + 1) * T],
                                    qkT[lo:lo + HD, i, P:T], qkT[lo:lo + HD, 4, :],
                                    start=i % 2 == 0, stop=True, skip_group_check=True)
            ins.then_inc(scores_done, 1)
            pe.wait_ge(v_ready, 2)
            for i in range(4):
                for half in range(2):
                    lo = half * HD
                    ins = pe.matmul(bank[2 + 5 * half][:, i * P:(i + 1) * P], qkT[lo:lo + HD, i, 0:P], qkT[lo:lo + HD, 4, 0:P],
                                    start=i == 0, stop=True, skip_group_check=True)
            ins.then_inc(scores_done, 1)

            def project_half(t, to, at):
                for k in range(KD):
                    ins = pe.matmul(bank[to][:, :], xT[:, k, t * P:(t + 1) * P], w_in[:, k, at:at + G1], start=k == 0, stop=k == KD - 1)
                ins.then_inc(proj_done, 1)

            pe.wait_ge(w_g_in, 16)
            for t in range(TT):
                project_half(t, 5 + t, W_QKV + G1)
            t_bank = {1: (3, 4), 2: (2, 7), 0: (5, 6)}
            pe.wait_ge(prob_ready, 1)
            for j in (1, 2, 0):
                if j == 2:
                    pe.wait_ge(neg_max, 2)
                if j == 0:
                    pe.wait_ge(prob_ready, 2)
                    pe.wait_ge(ug_biased, 2)
                for hh in range(NQ):
                    src = prob0[:, hh, :] if j == 0 else prob1[:, hh, (j - 1) * P:j * P]
                    ins = pe.transpose(bank[t_bank[j][hh // 4]][:, (hh % 4) * P:(hh % 4 + 1) * P], src, ident)
                ins.then_inc(pT_done, 1)
            pe.wait_ge(w_u_in, 16)
            project_half(0, 0, W_QKV)
            pe.wait_ge(pT_ready, 3)
            for hh in range(NQ):
                kv = hh // 4 * HD
                half = hh % 2 * HD
                for t in range(TT):
                    to = bank[3 + hh // 4][half:half + HD, (hh // 2 % 2) * T + t * P:(hh // 2 % 2) * T + (t + 1) * P]
                    fresh = hh // 2 % 2 == 0 and t == 0
                    if t == 0:
                        ins = pe.matmul(to, v_nat[:, 0, kv:kv + HD], pT[:, 0, hh, :], start=fresh, stop=True, skip_group_check=True)
                    else:
                        pe.matmul(to, v_nat[:, 0, kv:kv + HD], pT[:, 1, hh, :], start=False, stop=False, skip_group_check=True)
                        ins = pe.matmul(to, v_nat[:, 1, kv:kv + HD], pT[:, 2, hh, :], start=False, stop=True, skip_group_check=True)
            ins.then_inc(attn_done, 1)
            project_half(1, 1, W_QKV)
            pe.wait_ge(wsT_masked, 1)
            pe.wait_ge(g_normed, 1)
            for g in range(NG):
                ins = pe.matmul(bank[(2, 7)[g // 4]][:, (g % 4) * P:(g % 4 + 1) * P].rearrange("p (c d) -> p c d", c=TT),
                                wsT[:, g, :], g_nat[:, :, g * GD:(g + 1) * GD],
                                start=g % 4 == 0, stop=True, skip_group_check=True)
            ins.then_inc(mixed_done, 1)
            mix_bank = [[0, 1], [5, 6]]

            def project_out(t, ks):
                for n in range(2):
                    for k in ks:
                        ins = pe.matmul(bank[mix_bank[t][n]][:, :], mixT[:, k, t * P:(t + 1) * P], w_out[:, k, n * BANK:(n + 1) * BANK],
                                        start=k == 0, stop=k == KD - 1)
                    if ks[-1] == KD - 1:
                        ins.then_inc(mix_done, 1)

            pe.wait_ge(attn_ready, 2)
            pe.wait_ge(w_out_in, 4 * 16)
            pe.wait_ge(ug_biased, 4)
            project_out(0, range(0, 4))
            project_out(1, range(0, 4))
            pe.wait_ge(sgu_ready, 1)
            for c in range(4):
                for t in range(TT):
                    ins = pe.transpose(bank[(2, 7)[c // 2]][:, (c % 2) * T + t * P:(c % 2) * T + (t + 1) * P],
                                       u_nat[:, t, c * P:(c + 1) * P], ident)
            ins.then_inc(sguT_done, 1)
            pe.wait_ge(sguT_ready, 2)
            for t in range(TT):
                project_out(t, range(4, KD))
            for t in range(TT):
                pe.wait_ge(h_ready, t + 1)
                for k in range(KD):
                    ins = pe.transpose(bank[3 + 2 * t + k // 4][:, (k % 4) * P:(k % 4 + 1) * P], h[:, t, k * P:(k + 1) * P], ident)
                ins.then_inc(hT_done, 1)
                pe.wait_ge(router_in, 16)
                pe.wait_ge(hT_ready, 2 * t + 2)
                for k in range(KD):
                    ins = pe.matmul(bank[7][:, t * NE:(t + 1) * NE], hT[:, k, t * P:(t + 1) * P], w_router[:, k, :],
                                    start=k == 0, stop=k == KD - 1, skip_group_check=True)
                if t == TT - 1:
                    ins.then_inc(router_done, 1)
                for n in range(2):
                    pe.matmul(bank[2 * t + n][:, :], alpha_ident, h[:, t, n * BANK:(n + 1) * BANK], start=True, stop=False, skip_group_check=True)
            pe.wait_ge(chosen_ready, 1)
            m0, m1 = chosen[:, 0, :], chosen[:, 1, :]
            pe.matmul(bank[5][:, 0:NE], const("upto"), m0, start=True, stop=True, skip_group_check=True)
            pe.matmul(bank[5][:, NE:2 * NE], const("ones"), m0, start=False, stop=False, skip_group_check=True)
            pe.matmul(bank[5][:, NE:2 * NE], const("upto"), m1, start=False, stop=True, skip_group_check=True).then_inc(router_done, 1)
            pe.matmul(bank[4][0:1, 0:NE], const("ones")[:, 0:1], m0, start=True, stop=False)
            pe.matmul(bank[4][0:1, 0:NE], const("ones")[:, 0:1], m1, start=False, stop=True).then_inc(router_done, 1)

            gate_bank, up_bank, x_bank, y_bank = bank[4], bank[5], bank[6], bank[7]

            def gather():
                for k in range(KD):
                    for n, (t, part) in enumerate((t, part) for t in range(TT) for part in range(3)):
                        ins = pe.matmul(x_bank[:, k * CAP:(k + 1) * CAP], h_part[:, part, t, k * P:(k + 1) * P], place[:, t, :],
                                        start=n == 0, stop=n == 5, skip_group_check=True)
                ins.then_inc(gather_done, 1)

            def scatter(stop):
                for t in range(TT):
                    for n in range(2):
                        lo = n * CAP
                        ins = pe.matmul(bank[2 * t + n][:, :], place_T[lo:lo + CAP, t * P:(t + 1) * P], yy[lo:lo + CAP, :],
                                        start=False, stop=stop, skip_group_check=True)
                return ins

            pe.wait_ge(split_ready, 4)
            pe.wait_ge(place_ready, 1)
            pe.wait_ge(rest_ready, 4)
            gather()
            pe.wait_ge(iter_ready, 1)
            n = pe.value_load(n_iter[0:1, 0:1], min_val=NE, max_val=NE * PASSES)
            with pe.Fori(0, n) as it:
                now, ahead, landed = pe.snap(it + 1), pe.snap(it + 2), pe.snap(it * 16 + 16)
                pe.wait_ge(x_e_ready, now)
                pe.wait_ge(place_T_ready, now)
                pe.wait_ge(bias_in, landed)
                for b, to in enumerate((gate_bank, up_bank)):
                    for n2 in range(2):
                        ins = pe.matmul(to[n2 * CAP:(n2 + 1) * CAP, :], const("ones")[0:1, 0:CAP],
                                        bias_row[:, b * D + n2 * BANK:b * D + (n2 + 1) * BANK], start=True, stop=False)
                ins.then_inc(bias_free, 1)
                for j in range(8):
                    to = (gate_bank, up_bank)[j % 2]
                    pe.wait_ge(slot_in[j], landed)
                    for kk in range(2):
                        for n2 in range(2):
                            ins = pe.matmul(to[n2 * CAP:(n2 + 1) * CAP, :], x_e[:, j // 2 * 2 + kk, :],
                                            slot_view(j)[:, kk, n2 * BANK:(n2 + 1) * BANK],
                                            start=False, stop=j >= 6 and kk == 1)
                    ins.then_inc(slots_used, 1)
                pe.wait_ge(place_ready, ahead)
                gather()
                pe.wait_ge(y_ready, now)
                scatter(False)
                pe.wait_ge(hid_ready, now)
                for j in range(4):
                    ins = pe.transpose(gate_bank[:, j * P:(j + 1) * P], hid[:, j * P:(j + 1) * P], ident)
                ins.then_inc(hidT_done, 1)
                pe.wait_ge(place_g_ready, now)
                for t in range(TT):
                    ins = pe.transpose(up_bank[:, t * P:(t + 1) * P], place_g[:, t, :], ident)
                ins.then_inc(place_T_done, 1)
                pe.wait_ge(down_bias_in, landed)
                for n2 in range(2):
                    pe.matmul(y_bank[n2 * CAP:(n2 + 1) * CAP, :], const("ones")[0:1, 0:CAP], down_bias_row[:, n2 * BANK:(n2 + 1) * BANK],
                              start=True, stop=False)
                pe.wait_ge(hidT_ready, now)
                for j in range(4):
                    pe.wait_ge(slot_in[8 + j], landed)
                    for kk in range(2):
                        k = 2 * j + kk
                        for n2 in range(2):
                            ins = pe.matmul(y_bank[n2 * CAP:(n2 + 1) * CAP, :], hidT[:, k % 4, k // 4 * CAP:(k // 4 + 1) * CAP],
                                            slot_view(8 + j)[:, kk, n2 * BANK:(n2 + 1) * BANK], start=False, stop=k == 7)
                    ins.then_inc(slots_used, 1)
            pe.wait_ge(y_ready, pe.snap(n + 1))
            pe.wait_ge(place_T_ready, pe.snap(n + 1))
            scatter(True).then_inc(acc_done, 1)

            def transpose_hn(src, before):
                for t in range(TT):
                    pe.wait_ge(hn_ready, before + t + 1)
                    for k in range(KD):
                        ins = pe.matmul(bank[4 + 2 * t + k // 4][:, (k % 4) * P:(k % 4 + 1) * P], src[:, t, k * P:(k + 1) * P], rms_diag[:, t, :],
                                        start=k % 4 == 0, stop=True, skip_group_check=True)
                    ins.then_inc(hT_done, 1)

            transpose_hn(x1, 0)

            def three_passes(to, left, right, start, stop):
                pe.matmul(to, left[0], right[0], start=start, stop=False, skip_group_check=True)
                pe.matmul(to, left[0], right[1], start=False, stop=False, skip_group_check=True)
                return pe.matmul(to, left[1], right[0], start=False, stop=stop, skip_group_check=True)

            def halves(f):
                for half in range(2):
                    n2 = 2 * FILLS.index(f) + half
                    pe.wait_ge(half_rest, n2 + 1)
                    if f == FILLS[0]:
                        pe.wait_ge(x_rest, 2 * half + 2)
                    yield half, [a.rearrange("p (k n) -> p k n", k=KD // 2) for a in (upper_of(n2), rest_of(n2))]

            def project_T(f, pair):
                for half, w in halves(f):
                    for i in range(w[0].shape[2] // P):
                        for k in range(KD // 2):
                            kx = half * (KD // 2) + k
                            ins = three_passes(bank[2 * pair + i // 2][:, (i % 2) * T:(i % 2 + 1) * T], [a[:, k, i * P:(i + 1) * P] for a in w],
                                               (hnT_hi[kx], hnT_rest[:, kx, :]), kx == 0 and i % 2 == 0, kx == KD - 1)
                    ins.then_inc(half_used, 1)

            def project(f, pair):
                for half, w in halves(f):
                    for t in range(TT):
                        for k in range(KD // 2):
                            kx = half * (KD // 2) + k
                            ins = three_passes(bank[2 * pair + t][:, :], [a[:, t * P:(t + 1) * P] for a in (hnT_hi[kx], hnT_rest[:, kx, :])],
                                               [a[:, k, :] for a in w], kx == 0, kx == KD - 1)
                    ins.then_inc(half_used, 1)

            for n2, f in enumerate(("lora", "r", "k", "v")):
                project_T(f, (n2 + 3) % 4)
            pe.wait_ge(small2_in, 112)
            pe.wait_ge(lora_ready, 1)
            for i in range(NP2):
                ins = pe.matmul(bank[6 + i // 2][:, (i % 2) * T:(i % 2 + 1) * T], w_lora_up[0:HD, i * P:(i + 1) * P], lora[0:HD, 0, :],
                                start=True, stop=True, skip_group_check=True)
            ins.then_inc(lora_up_done, 1)
            pe.wait_ge(z_raw, 4)
            for i in range(NP2):
                ins = pe.matmul(bank[i // 2][:, (i % 2) * T:(i % 2 + 1) * T], w_lora_up[HD:P, i * P:(i + 1) * P], lora[HD:P, 0, :],
                                start=True, stop=True, skip_group_check=True)
            ins.then_inc(lora_up_done, 1)
            pe.wait_ge(z_raw, 6)
            pe.wait_ge(lora_ready, 3)
            for t in range(TT):
                pe.matmul(bank[2 + t][:, :], lora[:, 1, t * P:(t + 1) * P], w_gate_up[:, 0, :], start=True, stop=False)
                ins = pe.matmul(bank[2 + t][:, :], lora[0:CH, 2, t * P:(t + 1) * P], w_gate_up[0:CH, 1, :], start=False, stop=True)
            ins.then_inc(lora_up_done, 1)
            pe.wait_ge(z_raw, 8)
            project("q2", 2)
            pe.wait_ge(kk2_ready, 1)
            pe.wait_ge(lora_up_ready, 4)
            for b in range(2):
                ins = pe.matmul(bank[6 + b][:, :].rearrange("p (i t) -> p i t", i=2), const2("head_ones"), kk2[:, 2 * b:2 * b + 2, :],
                                start=True, stop=True)
            ins.then_inc(nrm_done, 1)
            pe.wait_ge(lora_up_ready, 8)
            project("k2", 0)
            pe.wait_ge(lora_up_ready, 10)
            project("v2", 1)
            pe.wait_ge(qkv2_raw, 2)
            project("gate_a0", 2)
            pe.wait_ge(rk_ready, 1)
            pe.wait_ge(nrm_ready, 2)
            for t in range(TT):
                for i in range(NP2):
                    ins = pe.matmul(bank[6][:, t * NQ + 2 * i:t * NQ + 2 * i + 2], kk2[:, i, t * P:(t + 1) * P], const2("head_col"),
                                    start=t == 0 and i == 0, stop=True, skip_group_check=True)
            ins.then_inc(bonus_done, 1)
            pe.wait_ge(hats_ready, 1)
            pe.wait_ge(qkv2_raw, 6)
            for y in (1, 2, 0, 3):
                if y == 2:
                    pe.wait_ge(gate_ready, 2)
                if y == 3:
                    pe.wait_ge(bonus_ready, 1)
                for t in range(TT):
                    for i in range(NP2):
                        src = (ar[:, i, 0, :], b_hat[:, i, :], k_hat[:, i, :], zv[:, i, :])[y][:, t * P:(t + 1) * P]
                        ins = pe.transpose(bank[2 * y + t][:, i * P:(i + 1) * P], src, ident)
                    ins.then_inc(nat_done, 1)

            pe.wait_ge(bk_ready, 2)
            project("gate_b0", 1)
            pe.wait_ge(qk2_ready, 1)
            pe.wait_ge(av_ready, 4)
            pe.wait_ge(bk_ready, 4)
            for w in range(2):
                for i in range(NP2):
                    for t in range(TT):
                        ins = pe.transpose(bank[4 * w + i // 2][:, (i % 2) * T + t * P:(i % 2) * T + (t + 1) * P],
                                           qk2[:, w, t, i * P:(i + 1) * P], ident)
            ins.then_inc(qkT2_done, 1)
            project("gate_a1", 3)
            pe.wait_ge(qkT2_ready, 4)
            for i in range(NP2):
                for half in range(2):
                    lo = half * HD
                    ins = pe.matmul(bank[4 * half + i // 2][:, (i % 2) * T:(i % 2 + 1) * T], qkT2[lo:lo + HD, 0, i, P:T],
                                    qkT2[lo:lo + HD, 1, i, :], start=i % 2 == 0, stop=True, skip_group_check=True)
            ins.then_inc(scores_done, 1)
            pe.wait_ge(gate_ready, 4)
            for i in range(NP2):
                for half in range(2):
                    lo = half * HD
                    ins = pe.matmul(bank[2 + half][:, i * P:(i + 1) * P], qkT2[lo:lo + HD, 0, i, 0:P], qkT2[lo:lo + HD, 1, i, 0:P],
                                    start=i == 0, stop=True, skip_group_check=True)
            ins.then_inc(scores_done, 1)
            pe.wait_ge(gate_ready, 6)
            project("gate_b1", 3)
            pe.wait_ge(prob_ready, 3)
            for j in (1, 2, 0):
                if j == 0:
                    pe.wait_ge(prob_ready, 4)
                for m in range(NQ):
                    src = prob2_0[:, m, :] if j == 0 else prob2_1[:, m, (j - 1) * P:j * P]
                    ins = pe.transpose(bank[2 * j + m // 4][:, (m % 4) * P:(m % 4 + 1) * P], src, ident)
                ins.then_inc(pT_done, 1)
            pe.wait_ge(pT_ready, 6)
            pe.wait_ge(gate_ready, 8)
            for m in range(NQ):
                half, i = m // 4, m % 4
                hh = 2 * i + half
                for t in range(TT):
                    to = bank[6 + i // 2][half * HD:(half + 1) * HD, (i % 2) * T + t * P:(i % 2) * T + (t + 1) * P]
                    for j in ([0] if t == 0 else [1, 2]):
                        ins = pe.matmul(to, v2[:, max(j - 1, 0), hh * HD:(hh + 1) * HD], pT2[:, j, m, :],
                                        start=i % 2 == 0 and j == 0, stop=j != 1, skip_group_check=True)
            ins.then_inc(attn_done, 1)

            def head(b, m):
                half, i = m // 2, 2 * b + m % 2
                return 2 * i + half, i, half * HD

            pe.wait_ge(pool_ready, 2)
            for tt in range(TT):
                cols = slice(tt * P, (tt + 1) * P)
                if tt > 0:
                    pe.wait_ge(y2_ready, 2 * tt)
                    pe.wait_ge(st_ready, tt * P // CH - 1)
                for b in range(2):
                    B = bank[4 * b:4 * b + 4]
                    if tt == 0 and b == 1:
                        pe.wait_ge(attn_ready, 4)
                    for m in range(4):
                        hh, i, lo = head(b, m)
                        pe.matmul(B[2 * (m // 2)][:, (m % 2) * P:(m % 2 + 1) * P], ar_of[m // 2][:, i, 0, cols], b_hat[:, i, cols],
                                  start=m % 2 == 0, stop=True, skip_group_check=True)
                        ins = pe.matmul(B[2 * (m // 2) + 1][:, (m % 2) * T:(m % 2 + 1) * T].rearrange("p (w t) -> p w t", w=2),
                                        b_hat[:, i, cols], ar_of[m // 2][:, i, :, cols],
                                        start=m % 2 == 0, stop=True, skip_group_check=True)
                    ins.then_inc(rec_done, 1)
                for b in range(2):
                    B = bank[4 * b:4 * b + 4]
                    pe.wait_ge(rec_ready, count(vector_steps, "Mb", tt, b))
                    for m in range(4):
                        hh, i, lo = head(b, m)
                        ins = pe.matmul(B[2 * (m // 2)][:, (m % 2) * T:(m % 2 + 1) * T].rearrange("p (w t) -> p w t", w=2),
                                        k_hat[:, i, cols], ar_of[m // 2][:, i, :, cols],
                                        start=m % 2 == 0, stop=True, skip_group_check=True)
                    ins.then_inc(rec_done, 1)
                for b in range(2):
                    B, Z = bank[4 * b:4 * b + 4], batch[b]
                    pe.wait_ge(rec_ready, count(vector_steps, "MA", tt, b))
                    for m in range(4):
                        c = slice(m * P, (m + 1) * P)
                        pe.matmul(B[1][:, c], Z["MA"][:, m, 0, :], Z["Mb"][:, m, :], start=m == 0, stop=True, skip_group_check=True)
                        ins = pe.matmul(B[3][:, c], Z["Mb"][:, m, :], Z["MA"][:, m, 0, :], start=m == 0, stop=True, skip_group_check=True)
                    ins.then_inc(rec_done, 1)
                for b in range(2):
                    B, Z = bank[4 * b:4 * b + 4], batch[b]
                    pe.wait_ge(rec_ready, count(vector_steps, "NK", tt, b))
                    for m in range(4):
                        hh, i, lo = head(b, m)
                        ins = pe.matmul(B[2][:, m * HD:(m + 1) * HD], Z["NK"][:, m, 0, :], vn[:, tt, hh * HD:(hh + 1) * HD],
                                        start=m == 0, stop=True, skip_group_check=True)
                    ins.then_inc(rec_done, 1)
                for b in range(2):
                    B, Z = bank[4 * b:4 * b + 4], batch[b]
                    pe.wait_ge(rec_copied, count(scalar_steps, "P2", tt, b))
                    pe.wait_ge(pool_ready, 2 + 2 * tt + b + 1)
                    for m in range(4):
                        pe.matmul(B[m // 2][:, (m % 2) * T:(m % 2 + 1) * T].rearrange("p (w t) -> p w t", w=2), Z["P2"][:, m, :], Z["PU"][:, m],
                                  start=m % 2 == 0, stop=True, skip_group_check=True)
                        ins = pe.matmul(B[3][:, m * P:(m + 1) * P], Z["PU"][:, m, 0, :], Z["P2"][:, m, :],
                                        start=m == 0, stop=True, skip_group_check=True)
                    ins.then_inc(rec_done, 1)
                for b in range(2):
                    B, Z = bank[4 * b:4 * b + 4], batch[b]
                    pe.wait_ge(rec_copied, count(scalar_steps, "P4", tt, b))
                    pe.wait_ge(rec_ready, count(vector_steps, "U2", tt, b))
                    pe.wait_ge(rec_copied, count(scalar_steps, "x0", tt, b))
                    for m in range(4):
                        c = slice(m * P, (m + 1) * P)
                        pe.matmul(B[2][:, c], Z["MA"][:, m, 0, :], Z["Mb"][:, m, :], start=m == 0, stop=True, skip_group_check=True)
                        ins = pe.matmul(B[0][:, c], Z["Mb"][:, m, :], Z["PU"][:, m, 1, :], start=m == 0, stop=True, skip_group_check=True)
                    ins.then_inc(rec_done, 1)
                for b in range(2):
                    B, Z = bank[4 * b:4 * b + 4], batch[b]
                    pe.wait_ge(rec_copied, count(scalar_steps, "P8", tt, b))
                    pe.wait_ge(rec_ready, count(vector_steps, "U4", tt, b))
                    for m in range(4):
                        ins = pe.matmul(B[1][:, m * P:(m + 1) * P], Z["P2"][:, m, :], Z["PU"][:, m, 1, :],
                                        start=m == 0, stop=True, skip_group_check=True)
                    ins.then_inc(rec_done, 1)
                for b in range(2):
                    B, Z = bank[4 * b:4 * b + 4], batch[b]
                    pe.wait_ge(rec_ready, count(vector_steps, "U8", tt, b))
                    for m in range(4):
                        ins = pe.matmul(B[3][:, m * P:(m + 1) * P], Z["PU"][:, m, 1, :], x0[:, tt, head(b, m)[0], :],
                                        start=m == 0, stop=True, skip_group_check=True)
                    ins.then_inc(rec_done, 1)
                for b in range(2):
                    B, Z = bank[4 * b:4 * b + 4], batch[b]
                    pe.wait_ge(rec_copied, count(scalar_steps, "X1", tt, b))
                    for m in range(4):
                        ins = pe.matmul(B[2][:, m * P:(m + 1) * P], Z["MoT"][:, m, :], Z["X1"][:, m, :],
                                        start=m == 0, stop=True, skip_group_check=True)
                    ins.then_inc(rec_done, 1)
                for b in range(2):
                    B, Z = bank[4 * b:4 * b + 4], batch[b]
                    pe.wait_ge(rec_copied, count(scalar_steps, "X2", tt, b))
                    for m in range(4):
                        ins = pe.matmul(B[0][:, m * P:(m + 1) * P], Z["PU"][:, m, 1, :], Z["Mb"][:, m, :],
                                        start=m == 0, stop=True, skip_group_check=True)
                    ins.then_inc(rec_done, 1)
                for b in range(2):
                    B, Z = bank[4 * b:4 * b + 4], batch[b]
                    pe.wait_ge(rec_ready, count(vector_steps, "X3", tt, b))
                    for m in range(4):
                        hh, i, lo = head(b, m)
                        ins = pe.matmul(B[1][lo:lo + HD, (m % 2) * P:(m % 2 + 1) * P], Z["X1"][:, m, 0:HD], Z["MA"][:, m, 1, :],
                                        start=m % 2 == 0, stop=True, skip_group_check=True)
                    ins.then_inc(rec_done, 1)
                for b in range(2):
                    B, Z = bank[4 * b:4 * b + 4], batch[b]
                    pe.wait_ge(rec_ready, count(vector_steps, "rT", tt, b))
                    for m in range(4):
                        hh, i, lo = head(b, m)
                        hc = slice(hh * HD, (hh + 1) * HD)
                        f_at, h_at = (slice(at + (m % 2) * HD, at + (m % 2 + 1) * HD) for at in (0, P))
                        rows_of = lambda c: slice(c * CH, (c + 1) * CH)
                        for c in passed_on(tt):
                            rows = rows_of(c)
                            pe.matmul(B[c][lo:lo + HD, f_at], Z["X1"][rows, m, 0:HD], bn[rows, tt, hc],
                                      start=m % 2 == 0, stop=True, skip_group_check=True)
                        for c in passed_on(tt, True):
                            rows = rows_of(c)
                            pe.matmul(B[c][lo:lo + HD, h_at], bn[rows, tt, hc], Z["X1"][rows, m, HD:P],
                                      start=m % 2 == 0 and c not in passed_on(tt), stop=False, skip_group_check=True)
                        for c in passed_on(tt, True):
                            rows = rows_of(c)
                            ins = pe.matmul(B[c][lo:lo + HD, h_at], kn[rows, tt, hc], vn[rows, tt, hc],
                                            start=False, stop=True, skip_group_check=True)
                    ins.then_inc(rec_done, 1)
                def outputs(items):
                    for b, m in items:
                        hh, i, lo = head(b, m)
                        y_to = bank[2 + m // 2][:, i * HD:(i + 1) * HD]
                        pe.matmul(y_to, batch[b]["MA"][:, m, 1, :], batch[b]["X1"][:, m, HD:P], start=b == 0 and m % 2 == 0, stop=False,
                                  skip_group_check=True)
                        ins = pe.matmul(y_to, batch[b]["NK"][:, m, 1, :], vn[:, tt, hh * HD:(hh + 1) * HD], start=False, stop=False,
                                        skip_group_check=True)
                    return ins

                pe.wait_ge(rec_ready, count(vector_steps, "FH", tt, 0))
                outputs([(0, 0), (0, 2), (0, 1)])
                pe.wait_ge(rec_ready, count(vector_steps, "FH", tt, 1))
                between = [[(0, 3)], [(1, 0), (1, 1)], [(1, 2), (1, 3)], []]
                for c in range(P // CH):
                    rows = slice(c * CH, (c + 1) * CH)
                    number = tt * P // CH + c
                    if number > 0:
                        now, to = hs[:, 0] if number == 1 else state[:, (number - 1) % 2], bank[number % 2]
                        if number > 1:
                            pe.wait_ge(st_ready, number - 1)
                        if number < CHUNKS - 1:
                            for i in range(NP2):
                                for half in range(2):
                                    lo = half * HD
                                    ins = pe.matmul(to[lo:lo + HD, i * HD:(i + 1) * HD], ft[lo:lo + HD, c, i, :], now[lo:lo + HD, i, :],
                                                    start=i == 0, stop=True, skip_group_check=True)
                            ins.then_inc(st_done, 1)
                        for i in range(NP2):
                            for half in range(2):
                                lo = half * HD
                                ins = pe.matmul(bank[2 + half][rows, i * HD:(i + 1) * HD], rT[lo:lo + HD, i, rows], now[lo:lo + HD, i, :],
                                                start=False, stop=True, skip_group_check=True)
                    if between[c]:
                        ins = outputs(between[c])
                ins.then_inc(y2_done, 1)
            def branch(f, yT, to):
                pe.wait_ge(tail_in[f], 16)
                for n2 in range(2):
                    for t in range(TT):
                        for k in range(NP2):
                            ins = pe.matmul(bank[to[n2] + t][:, :], yT[:, k, t * P:(t + 1) * P], tail[f][:, k, n2 * BANK:(n2 + 1) * BANK],
                                            start=k == 0, stop=k == NP2 - 1)
                    ins.then_inc(branch_done, 1)

            pe.wait_ge(st_ready, CHUNKS - 2)
            branch("branch_b", ybT, (0, 4))
            pe.wait_ge(ya_ready, 1)
            for i in range(NP2):
                for t in range(TT):
                    ins = pe.transpose(bank[2 + i // 2][:, (i % 2) * T + t * P:(i % 2) * T + (t + 1) * P], y2[:, t, i * P:(i + 1) * P], ident)
            ins.then_inc(sguT_done, 1)
            pe.wait_ge(sguT_ready, 4)
            branch("branch_a", yaT, (6, 2))
            for t in range(TT):
                pe.wait_ge(mm_ready, t + 1)
                for n2 in range(2):
                    pe.matmul(bank[2 * t + n2][:, :], ident, x1[:, t, n2 * BANK:(n2 + 1) * BANK], start=True, stop=False, skip_group_check=True)
            for t in range(TT):
                for k in range(KD):
                    ins = pe.transpose(bank[4 + 2 * t + k // 4][:, (k % 4) * P:(k % 4 + 1) * P], mm[:, t, k * P:(k + 1) * P], ident)
                ins.then_inc(hT_done, 1)
            pe.wait_ge(hT_ready, 12)
            pe.wait_ge(tail_in["out"], 32)
            for t in range(TT):
                for n2 in range(2):
                    for k in range(KD):
                        ins = pe.matmul(bank[2 * t + n2][:, :], mT[:, k, t * P:(t + 1) * P],
                                        tail["out0" if k < 4 else "out1"][:, k % 4, n2 * BANK:(n2 + 1) * BANK],
                                        start=False, stop=False, skip_group_check=True)
                    ins.then_inc(u_done, 1)
            transpose_hn(hn2, TT)

            def ffn_up(i, use, first=False):
                pe.wait_ge(up_rest[i], use)
                w = [a[i][:, 0:2 * D].rearrange("p (c k n) -> p c k n", c=2, k=KD) for a in (ff_hi, ff_rest)]
                for c in range(2):
                    for k in range(KD):
                        if first and c == 0 and k % 4 == 0:
                            pe.wait_ge(x_rest, 4 + k // 2 + 2)
                        ins = three_passes(bank[4 + i][:, c * T:(c + 1) * T], [a[:, c, k, :] for a in w], (hnT_hi2[k], hnT_rest[:, k, :]),
                                           c == 0 and k == 0, k == KD - 1)
                ins.then_inc(ffu_used[i], 1)

            def ffn_down(i, use, last=False):
                pe.wait_ge(down_rest[i], use)
                pe.wait_ge(hid2_ready[i], use)
                w = [a[i][:, 2 * D:FF] for a in (ff_hi, ff_rest)]
                for t in range(TT):
                    for n2 in range(2):
                        ins = three_passes(bank[2 * t + n2][:, :], [a[:, i, t * P:(t + 1) * P] for a in (hid2_hi, hid2_lo)],
                                           [a[:, n2 * BANK:(n2 + 1) * BANK] for a in w], False, last)
                ins.then_inc(ffn_done if last else ffd_used[i], 1)

            ffn_up(0, 1, first=True)
            with pe.Fori(0, FT_N // 2 - 1) as it:
                now, ahead = pe.snap(it + 1), pe.snap(it + 2)
                ffn_up(1, now)
                ffn_down(0, now)
                ffn_up(0, ahead)
                ffn_down(1, now)
            ffn_up(1, FT_N // 2)
            ffn_down(0, FT_N // 2)
            ffn_down(1, FT_N // 2, last=True)

        @block.scalar
        def _(act):
            act.dma_start(w_router, A["w_router"]).then_inc(router_in, 16)
            act.wait_ge(consts_in, 48)
            act.wait_ge(proj_done, 1)
            for i in range(4):
                act.activation(qkT[:, i, :], bank[i // 2][:, (i % 2) * T:(i % 2 + 1) * T], ACT.Identity,
                               bias=colv("b_in_qk")[:, i:i + 1]).then_inc(qk_ready, 1)
            for t, pr in enumerate((prob1, prob0)):
                act.wait_ge(neg_max, t + 1)
                for hh in range(NQ):
                    act.activation(pr[:, hh, :], pr[:, hh, :], ACT.Exp, bias=nmax[:, t * NQ + hh:t * NQ + hh + 1],
                                   accum_out=den[:, t * NQ + hh:t * NQ + hh + 1]).then_inc(exp_done, 1)
                act.activation(sink_e[:, t * NQ:(t + 1) * NQ], sink_e[:, t * NQ:(t + 1) * NQ], ACT.Exp).then_inc(exp_done, 1)

            def gelu_u(t):
                act.wait_ge(ug_biased, 3 + t)
                act.activation(u_nat[:, t, :], u_nat[:, t, :], ACT.Gelu_apprx_tanh).then_inc(ug_gelu, 1)

            act.wait_ge(ug_biased, 2)
            act.activation(g_nat, g_nat, ACT.Gelu_apprx_tanh).then_inc(ug_gelu, 1)
            t_bank = {1: (3, 4), 2: (2, 7), 0: (5, 6)}
            for n2, j in enumerate((1, 2, 0)):
                act.wait_ge(pT_done, n2 + 1)
                for b in range(2):
                    ins = act.copy(pT[:, j, 4 * b:4 * b + 4, :], bank[t_bank[j][b]][:, :].rearrange("p (h t) -> p h t", h=4))
                ins.then_inc(pT_ready, 1)
            act.wait_ge(g_var, 1)
            act.activation(g_std, g_sum2, ACT.Sqrt, bias=eps1, scale=1.0 / GD).then_inc(g_stds, 1)
            gelu_u(0)
            act.wait_ge(attn_done, 1)
            for b in range(2):
                act.copy(mixT[:, 2 * b:2 * b + 2, :], bank[3 + b][:, :].rearrange("p (k t) -> p k t", k=2)).then_inc(attn_ready, 1)
            gelu_u(1)
            def split_rest(t):
                act.wait_ge(rest_ready, 2 * t + 1)
                act.copy(h_part[:, 1, t, :], resid[:, t, :]).then_inc(split_ready, 1)

            for t in range(TT):
                act.wait_ge(var_ready, t + 1)
                act.activation(rstd[:, t:t + 1], mv[:, t, 1:2], ACT.Sqrt, bias=eps1).then_inc(std_ready, 1)
                if t > 0:
                    split_rest(t - 1)
                act.wait_ge(hT_done, t + 1)
                for b in range(2):
                    act.copy(hT[:, 4 * b:4 * b + 4, t * P:(t + 1) * P],
                             bank[3 + 2 * t + b][:, :].rearrange("p (k t) -> p k t", k=4)).then_inc(hT_ready, 1)
                act.copy(h_part[:, 0, t, :], h[:, t, :]).then_inc(split_ready, 1)
            split_rest(TT - 1)
            act.wait_ge(top_ready, 2)
            for t in range(TT):
                act.activation(gates4[:, t, :], gates4[:, t, :], ACT.Exp, bias=ntop[:, t:t + 1],
                               accum_out=gsum[:, t:t + 1]).then_inc(top_exp, 1)
            act.wait_ge(gather_done, 1)
            act.copy(x_e, bank[6][:, :].rearrange("p (k s) -> p k s", k=KD)).then_inc(x_e_ready, 1)
            act.wait_ge(iter_ready, 1)
            n = act.value_load(n_iter[0:1, 0:1], min_val=NE, max_val=NE * PASSES)
            with act.Fori(0, n) as it:
                now, ahead = act.snap(it + 1), act.snap(it + 2)
                act.wait_ge(gt_ready, now)
                act.activation(sg, gt, ACT.Sigmoid, scale=SWIGLU_ALPHA).then_inc(sg_ready, 1)
                act.wait_ge(gather_done, ahead)
                act.copy(x_e, bank[6][:, :].rearrange("p (k s) -> p k s", k=KD)).then_inc(x_e_ready, 1)
                act.wait_ge(hidT_done, now)
                act.copy(hidT, bank[4][:, :].rearrange("p (j c) -> p j c", j=4)).then_inc(hidT_ready, 1)
                act.wait_ge(slots_used, act.snap(it * SLOTS + SLOTS))
                act.copy(yy, bank[7][:, :]).then_inc(y_ready, 1)
            for n2 in range(2):
                act.wait_ge(half_in[n2], 16)
                act.copy(upper_of(n2), half_view(n2)).then_inc(half_upper, 1)

            def upper(f):
                for half in range(2):
                    n2 = 2 * FILLS.index(f) + half
                    act.wait_ge(half_in[n2 % 4], 16 * (n2 // 4 + 1))
                    act.copy(upper_of(n2), half_view(n2)).then_inc(half_upper, 1)

            def upper_x(n2, before):
                for b in range(2):
                    for t in range(TT):
                        act.wait_ge(hT_ready, before + 2 * t + b + 1)
                        for ks, hi in hi_parts(n2, b, slice(t * P, (t + 1) * P)):
                            ins = act.copy(hi, hnT[:, ks, t * P:(t + 1) * P])
                        ins.then_inc(x_upper, 1)

            for t in range(TT):
                act.wait_ge(var_ready, TT + t + 1)
                act.activation(rstd[:, t:t + 1], mv[:, t, 1:2], ACT.Sqrt, bias=eps1).then_inc(std_ready, 1)
                act.wait_ge(x1_ready, t + 1)
                act.activation(squares, x1[:, t, :], ACT.Square, accum_out=ss1[:, t:t + 1]).then_inc(sq_done, 1)
                act.wait_ge(sq_done, t + 1)
                act.activation(rms1[:, t:t + 1], ss1[:, t:t + 1], ACT.Sqrt, bias=eps2, scale=1.0 / D).then_inc(rms_std, 1)
            upper_x(0, 4)
            upper("r")
            act.wait_ge(half_used, used_count("lora"))
            act.copy(lora[:, 0:2, :], bank[6][:, :].rearrange("p (i t) -> p i t", i=2)).then_inc(z_raw, 1)
            act.copy(lora[0:CH, 2, :], bank[7][0:CH, 0:T]).then_inc(z_raw, 1)
            upper("k")
            act.wait_ge(lora_mixed, 1)
            act.activation(lora[0:HD, 0, :], lora[0:HD, 0, :], ACT.Tanh).then_inc(lora_ready, 1)
            act.activation(lora[:, 1, :], lora[:, 1, :], ACT.Sigmoid).then_inc(lora_ready, 1)
            act.activation(lora[0:CH, 2, :], lora[0:CH, 2, :], ACT.Sigmoid).then_inc(lora_ready, 1)
            for n2, (f, z, after_next) in enumerate((("r", zr, "v"), ("k", zk, "q2"), ("v", zv, None))):
                act.wait_ge(half_used, used_count(f))
                for b in range(2):
                    act.copy(z[:, 2 * b:2 * b + 2, :], bank[2 * n2 + b][:, :].rearrange("p (i t) -> p i t", i=2)).then_inc(z_raw, 1)
                if after_next:
                    upper(after_next)
            act.wait_ge(lora_up_done, 1)
            for i in range(NP2):
                act.activation(sd[:, i, :], bank[6 + i // 2][:, (i % 2) * T:(i % 2 + 1) * T], ACT.Sigmoid,
                               bias=col2("decay_bias_2")[:, i:i + 1]).then_inc(lora_up_ready, 1)
            act.wait_ge(lora_up_done, 2)
            for i in range(NP2):
                act.activation(aa[:, i, :], bank[i // 2][:, (i % 2) * T:(i % 2 + 1) * T], ACT.Sigmoid,
                               bias=col2("aaa_bias_2")[:, i:i + 1]).then_inc(lora_up_ready, 1)
            act.wait_ge(lora_up_done, 3)
            for t in range(TT):
                act.copy(g_gate[:, t, :], bank[2 + t][:, :]).then_inc(lora_up_ready, 1)
            upper("k2")
            act.wait_ge(cs_ready, 1)
            act.activation(e_pos, cs, ACT.Exp, scale=-KAPPA).then_inc(exp3_ready, 1)
            act.activation(e_neg, cs, ACT.Exp, scale=KAPPA).then_inc(exp3_ready, 1)
            act.activation(e_before, sd, ACT.Exp, scale=-KAPPA).then_inc(exp3_ready, 1)
            act.wait_ge(nrm_done, 1)
            for b in range(2):
                act.activation(nrm[:, 2 * b:2 * b + 2, :], bank[6 + b][:, :].rearrange("p (i t) -> p i t", i=2), ACT.Sqrt).then_inc(nrm_ready, 1)
            for w, (f, pair, after_next) in enumerate((("q2", 2, "v2"), ("k2", 0, "gate_a0"))):
                act.wait_ge(half_used, used_count(f))
                for t in range(TT):
                    act.copy(qk2[:, w, t, :], bank[2 * pair + t][:, :]).then_inc(qkv2_raw, 1)
                upper(after_next)
            act.wait_ge(half_used, used_count("v2"))
            for t in range(TT):
                act.copy(v2[:, t, :], bank[2 + t][:, :]).then_inc(qkv2_raw, 1)
            act.wait_ge(ang_ready, 1)
            act.activation(sinv, ang, ACT.Sin).then_inc(trig_ready, 1)
            act.activation(cosv, ang_n, ACT.Sin).then_inc(trig_ready, 1)
            act.wait_ge(ss_ready, 1)
            act.activation(rs_qk, ss_qk, ACT.Sqrt, bias=eps2, scale=1.0 / HD).then_inc(rs_ready, 1)
            upper("gate_b0")

            def gates(f, pair):
                act.wait_ge(half_used, used_count(f))
                for t in range(TT):
                    act.activation(gate[f][:, t, :], bank[2 * pair + t][:, :], ACT.Sigmoid).then_inc(gate_ready, 1)

            gates("gate_a0", 2)
            for n2, to in enumerate((bn, kn)):
                for t in range(TT):
                    act.wait_ge(nat_done, 2 * n2 + t + 1)
                    act.copy(to[:, t, :], bank[2 * (n2 + 1) + t][:, :]).then_inc(bk_ready, 1)
            upper("gate_a1")
            gates("gate_b0", 1)
            upper("gate_b1")
            act.wait_ge(qkT2_done, 1)
            for w in range(2):
                for b in range(2):
                    act.copy(qkT2[:, w, 2 * b:2 * b + 2, :], bank[4 * w + b][:, :].rearrange("p (i t) -> p i t", i=2)).then_inc(qkT2_ready, 1)
            gates("gate_a1", 3)
            for t, pr in enumerate((prob2_1, prob2_0)):
                act.wait_ge(neg_max, 2 + t + 1)
                for m in range(NQ):
                    o = t * NQ + m
                    act.activation(pr[:, m, :], pr[:, m, :], ACT.Exp, bias=nmax2[:, o:o + 1], accum_out=den2[:, o:o + 1]).then_inc(exp_done, 1)
            gates("gate_b1", 3)
            for n2, j in ((0, 1), (2, 0)):
                act.wait_ge(pT_done, 3 + n2 + 1)
                for b in range(2):
                    ins = act.copy(pT2[:, j, 4 * b:4 * b + 4, :], bank[2 * j + b][:, :].rearrange("p (h t) -> p h t", h=4))
                ins.then_inc(pT_ready, 1)
            act.wait_ge(attn_done, 2)
            for b in range(2):
                act.copy(ybT[:, 2 * b:2 * b + 2, :], bank[6 + b][:, :].rearrange("p (i t) -> p i t", i=2)).then_inc(attn_ready, 1)
            four = lambda a: a[:, :].rearrange("p (m t) -> p m t", m=4)
            for tt in range(TT):
                for b in range(2):
                    B, Z = bank[4 * b:4 * b + 4], batch[b]
                    act.wait_ge(rec_done, count(tensor_steps, "p2", tt, b))
                    act.copy(Z["P2"], four(B[1]))
                    act.copy(Z["PU"][:, :, 0, :], four(B[3])).then_inc(rec_copied, 1)
                for b in range(2):
                    B = bank[4 * b:4 * b + 4]
                    act.wait_ge(rec_done, count(tensor_steps, "nv", tt, b))
                    for half in range(2):
                        ins = act.copy(x0[:, tt, 4 * b + half:4 * b + half + 3:2, HD:P],
                                       B[2][:, half * P:(half + 1) * P].rearrange("p (m v) -> p m v", m=2))
                    ins.then_inc(rec_copied, 1)
                for b in range(2):
                    B, Z = bank[4 * b:4 * b + 4], batch[b]
                    act.wait_ge(rec_done, count(tensor_steps, "p4", tt, b))
                    act.copy(Z["Mb"], four(B[3])).then_inc(rec_copied, 1)
                for b in range(2):
                    B, Z = bank[4 * b:4 * b + 4], batch[b]
                    act.wait_ge(rec_done, count(tensor_steps, "p8", tt, b))
                    act.copy(Z["P2"], four(B[2])).then_inc(rec_copied, 1)
                for b in range(2):
                    B, Z = bank[4 * b:4 * b + 4], batch[b]
                    act.wait_ge(rec_done, count(tensor_steps, "x1", tt, b))
                    act.copy(Z["X1"], four(B[3])).then_inc(rec_copied, 1)
                for b in range(2):
                    B, Z = bank[4 * b:4 * b + 4], batch[b]
                    act.wait_ge(rec_done, count(tensor_steps, "x2", tt, b))
                    act.copy(Z["Mb"], four(B[2])).then_inc(rec_copied, 1)
                act.wait_ge(y2_done, tt + 1)
                for half in range(2):
                    act.copy(y2[:, tt, :].rearrange("p (i h v) -> p i h v", i=NP2, h=2)[:, :, half, :],
                             bank[2 + half][:, 0:T].rearrange("p (i v) -> p i v", i=NP2)).then_inc(y2_ready, 1)
            act.wait_ge(g_var, 2)
            act.activation(y_std, y_sum2, ACT.Sqrt, bias=eps3, scale=1.0 / HD).then_inc(g_stds, 1)
            act.wait_ge(sguT_done, 2)
            for b in range(2):
                act.copy(yaT[:, 2 * b:2 * b + 2, :], bank[2 + b][:, :].rearrange("p (i t) -> p i t", i=2)).then_inc(sguT_ready, 1)

            def ff_part(i, use, cols):
                act.wait_ge(ff_in[i], use * 32)
                act.copy(ff_hi[i][:, cols], ff_land[i][:, cols]).then_inc(ff_upper[i], 1)

            up_cols, down_cols = slice(0, 2 * D), slice(2 * D, FF)
            for t in range(TT):
                act.wait_ge(hT_done, 4 + t + 1)
                for b in range(2):
                    act.copy(mT[:, 4 * b:4 * b + 4, t * P:(t + 1) * P], bank[4 + 2 * t + b][:, :].rearrange("p (k t) -> p k t", k=4)).then_inc(hT_ready, 1)
            act.wait_ge(branch_done, 4)
            ff_part(0, 1, up_cols)
            ff_part(0, 1, down_cols)
            for t in range(TT):
                for n2 in range(2):
                    act.wait_ge(u_done, 2 * t + n2 + 1)
                    act.activation(squares2[:, t, n2 * BANK:(n2 + 1) * BANK], bank[2 * t + n2][:, :], ACT.Square, scale=D ** -0.5,
                                   accum_out=ss2[:, t, n2:n2 + 1]).then_inc(sq_done, 1)
                act.wait_ge(rms_ready, t + 1)
                act.activation(rms2[:, t:t + 1], ms2[:, t:t + 1], ACT.Sqrt).then_inc(rms_std, 1)
            upper_x(1, 12)
            ff_part(1, 1, up_cols)
            ff_part(1, 1, down_cols)

            def gelu(i, use):
                act.wait_ge(conv_ready[i], use)
                act.activation(conv[:, i, :], conv[:, i, :], ACT.Gelu).then_inc(gelu_ready[i], 1)

            def next_part(i, now, cols):
                act.wait_ge(ffu_used[i] if cols is up_cols else ffd_used[i], now)
                ff_part(i, act.snap(now + 1), cols)

            with act.Fori(0, FT_N // 2 - 1) as it:
                now = act.snap(it + 1)
                gelu(0, now)
                next_part(0, now, up_cols)
                gelu(1, now)
                next_part(0, now, down_cols)
                next_part(1, now, up_cols)
                next_part(1, now, down_cols)
            for i in range(2):
                gelu(i, FT_N // 2)
            act.wait_ge(ffn_done, 1)
            for n2 in range(2):
                act.copy(out_sb[:, 0, n2 * BANK:(n2 + 1) * BANK], bank[n2][:, :]).then_inc(out_ready[0], 1)

        @block.vector
        def _(dve):
            step = [0]

            def link(ins):
                step[0] += 1
                ins.then_inc(dve_step, 1)
                dve.wait_ge(dve_step, step[0])

            def wide(a, n):
                return a.unsqueeze(len(a.shape)).broadcast_to(list(a.shape) + [n])

            link(dve.memset(eps1, LN_EPS))
            link(dve.memset(eps2, NORM_EPS))
            link(dve.memset(eps3, GN_EPS))
            dve.wait_ge(consts_in, 48)
            link(dve.tensor_scalar(alpha_ident, ident, ALPHA1, None, ALU.mult))
            b_vug = rowv("b_in_vug")
            dve.wait_ge(proj_done, 2)
            dve.tensor_scalar(qkT[:, 4, :], bank[2][:, 0:T], colv("b_in_qk")[:, 4:5], None, ALU.add).then_inc(qk_ready, 1)
            for t in range(TT):
                dve.tensor_tensor(v_nat[:, t, :], bank[2][:, T + t * P:T + (t + 1) * P], b_vug[:, 0:P], ALU.add).then_inc(v_ready, 1)

            def masked(to, frm, masks):
                link(dve.scalar_tensor_tensor(out=to, in0=frm, scalar=HD ** -0.5, in1=masks, op0=ALU.mult, op1=ALU.add))

            def soft_max(t, pr):
                o = t * NQ
                link(dve.tensor_reduce(nmax[:, o:o + NQ], pr, AX.X, ALU.max))
                link(dve.tensor_tensor(nmax[:, o:o + NQ], nmax[:, o:o + NQ], rowv("sinks"), ALU.max))
                link(dve.tensor_tensor(sink_e[:, o:o + NQ], rowv("sinks"), nmax[:, o:o + NQ], ALU.subtract))
                dve.tensor_scalar(nmax[:, o:o + NQ], nmax[:, o:o + NQ], -1.0, None, ALU.mult).then_inc(neg_max, 1)

            over = lambda a, n: a.unsqueeze(1).broadcast_to([P, n] + list(a.shape[1:]))
            dve.wait_ge(scores_done, 1)
            for b, nb in enumerate((0, 1, 3, 4)):
                s3 = bank[nb][:, :].rearrange("p (q s) -> p q s", q=2)
                masked(prob1[:, 2 * b:2 * b + 2, 0:P], s3[:, :, 0:P], over(const("before"), 2))
                masked(prob1[:, 2 * b:2 * b + 2, P:T], s3[:, :, P:T], over(const("causal"), 2))
            soft_max(0, prob1)
            dve.wait_ge(scores_done, 2)
            for half in range(2):
                masked(prob0[:, 4 * half:4 * half + 4, :], bank[2 + 5 * half][:, :].rearrange("p (h s) -> p h s", h=4), over(const("causal"), 4))
            soft_max(1, prob0)
            for t, pr in enumerate((prob1, prob0)):
                o = t * NQ
                dve.wait_ge(exp_done, (t + 1) * (NQ + 1))
                link(dve.tensor_tensor(den[:, o:o + NQ], den[:, o:o + NQ], sink_e[:, o:o + NQ], ALU.add))
                link(dve.reciprocal(den[:, o:o + NQ], den[:, o:o + NQ]))
                dve.tensor_tensor(pr, pr, wide(den[:, o:o + NQ], pr.shape[2]), ALU.mult).then_inc(prob_ready, 1)
            dve.wait_ge(wsT_in, 16)
            dve.tensor_tensor(wsT, wsT, const("upto").unsqueeze(1).broadcast_to([P, NG, P]), ALU.mult).then_inc(wsT_masked, 1)

            def bias_half(a, t, to, at, done):
                dve.wait_ge(proj_done, done)
                dve.tensor_tensor(a[:, t, :], bank[to][:, :], b_vug[:, at:at + G1], ALU.add).then_inc(ug_biased, 1)

            for t in range(TT):
                bias_half(g_nat, t, 5 + t, P + G1, 3 + t)
            g3 = g_nat.rearrange("p t (g d) -> p (t g) d", d=GD)
            sq3 = sq.rearrange("p t (g d) -> p (t g) d", d=GD)
            dve.wait_ge(ug_gelu, 1)
            link(dve.tensor_reduce(g_sum, g3, AX.X, ALU.add))
            link(dve.tensor_scalar(g_sum, g_sum, 1.0 / GD, None, ALU.mult))
            link(dve.tensor_tensor(g3, g3, wide(g_sum, GD), ALU.subtract))
            link(dve.tensor_tensor(sq3, g3, g3, ALU.mult))
            dve.tensor_reduce(g_sum2, sq3, AX.X, ALU.add).then_inc(g_var, 1)
            bias_half(u_nat, 0, 0, P, 5)
            dve.wait_ge(g_stds, 1)
            link(dve.reciprocal(g_sum2, g_std))
            link(dve.tensor_tensor(g3, g3, wide(g_sum2, GD), ALU.mult))
            link(dve.tensor_tensor(g_nat, g_nat, rowv("ln_v_g").unsqueeze(1).broadcast_to([P, TT, G1]), ALU.mult))
            dve.tensor_tensor(g_nat, g_nat, rowv("ln_v_b").unsqueeze(1).broadcast_to([P, TT, G1]), ALU.add).then_inc(g_normed, 1)
            bias_half(u_nat, 1, 1, P, 6)
            dve.wait_ge(ln_rows_in, 32)
            link(dve.scalar_tensor_tensor(out=x_nat, in0=x_nat, scalar=ALPHA1, in1=over(rowv("b_out"), TT), op0=ALU.mult, op1=ALU.add))
            dve.wait_ge(mixed_done, 1)
            dve.wait_ge(ug_gelu, 3)
            for b in range(2):
                m4 = bank[(2, 7)[b]][:, :].rearrange("p (g c d) -> p c g d", g=4, c=TT)
                s4 = sq[:, :, b * T:(b + 1) * T].rearrange("p c (g d) -> p c g d", g=4)
                for c in range(TT):
                    link(dve.tensor_tensor(s4[:, c], m4[:, c], wide(colv("b_s")[:, 4 * b:4 * b + 4], GD), ALU.add))
            dve.tensor_tensor(u_nat, u_nat, sq, ALU.mult).then_inc(sgu_ready, 1)
            dve.wait_ge(sguT_done, 1)
            for b in range(2):
                dve.tensor_copy(mixT[:, 4 + 2 * b:6 + 2 * b, :], bank[(2, 7)[b]][:, :].rearrange("p (k t) -> p k t", k=2)).then_inc(sguT_ready, 1)

            def layer_norm(t, halves, g, b, done, before, to, meanwhile=None):
                for n in range(2):
                    link(dve.bn_stats(stats[:, n, :], halves(n)))
                dve.bn_aggr(mv[:, t, :], stats.rearrange("p n s -> p (n s)")).then_inc(var_ready, 1)
                dve.wait_ge(var_ready, before + t + 1)
                for n in range(2):
                    cols = slice(n * BANK, (n + 1) * BANK)
                    link(dve.scalar_tensor_tensor(out=resid[:, t, cols], in0=halves(n), scalar=mv[:, t, 0:1], in1=g[:, cols],
                                                  op0=ALU.subtract, op1=ALU.mult))
                if meanwhile:
                    meanwhile()
                dve.wait_ge(std_ready, before + t + 1)
                link(dve.reciprocal(rstd[:, t:t + 1], rstd[:, t:t + 1]))
                dve.scalar_tensor_tensor(out=to[:, t, :], in0=resid[:, t, :], scalar=rstd[:, t:t + 1], in1=b,
                                         op0=ALU.mult, op1=ALU.add).then_inc(done, 1)

            def mixed(t):
                def half(n):
                    return resid[:, t, n * BANK:(n + 1) * BANK]
                for n in range(2):
                    cols = slice(n * BANK, (n + 1) * BANK)
                    dve.wait_ge(mix_done, 2 * t + n + 1)
                    link(dve.tensor_tensor(half(n), x_nat[:, t, cols], bank[mix_bank[t][n]][:, :], ALU.add))
                return half

            mix_bank = [[0, 1], [5, 6]]
            for t in range(TT):
                layer_norm(t, mixed(t), rowv("ln1_g"), rowv("ln1_b"), h_ready, 0, h)
            dve.wait_ge(h_ready, 2)
            dve.memset(place_T, 0.0).then_inc(place_T_ready, 1)
            dve.memset(yy, 0.0).then_inc(y_ready, 1)
            dve.wait_ge(router_done, 1)
            link(dve.tensor_tensor(logits, bank[7][:, 0:TT * NE].rearrange("p (t e) -> p t e", t=TT), over(rowv("b_router"), TT), ALU.add))
            for t in range(TT):
                link(dve.max(top8[:, t, :], logits[:, t, :]))
                link(dve.max_index(top_i[:, t, :], top8[:, t, :], logits[:, t, :]))
            link(dve.tensor_copy(top_f, top_i[:, :, 0:TOPK]))
            for t in range(TT):
                link(dve.tensor_tensor(chosen4[:, t], over(const("iota32"), TOPK), wide(top_f[:, t, :], NE), ALU.is_equal))
                ins = dve.tensor_reduce(chosen[:, t, :], chosen4[:, t].rearrange("p k e -> p e k"), AX.X, ALU.add)
                if t == 0:
                    link(ins)
            ins.then_inc(chosen_ready, 1)
            link(dve.tensor_copy(gates4, top8[:, :, 0:TOPK]))
            dve.tensor_scalar(ntop, top8[:, :, 0], -1.0, None, ALU.mult).then_inc(top_ready, 2)
            link(dve.memset(gate_of[:, :, NE * PASSES:COLS], 0.0))
            link(dve.memset(posm[:, :, NE * PASSES:COLS], 0.0))
            dve.wait_ge(router_done, 2)
            link(dve.tensor_tensor(posm[:, :, 0:NE], bank[5][:, 0:TT * NE].rearrange("p (t e) -> p t e", t=TT), chosen, ALU.mult))

            def build_place(col):
                for t in range(TT):
                    ins = dve.tensor_scalar(place[:, t, :], const("iota2")[:, 0:CAP], posm[:, t, bass.ds(col, 1)], None, ALU.is_equal)
                ins.then_inc(place_ready, 1)

            def build_place_g(col):
                for t in range(TT):
                    ins = dve.tensor_scalar(place_g[:, t, :], const("iota2"), posm[:, t, bass.ds(col, 1)],
                                            gate_of[:, t, bass.ds(col, 1)], ALU.is_equal, ALU.mult)
                ins.then_inc(place_g_ready, 1)

            build_place(0)
            dve.wait_ge(router_done, 3)
            link(dve.tensor_reduce(n_iter_f[0:1, 0:1], bank[4][0:1, 0:NE], AX.X, ALU.max))
            link(dve.tensor_scalar(passes, const("thresholds")[0:1, :], n_iter_f[0:1, 0:1], float(NE), ALU.is_lt, ALU.mult))
            link(dve.tensor_reduce(n_iter_f[0:1, 1:2], passes, AX.X, ALU.add))
            link(dve.tensor_scalar(n_iter_f[0:1, 2:3], n_iter_f[0:1, 1:2], -1.0, None, ALU.add))
            dve.tensor_copy(n_iter[0:1, 0:2], n_iter_f[0:1, 1:3]).then_inc(iter_ready, 1)
            for b in range(1, PASSES):
                link(dve.tensor_scalar(posm[:, :, b * NE:(b + 1) * NE], posm[:, :, 0:NE], float(-b * CAP), None, ALU.add))
            dve.wait_ge(top_exp, 2)
            link(dve.reciprocal(gsum, gsum))
            for t in range(TT):
                link(dve.tensor_scalar(gates4[:, t, :], gates4[:, t, :], gsum[:, t:t + 1], None, ALU.mult))
                link(dve.tensor_tensor(chosen4[:, t], chosen4[:, t], wide(gates4[:, t, :], NE), ALU.mult))
                link(dve.tensor_reduce(gate_of[:, t, 0:NE], chosen4[:, t].rearrange("p k e -> p e k"), AX.X, ALU.add))
            for b in range(1, PASSES):
                ins = dve.tensor_copy(gate_of[:, :, b * NE:(b + 1) * NE], gate_of[:, :, 0:NE])
                if b < PASSES - 1:
                    link(ins)
            ins.then_inc(chosen_ready, 1)
            dve.wait_ge(chosen_ready, 2)
            build_place_g(0)
            dve.wait_ge(gather_done, 1)
            build_place(1)
            n = dve.value_load(n_iter[0:1, 0:1], min_val=NE, max_val=NE * PASSES)
            with dve.Fori(0, n) as it:
                now = dve.snap(it + 1)
                dve.wait_ge(slots_used, dve.snap(it * SLOTS + 8))
                dve.tensor_scalar(gt, bank[4][:, :], LIMIT, None, ALU.min).then_inc(gt_ready, 1)
                dve.tensor_scalar(uc, bank[5][:, :], LIMIT, -LIMIT, ALU.min, ALU.max).then_inc(uc_ready, 1)
                dve.wait_ge(uc_ready, now)
                dve.wait_ge(gt_ready, now)
                dve.scalar_tensor_tensor(out=vv, in0=uc, scalar=1.0, in1=gt, op0=ALU.add, op1=ALU.mult).then_inc(vv_ready, 1)
                dve.wait_ge(sg_ready, now)
                dve.wait_ge(vv_ready, now)
                dve.tensor_tensor(hid, vv, sg, ALU.mult).then_inc(hid_ready, 1)
                dve.wait_ge(place_T_done, now)
                dve.tensor_copy(place_T, bank[5][:, 0:T]).then_inc(place_T_ready, 1)
                build_place(it + 2)
                build_place_g(it + 1)
            def norm(t, rms):
                dve.wait_ge(rms_std, t + 1)
                link(dve.reciprocal(rms, rms))
                dve.tensor_scalar(rms_diag[:, t % TT, :], ident, rms, None, ALU.mult).then_inc(hn_ready, 1)

            def norm_first():
                norm(0, rms1[:, 0:1])

            dve.wait_ge(acc_done, 1)
            for t in range(TT):
                layer_norm(t, lambda n: bank[2 * t + n][:, :], rowv("ln2_g"), rowv("ln2_b"), x1_ready, TT, resid, norm_first if t == 1 else None)
            norm(1, rms1[:, 1:2])

            def scaled_T(base, g, n2):
                def scaled(t, b):
                    dve.wait_ge(hT_done, base + t + 1)
                    dve.tensor_tensor(hnT[:, 4 * b:4 * b + 4, t * P:(t + 1) * P],
                                      bank[4 + 2 * t + b][:, :].rearrange("p (k t) -> p k t", k=4),
                                      wide(col2(g)[:, 4 * b:4 * b + 4], P), ALU.mult).then_inc(hT_ready, 1)

                def rest(t, b):
                    cols = slice(t * P, (t + 1) * P)
                    dve.wait_ge(x_upper, 4 * n2 + 2 * b + t + 1)
                    for ks, hi in hi_parts(n2, b, cols):
                        ins = dve.tensor_tensor(hnT_rest[:, ks, cols], hnT[:, ks, cols], hi.bitcast(F32), ALU.subtract)
                    ins.then_inc(x_rest, 1)

                scaled(0, 0)
                scaled(0, 1)
                rest(0, 0)
                scaled(1, 0)
                scaled(1, 1)
                rest(1, 0)
                rest(0, 1)
                rest(1, 1)

            dve.wait_ge(small2_in, 112)
            scaled_T(2, "norm1_g_2", 0)

            def mix_before(z, mu, n):
                link(dve.tensor_tensor(tmp[:, 0:n, 1:T], z[:, :, 0:T - 1], z[:, :, 1:T], ALU.subtract))
                link(dve.tensor_scalar(tmp[:, 0:n, 0:1], z[:, :, 0:1], -1.0, None, ALU.mult))
                for i in range(n):
                    ins = dve.scalar_tensor_tensor(out=z[:, i, :], in0=tmp[:, i, :], scalar=mu[:, i:i + 1], in1=z[:, i, :],
                                                   op0=ALU.mult, op1=ALU.add)
                    if i < n - 1:
                        link(ins)
                return ins

            link(dve.tensor_copy(pos_f, pos_i))
            link(dve.tensor_tensor(ang, const2("inv_freq").unsqueeze(1).broadcast_to([P, TT, ROT]), wide(pos_f, ROT), ALU.mult))
            link(dve.tensor_scalar(ang_n, ang, float(1 / (2 * np.pi)), 1.5 * 2.0 ** 23, ALU.mult, ALU.add))
            link(dve.tensor_scalar(ang_n, ang_n, -1.5 * 2.0 ** 23, None, ALU.add))
            link(dve.scalar_tensor_tensor(out=ang, in0=ang_n, scalar=-6.28125, in1=ang, op0=ALU.mult, op1=ALU.add))
            link(dve.scalar_tensor_tensor(out=ang, in0=ang_n, scalar=float(6.28125 - 2 * np.pi), in1=ang, op0=ALU.mult, op1=ALU.add))
            link(dve.tensor_scalar(ang, ang, 3.1415925, -3.1415925, ALU.min, ALU.max))
            link(dve.scalar_tensor_tensor(out=ang_n, in0=ang, scalar=-1.0, in1=ang, op0=ALU.mult, op1=ALU.max))
            dve.tensor_scalar(ang_n, ang_n, -1.0, float(np.pi / 2), ALU.mult, ALU.add).then_inc(ang_ready, 1)
            dve.wait_ge(z_raw, 2)
            link(mix_before(lora[:, 0:2, :], col2("mu_lora"), 2))
            link(dve.tensor_tensor(tmp[0:CH, 0, 1:T], lora[0:CH, 2, 0:T - 1], lora[0:CH, 2, 1:T], ALU.subtract))
            link(dve.tensor_scalar(tmp[0:CH, 0, 0:1], lora[0:CH, 2, 0:1], -1.0, None, ALU.mult))
            dve.scalar_tensor_tensor(out=lora[0:CH, 2, :], in0=tmp[0:CH, 0, :], scalar=col2("mu_lora")[0:CH, 2:3], in1=lora[0:CH, 2, :],
                                     op0=ALU.mult, op1=ALU.add).then_inc(lora_mixed, 1)
            dve.wait_ge(z_raw, 4)
            link(mix_before(zr, col2("mu_r"), NP2))
            dve.wait_ge(z_raw, 6)
            link(mix_before(zk, col2("mu_k"), NP2))
            link(dve.tensor_tensor(kk, zk, wide(col2("rwkv_k_k_2"), T), ALU.mult))
            dve.tensor_tensor(kk2, kk, kk, ALU.mult).then_inc(kk2_ready, 1)
            dve.wait_ge(z_raw, 8)
            link(mix_before(zv, col2("mu_v"), NP2))
            dve.wait_ge(lora_up_ready, 4)
            for i in range(NP2):
                link(dve.tensor_tensor_scan(cs[:, i, :], const2("chunk_start"), sd[:, i, :], 0.0, ALU.mult, ALU.add))
            dve.tensor_tensor(sd, cs, sd, ALU.subtract).then_inc(cs_ready, 1)
            dve.wait_ge(lora_up_ready, 8)
            dve.wait_ge(nrm_ready, 2)
            link(dve.tensor_scalar(nrm, nrm, 1e-12, None, ALU.max))
            link(dve.reciprocal(nrm, nrm))
            link(dve.tensor_tensor(kk, kk, nrm, ALU.mult))
            for i in range(NP2):
                link(dve.tensor_scalar(nrm[:, i, :], aa[:, i, :], -1.0, col2("rwkv_k_a_2")[:, i:i + 1], ALU.add, ALU.mult))
            link(dve.scalar_tensor_tensor(out=zk, in0=nrm, scalar=1.0, in1=zk, op0=ALU.add, op1=ALU.mult))
            for i in range(NP2):
                ins = dve.scalar_tensor_tensor(out=kk2[:, i, :], in0=zr[:, i, :], scalar=col2("rwkv_r_k_2")[:, i:i + 1], in1=zk[:, i, :],
                                               op0=ALU.mult, op1=ALU.mult)
            ins.then_inc(rk_ready, 1)
            dve.wait_ge(exp3_ready, 3)
            link(dve.tensor_tensor(ar[:, :, 1, :], zr, e_pos, ALU.mult))
            link(dve.scalar_tensor_tensor(out=ar[:, :, 0, :], in0=kk, scalar=-1.0, in1=e_before, op0=ALU.mult, op1=ALU.mult))
            link(dve.tensor_tensor(aa, aa, kk, ALU.mult))
            link(dve.tensor_tensor(b_hat, aa, e_neg, ALU.mult))
            dve.tensor_tensor(k_hat, zk, e_neg, ALU.mult).then_inc(hats_ready, 1)
            dve.wait_ge(qkv2_raw, 4)
            heads = lambda a: a.rearrange("p w t (h d) -> p (w t h) d", d=HD)
            dve.wait_ge(hats_ready, 1)
            link(dve.tensor_tensor(sq2, qk2, qk2, ALU.mult))
            dve.tensor_reduce(ss_qk, heads(sq2), AX.X, ALU.add).then_inc(ss_ready, 1)
            dve.wait_ge(rs_ready, 1)
            link(dve.reciprocal(rs_qk, rs_qk))
            link(dve.tensor_tensor(heads(qk2), heads(qk2), wide(rs_qk, HD), ALU.mult))

            def rotate(w, g):
                a = qk2[:, w].rearrange("p t (h d) -> p (t h) d", d=HD)
                link(dve.tensor_tensor(a, a, row2(g).unsqueeze(1).broadcast_to([P, TT * NQ, HD]), ALU.mult))
                at = qk2[:, w].rearrange("p t (h d) -> p t h d", d=HD)
                lo, hi = at[:, :, :, 0:ROT], at[:, :, :, ROT:2 * ROT]
                c8, s8 = (x.unsqueeze(2).broadcast_to([P, TT, NQ, ROT]) for x in (cosv, sinv))
                dve.tensor_tensor(rope_t[:, 0], lo, c8, ALU.mult)
                dve.tensor_tensor(rope_t[:, 1], hi, s8, ALU.mult)
                dve.tensor_tensor(rope_t[:, 2], hi, c8, ALU.mult)
                link(dve.tensor_tensor(rope_t[:, 3], lo, s8, ALU.mult))
                dve.tensor_tensor(lo, rope_t[:, 0], rope_t[:, 1], ALU.subtract)
                return dve.tensor_tensor(hi, rope_t[:, 2], rope_t[:, 3], ALU.add)

            dve.wait_ge(bonus_done, 1)
            dve.tensor_copy(bonus, bank[6][:, 0:TT * NQ].rearrange("p (t h) -> p t h", t=TT)).then_inc(bonus_ready, 1)
            dve.wait_ge(trig_ready, 2)
            link(rotate(0, "q_norm_g_2"))
            for t in range(TT):
                dve.wait_ge(nat_done, 4 + t + 1)
                dve.tensor_copy(x0[:, t, :, 0:HD], bank[t][:, :].rearrange("p (h k) -> p h k", h=NQ)).then_inc(av_ready, 1)
            rotate(1, "k_norm_g_2").then_inc(qk2_ready, 1)
            for t in range(TT):
                dve.wait_ge(nat_done, 6 + t + 1)
                dve.tensor_copy(vn[:, t, :], bank[6 + t][:, :]).then_inc(av_ready, 1)

            def soft_max2(t, pr):
                o = t * NQ
                link(dve.tensor_reduce(nmax2[:, o:o + NQ], pr, AX.X, ALU.max))
                dve.tensor_scalar(nmax2[:, o:o + NQ], nmax2[:, o:o + NQ], -1.0, None, ALU.mult).then_inc(neg_max, 1)

            dve.wait_ge(scores_done, 3)
            for b in range(4):
                s3 = bank[(0, 1, 4, 5)[b]][:, :].rearrange("p (m s) -> p m s", m=2)
                link(dve.tensor_scalar(prob2_1[:, 2 * b:2 * b + 2, 0:P], s3[:, :, 0:P], HD ** -0.5, None, ALU.mult))
                masked(prob2_1[:, 2 * b:2 * b + 2, P:T], s3[:, :, P:T], const("causal").unsqueeze(1).broadcast_to([P, 2, P]))
            soft_max2(0, prob2_1)
            dve.wait_ge(scores_done, 4)
            for half in range(2):
                masked(prob2_0[:, 4 * half:4 * half + 4, :], bank[2 + half][:, :].rearrange("p (m s) -> p m s", m=4),
                       const("causal").unsqueeze(1).broadcast_to([P, 4, P]))
            soft_max2(1, prob2_0)
            for t, pr in enumerate((prob2_1, prob2_0)):
                o = t * NQ
                dve.wait_ge(exp_done, 18 + (t + 1) * NQ)
                link(dve.reciprocal(den2[:, o:o + NQ], den2[:, o:o + NQ]))
                dve.tensor_tensor(pr, pr, wide(den2[:, o:o + NQ], pr.shape[2]), ALU.mult).then_inc(prob_ready, 1)
            dve.wait_ge(pT_done, 3 + 2)
            for b in range(2):
                ins = dve.tensor_copy(pT2[:, 2, 4 * b:4 * b + 4, :], bank[4 + b][:, :].rearrange("p (h t) -> p h t", h=4))
            ins.then_inc(pT_ready, 1)

            two = lambda a: a[:, :].rearrange("p (m w t) -> p m w t", m=2, w=2)
            both = lambda n: const2_sb[:, const2_at[n][0]:const2_at[n][0] + T].rearrange("p (w t) -> p w t", w=2)
            MA_mask, NK_mask = both("subT_before"), both("chunkT_before")
            for tt in range(TT):
                for b in range(2):
                    B, Z = bank[4 * b:4 * b + 4], batch[b]
                    dve.wait_ge(rec_done, count(tensor_steps, "m", tt, b))
                    for half in range(2):
                        ins = dve.tensor_tensor(Z["Mb"][:, 2 * half:2 * half + 2, :], B[2 * half][:, 0:T].rearrange("p (m t) -> p m t", m=2),
                                                over(const2("sub_before"), 2), ALU.mult)
                    ins.then_inc(rec_ready, 1)
                for b in range(2):
                    B, Z = bank[4 * b:4 * b + 4], batch[b]
                    for half in range(2):
                        src, hd = two(B[2 * half + 1]), slice(2 * half, 2 * half + 2)
                        dve.tensor_tensor(Z["MA"][:, hd], src, over(MA_mask, 2), ALU.mult)
                        ins = dve.tensor_tensor(Z["MoT"][:, hd, :], src[:, :, 0, :], over(const2("off_subT"), 2), ALU.mult)
                    ins.then_inc(rec_ready, 1)
                for b in range(2):
                    B, Z = bank[4 * b:4 * b + 4], batch[b]
                    dve.wait_ge(rec_done, count(tensor_steps, "nk", tt, b))
                    for half in range(2):
                        src, hd = two(B[2 * half]), slice(2 * half, 2 * half + 2)
                        ins = dve.tensor_tensor(Z["NK"][:, hd], src, over(NK_mask, 2), ALU.mult)
                    ins.then_inc(rec_ready, 1)
                for b in range(2):
                    B, Z = bank[4 * b:4 * b + 4], batch[b]
                    dve.wait_ge(rec_done, count(tensor_steps, "p4", tt, b))
                    for half in range(2):
                        src, hd = two(B[half]), slice(2 * half, 2 * half + 2)
                        dve.tensor_copy(Z["MA"][:, hd, 0, :], src[:, :, 0, :])
                        ins = dve.tensor_tensor(Z["PU"][:, hd, 1, :], Z["PU"][:, hd, 1, :], src[:, :, 1, :], ALU.add)
                    ins.then_inc(rec_ready, 1)
                for done, which, before in (("p8", 0, "U2"), ("du", 1, "U4")):
                    for b in range(2):
                        B, Z = bank[4 * b:4 * b + 4], batch[b]
                        dve.wait_ge(rec_done, count(tensor_steps, done, tt, b))
                        dve.wait_ge(rec_ready, count(vector_steps, before, tt, b))
                        dve.tensor_tensor(Z["PU"][:, :, 1, :], Z["PU"][:, :, 1, :], B[which][:, :].rearrange("p (m t) -> p m t", m=4),
                                          ALU.add).then_inc(rec_ready, 1)
                for b in range(2):
                    B, Z = bank[4 * b:4 * b + 4], batch[b]
                    dve.wait_ge(rec_done, count(tensor_steps, "x3", tt, b))
                    dve.tensor_tensor(Z["X1"], Z["X1"], B[0][:, :].rearrange("p (m t) -> p m t", m=4), ALU.add).then_inc(rec_ready, 1)
                for b in range(2):
                    B = bank[4 * b:4 * b + 4]
                    dve.wait_ge(rec_done, count(tensor_steps, "rT", tt, b))
                    dve.tensor_tensor(rT[:, 2 * b:2 * b + 2, :], B[1][:, 0:T].rearrange("p (i t) -> p i t", i=2),
                                      ar[:, 2 * b:2 * b + 2, 1, tt * P:(tt + 1) * P], ALU.add).then_inc(rec_ready, 1)
                c0 = passed_on(tt)[0]
                ends = slice(tt * P + c0 * CH - 1, (tt + 1) * P - 1, CH)
                r_t = rT[:, :, c0 * CH:].rearrange("p i (c t) -> p i c t", t=CH)
                dve.wait_ge(rec_ready, count(vector_steps, "rT", tt, 1))
                dve.tensor_tensor(r_t, r_t, wide(e_pos[:, :, ends], CH), ALU.mult)
                for b in range(2):
                    B, pr = bank[4 * b:4 * b + 4], slice(2 * b, 2 * b + 2)
                    dve.wait_ge(rec_done, count(tensor_steps, "fh", tt, b))
                    for c in passed_on(tt, True):
                        ins = dve.tensor_copy(hs[:, c, pr, :], B[c][:, P:T].rearrange("p (i v) -> p i v", i=2))
                    for c in passed_on(tt):
                        ins = dve.tensor_tensor(ft[:, c, pr, :], B[c][:, 0:P].rearrange("p (i k) -> p i k", i=2), over(const2("ident64"), 2), ALU.add)
                    link(ins)
                    f_t, n = ft[:, c0:passed_on(tt)[-1] + 1, pr, :], len(passed_on(tt))
                    ecl = e_pos[:, pr, ends].rearrange("p i c -> p c i")[:, 0:n]
                    dve.tensor_tensor(f_t, f_t, wide(ecl, HD), ALU.mult).then_inc(rec_ready, 1)
                for c in passed_on(tt):
                    number = tt * P // CH + c
                    dve.wait_ge(st_done, number)
                    dve.tensor_tensor(state[:, number % 2], bank[number % 2][:, 0:T].rearrange("p (i v) -> p i v", i=NP2), hs[:, c],
                                      ALU.add).then_inc(st_ready, 1)
            dve.wait_ge(y2_ready, 4)
            y3 = y2.rearrange("p t (h d) -> p (t h) d", d=HD)
            q3 = sqy.rearrange("p t (h d) -> p (t h) d", d=HD)
            link(dve.tensor_reduce(y_sum, y3, AX.X, ALU.add))
            link(dve.tensor_scalar(y_sum, y_sum, 1.0 / HD, None, ALU.mult))
            link(dve.tensor_tensor(y3, y3, wide(y_sum, HD), ALU.subtract))
            link(dve.tensor_tensor(q3, y3, y3, ALU.mult))
            dve.tensor_reduce(y_sum2, q3, AX.X, ALU.add).then_inc(g_var, 1)
            link(dve.tensor_tensor(bv.rearrange("p t (h d) -> p (t h) d", d=HD), vn.rearrange("p t (h d) -> p (t h) d", d=HD),
                                   wide(bonus.rearrange("p t h -> p (t h)"), HD), ALU.mult))
            dve.wait_ge(g_stds, 2)
            link(dve.reciprocal(y_std, y_std))
            link(dve.tensor_tensor(y3, y3, wide(y_std, HD), ALU.mult))
            link(dve.tensor_tensor(y2, y2, over(row2("rwkv_ln_g_2"), TT), ALU.mult))
            link(dve.tensor_tensor(y2, y2, over(row2("rwkv_ln_b_2"), TT), ALU.add))
            link(dve.tensor_tensor(y2, y2, bv, ALU.add))
            dve.tensor_tensor(y2, y2, g_gate, ALU.mult).then_inc(ya_ready, 1)
            for n2 in range(2):
                g_a, g_b = gate[f"gate_a{n2}"], gate[f"gate_b{n2}"]
                dve.wait_ge(branch_done, n2 + 1)
                for t in range(TT):
                    link(dve.tensor_tensor(g_b[:, t, :], g_b[:, t, :], bank[4 * n2 + t][:, :], ALU.mult))
                dve.wait_ge(branch_done, 3 + n2)
                for t in range(TT):
                    link(dve.tensor_tensor(g_a[:, t, :], g_a[:, t, :], bank[(6, 2)[n2] + t][:, :], ALU.mult))
                    ins = dve.tensor_tensor(mm[:, t, n2 * BANK:(n2 + 1) * BANK], g_a[:, t, :], g_b[:, t, :], ALU.add)
                ins.then_inc(mm_ready, 1)
            dve.wait_ge(ff_upper[0], 1)
            dve.wait_ge(mm_ready, 2)
            dve.tensor_tensor(ff_rest[0][:, 0:2 * D], ff_land[0][:, 0:2 * D], ff_hi[0][:, 0:2 * D].bitcast(F32), ALU.subtract).then_inc(up_rest[0], 1)
            for t in range(TT):
                for n2 in range(2):
                    dve.wait_ge(sq_done, TT + 2 * t + n2 + 1)
                    if n2 == 1:
                        dve.tensor_scalar(ms2[:, t:t + 1], ss2[:, t, 0:1], ss2[:, t, 1:2], NORM_EPS, ALU.add, ALU.add).then_inc(rms_ready, 1)
                    dve.tensor_copy(hn2[:, t, n2 * BANK:(n2 + 1) * BANK], bank[2 * t + n2][:, :])
                norm(TT + t, rms2[:, t:t + 1])
            scaled_T(6, "norm2_g_2", 1)
            def up_part(i, use):
                dve.wait_ge(ff_upper[i], dve.snap(use * 2 - 1) if not isinstance(use, int) else 2 * use - 1)
                dve.tensor_tensor(ff_rest[i][:, 0:2 * D], ff_land[i][:, 0:2 * D], ff_hi[i][:, 0:2 * D].bitcast(F32), ALU.subtract).then_inc(up_rest[i], 1)

            def convolve(i, now, j):
                tap = lambda n: col2(n)[:, bass.ds(j, 1)]
                a = bank[4 + i][:, 0:T]
                dve.wait_ge(ffu_used[i], now)
                dve.tensor_scalar(conv[:, i, :], a, tap("conv2"), tap("ffn_conv_b_2"), ALU.mult, ALU.add).then_inc(hidden_step[i], 1)
                dve.wait_ge(hidden_step[i], dve.snap(now * 4 - 3))
                dve.scalar_tensor_tensor(out=conv[:, i, 1:T], in0=a[:, 0:T - 1], scalar=tap("conv1"), in1=conv[:, i, 1:T],
                                         op0=ALU.mult, op1=ALU.add).then_inc(hidden_step[i], 1)
                dve.wait_ge(hidden_step[i], dve.snap(now * 4 - 2))
                dve.scalar_tensor_tensor(out=conv[:, i, 2:T], in0=a[:, 0:T - 2], scalar=tap("conv0"), in1=conv[:, i, 2:T],
                                         op0=ALU.mult, op1=ALU.add).then_inc(conv_ready[i], 1)

            def hidden(i, now):
                dve.wait_ge(gelu_ready[i], now)
                dve.tensor_tensor(hid2[:, i, :], conv[:, i, :], bank[4 + i][:, T:2 * T], ALU.mult).then_inc(hidden_step[i], 1)
                dve.wait_ge(hidden_step[i], dve.snap(now * 4 - 1))
                dve.tensor_copy(hid2_hi[:, i, :], hid2[:, i, :]).then_inc(hidden_step[i], 1)
                dve.wait_ge(hidden_step[i], dve.snap(now * 4))
                dve.tensor_tensor(hid2_lo[:, i, :], hid2[:, i, :], hid2_hi[:, i, :].bitcast(F32), ALU.subtract).then_inc(hid2_ready[i], 1)

            up_part(1, 1)
            with dve.Fori(0, FT_N // 2 - 1) as it:
                now = dve.snap(it + 1)
                for i in range(2):
                    convolve(i, now, it * 2 + i)
                    hidden(i, now)
                    up_part(i, it + 2)
            for i in range(2):
                convolve(i, FT_N // 2, FT_N - 2 + i)
                hidden(i, FT_N // 2)
            dve.wait_ge(ffn_done, 1)
            for n2 in range(2):
                dve.tensor_copy(out_sb[:, 1, n2 * BANK:(n2 + 1) * BANK], bank[2 + n2][:, :]).then_inc(out_ready[1], 1)

        @block.gpsimd
        def _(pool):
            for t in range(TT):
                pool.wait_ge(split_ready, 2 * t + 1)
                pool.tensor_tensor(resid[:, t, :], h[:, t, :], h_part[:, 0, t, :], ALU.subtract).then_inc(rest_ready, 1)
                pool.wait_ge(split_ready, 2 * t + 2)
                pool.tensor_tensor(h_part[:, 2, t, :], resid[:, t, :], h_part[:, 1, t, :], ALU.subtract).then_inc(rest_ready, 1)
            for n2 in range(len(HALVES)):
                pool.wait_ge(half_upper, n2 + 1)
                pool.tensor_tensor(rest_of(n2), half_view(n2), upper_of(n2).bitcast(F32), ALU.subtract).then_inc(half_rest, 1)
            for half in range(2):
                pool.wait_ge(hats_ready, 1)
                pool.wait_ge(half_used, used_count("gate_a1") + half)
                pool.tensor_scalar(ar_of[half], ar, const2("head_col")[:, half:half + 1], None, ALU.mult).then_inc(pool_ready, 1)
            for tt in range(TT):
                for b in range(2):
                    Z = batch[b]
                    pool.wait_ge(rec_ready, count(vector_steps, "MA", tt, b))
                    pool.tensor_tensor(Z["PU"][:, :, 1, :], Z["MA"][:, :, 0, :], ident.unsqueeze(1).broadcast_to([P, 4, P]),
                                       ALU.add).then_inc(pool_ready, 1)

            def down_part(i, upper):
                pool.wait_ge(ff_upper[i], upper)
                pool.tensor_tensor(ff_rest[i][:, 2 * D:FF], ff_land[i][:, 2 * D:FF], ff_hi[i][:, 2 * D:FF].bitcast(F32), ALU.subtract).then_inc(down_rest[i], 1)

            pool.wait_ge(mm_ready, 2)
            for i in range(2):
                down_part(i, 2)
            with pool.Fori(1, FT_N // 2) as it:
                for i in range(2):
                    down_part(i, pool.snap(it * 2 + 2))


def tiled(a, width):
    return np.ascontiguousarray(a.reshape(-1, P, width).transpose(1, 0, 2))


def arrange(inputs):
    i = {k: np.asarray(v) for k, v in inputs.items()}
    x = i["x"][0]
    heads = np.concatenate([np.r_[j * HD:(j + 1) * HD, (4 + j) * HD:(5 + j) * HD] for j in range(4)])
    order = np.concatenate([heads, np.arange(512, 1792)])
    w_in, b_in = i["w_in"][0][:, order], i["b_in"][0][order]
    row_of = {"b_in_vug": b_in[W_QK:]}
    rows = np.concatenate([row_of.get(n, i[n][0] if n in i else None) for n, _ in ROWS])
    columns = np.concatenate([b_in[:W_QK].reshape(5, P).T, i["b_spatial"][0].T], axis=1)
    w = i["w_in_2"][0]
    part = lambda lo, n: tiled(w[:, lo:lo + n], n).reshape(P, -1)
    lora_at, q_at, gates_at = 3 * C2, 3 * C2 + LORA, 6 * C2 + LORA
    mu = i["rwkv_mu_2"][0]
    mu_lora = np.pad(mu[lora_at:q_at], (0, 3 * P - LORA))
    vectors = {"mu_lora": mu_lora, "mu_r": mu[:C2], "mu_k": mu[C2:2 * C2], "mu_v": mu[2 * C2:3 * C2]}
    vectors |= {f"conv{j}": i["ffn_conv_w_2"][0][j] for j in range(3)}
    columns2 = [(vectors[n] if n in vectors else i[n][0]).reshape(-1, P).T for n, _ in COLUMNS2]
    up = i["w_ffn_up_2"][0].reshape(KD, P, 2, FT_N, P).transpose(3, 1, 2, 0, 4).reshape(FT_N, P, 2 * D)
    second = {
        "consts2": constants2(), "columns2": np.ascontiguousarray(np.concatenate(columns2, axis=1)),
        "rows2": np.concatenate([i[n][0] for n, _ in ROWS2]),
        "w_lora_up": np.concatenate([i["w_decay_up_2"][0], i["w_aaa_up_2"][0]]), "w_gate_up_2": i["w_gate_up_2"][0],
        "pos": np.ascontiguousarray(i["positions_2"].reshape(TT, P).T),
        "ffn_up": np.ascontiguousarray(up), "ffn_down": i["w_ffn_down_2"][0],
        "w2_lora": tiled(np.pad(w[:, lora_at:q_at], ((0, 0), (0, LORA_W - LORA))), LORA_W).reshape(P, -1), "w2_r": part(0, C2), "w2_k": part(C2, C2), "w2_v": part(2 * C2, C2),
        "w2_q2": part(q_at, C2), "w2_k2": part(q_at + C2, C2), "w2_v2": part(q_at + 2 * C2, C2),
        "w2_branch_a": tiled(i["w_branch_a_2"][0], D).reshape(P, -1), "w2_branch_b": tiled(i["w_branch_b_2"][0], D).reshape(P, -1),
        "w2_out0": tiled(i["w_out_2"][0][:C2], D).reshape(P, -1), "w2_out1": tiled(i["w_out_2"][0][C2:], D).reshape(P, -1),
    }
    second |= {f"w2_gate_{'ab'[br]}{n}": part(gates_at + br * D + n * C2, C2) for br in range(2) for n in range(2)}
    return second | {
        "x": x, "xT": tiled(np.ascontiguousarray(x.T), T), "consts": constants(), "columns": np.ascontiguousarray(columns),
        "rows": rows, "w_in": tiled(w_in, 1792), "w_out": tiled(i["w_out"][0], D),
        "wsT": np.ascontiguousarray(i["w_spatial"][0].transpose(2, 0, 1)), "w_router": tiled(i["w_router"][0], NE),
        "w_gate": i["w_gate"][0], "w_up": i["w_up"][0], "w_down": i["w_down"][0], "b_down": i["b_down"][0],
        "b_gate_up": np.concatenate([i["b_gate"][0], i["b_up"][0]], axis=1),
    }


def kernel(**inputs):
    from concourse import bacc
    from concourse.bass_utils import run_bass_kernel_spmd

    nc = bacc.Bacc("TRN2", target_bir_lowering=False, num_devices=1)
    arrays = arrange(inputs)
    A = {n: nc.dram_tensor(f"in_{n}", a.shape, mybir.dt.from_np(a.dtype), kind="ExternalInput").ap() for n, a in arrays.items()}
    out = nc.dram_tensor("out", (T, D), F32, kind="ExternalOutput").ap()
    program(nc, A, out)
    r = run_bass_kernel_spmd(nc, [{f"in_{n}": a for n, a in arrays.items()}], core_ids=[0])
    return r.results[0]["out"].reshape(1, T, D)
```
